# Optimizing a Trainium2 kernel written in Bass

```python
import math
import jax
import jax.numpy as jnp
from jax import lax
import numpy as np

D_MODEL = 1024
BATCH = 1
SEQ = 512
DEPTH = 2

GRID_W = 64
CTX_LEN = 256
N_MIXERS = 4
MIX_DIFF, MIX_GMLP, MIX_NATTEN, MIX_FOURIER = 0, 1, 2, 3
CTX_READERS = (MIX_DIFF, MIX_NATTEN)
EPS = 1e-6
NEG_INF = -1e30
ROPE_BASE = 10000.0

DA_HEADS = 8
DA_HEAD_DIM = 64
DA_V_DIM = 2 * DA_HEAD_DIM
DA_WIDTH = DA_HEADS * DA_V_DIM
DA_Q_BLOCK = 128

GM_CHUNK = 128
GM_GROUPS = 8
GM_WIDTH = 2 * D_MODEL
GM_GROUP_DIM = GM_WIDTH // GM_GROUPS

NA_HEADS = 16
NA_HEAD_DIM = D_MODEL // NA_HEADS
NA_WIDTH = NA_HEADS * NA_HEAD_DIM
NA_WIN_R = 8
NA_WIN_C = 16
NA_COL_BLOCK = 16
NA_COL_BAND = 2 * NA_COL_BLOCK

FN_GROUPS = 4

N_EXPERTS = 16
EXPERT_DIM = D_MODEL
EC_CAPACITY_FACTOR = 2

kernel_name = 'hybrid_diffusion_trunk'

def rmsnorm(x, g):
    xf = x.astype(jnp.float32)
    y = xf * lax.rsqrt(jnp.mean(xf * xf, axis=-1, keepdims=True) + EPS)
    return (y * g.astype(jnp.float32)).astype(x.dtype)

def adaln_params(cond, w, b, n_mod):
    m = jax.nn.silu(cond) @ w[:, :n_mod * D_MODEL] + b[:n_mod * D_MODEL]
    return [t[:, None, :] for t in jnp.split(m, n_mod, axis=-1)]

def modulate(h, shift, scale):
    return h * (1.0 + scale) + shift

def axial_rope_angles(n_tok, dim):
    t = jnp.arange(n_tok, dtype=jnp.int32)
    n_freq = dim // 4
    inv = ROPE_BASE ** (-jnp.arange(n_freq, dtype=jnp.float32) / n_freq)
    rows = (t // GRID_W).astype(jnp.float32)
    cols = (t % GRID_W).astype(jnp.float32)
    return rows[:, None] * inv, cols[:, None] * inv

def rope_axis(x, ang):
    x1, x2 = jnp.split(x, 2, axis=-1)
    cos = jnp.cos(ang)[:, None, :].astype(x.dtype)
    sin = jnp.sin(ang)[:, None, :].astype(x.dtype)
    return jnp.concatenate([x1 * cos - x2 * sin, x1 * sin + x2 * cos], axis=-1)

def axial_rope(x, ang_r, ang_c):
    xr, xc = jnp.split(x, 2, axis=-1)
    return jnp.concatenate([rope_axis(xr, ang_r), rope_axis(xc, ang_c)], axis=-1)

def query_blocks(fn, q, block):
    b, n = q.shape[:2]
    qb = jnp.moveaxis(q.reshape((b, n // block, block) + q.shape[2:]), 1, 0)
    out = jnp.moveaxis(lax.map(fn, qb), 0, 1)
    return out.reshape((b, n) + out.shape[3:])

def dense_attention(q, k, v):
    s = jnp.einsum('bqhd,bkhd->bhqk', q, k).astype(jnp.float32) * (q.shape[-1] ** -0.5)
    p = jax.nn.softmax(s, axis=-1).astype(v.dtype)
    return jnp.einsum('bhqk,bkhd->bqhd', p, v)

def diff_project(h, w_in, with_q):
    b, n, _ = h.shape
    k, v = jnp.split(h @ w_in[:, DA_WIDTH:], 2, axis=-1)
    k = k.reshape(b, n, DA_HEADS, 2, DA_HEAD_DIM)
    v = v.reshape(b, n, DA_HEADS, DA_V_DIM)
    q = (h @ w_in[:, :DA_WIDTH]).reshape(b, n, DA_HEADS, 2, DA_HEAD_DIM) if with_q else None
    return q, k, v

def rope_heads(t, ang_r, ang_c):
    b, n = t.shape[:2]
    return axial_rope(t.reshape(b, n, -1, DA_HEAD_DIM), ang_r, ang_c).reshape(t.shape)

def diff_attend(q, k, v, lam):
    s = jnp.einsum('bqhjd,bkhjd->bhjqk', q, k).astype(jnp.float32) * (DA_HEAD_DIM ** -0.5)
    p = jax.nn.softmax(s, axis=-1)
    a = (p[:, :, 0] - lam * p[:, :, 1]).astype(v.dtype)
    return jnp.einsum('bhqk,bkhe->bqhe', a, v)

def diff_output(o, subln_g, lam_init, w_out):
    b, n = o.shape[:2]
    o = rmsnorm(o, subln_g) * (1.0 - lam_init)
    return o.reshape(b, n, DA_WIDTH) @ w_out

def diff_attention_mixer(hx, hc, w_in, lq1, lk1, lq2, lk2, subln_g, w_out, lam_init, ang_r, ang_c, ctx_out):
    q, k, v = diff_project(hx, w_in, True)
    q = rope_heads(q, ang_r, ang_c)
    k = rope_heads(k, ang_r, ang_c)
    qc, kc, vc = diff_project(hc, w_in, ctx_out)
    lam = (jnp.exp(jnp.sum(lq1.astype(jnp.float32) * lk1.astype(jnp.float32)))
           - jnp.exp(jnp.sum(lq2.astype(jnp.float32) * lk2.astype(jnp.float32))) + lam_init)
    k_all = jnp.concatenate([kc, k], axis=1)
    v_all = jnp.concatenate([vc, v], axis=1)
    o = query_blocks(lambda qb: diff_attend(qb, k_all, v_all, lam), q, DA_Q_BLOCK)
    y = diff_output(o, subln_g, lam_init, w_out)
    yc = diff_output(diff_attend(qc, kc, vc, lam), subln_g, lam_init, w_out) if ctx_out else None
    return y, yc

def chunk_gmlp(h, w_in, v_g, w_s, b_s, w_out):
    b, n, _ = h.shape
    u, v = jnp.split(jax.nn.gelu(h @ w_in), 2, axis=-1)
    v = rmsnorm(v, v_g)
    v = v.reshape(b, n // GM_CHUNK, GM_CHUNK, GM_GROUPS, GM_GROUP_DIM)
    sv = jnp.einsum('gpq,bcqge->bcpge', w_s, v) + jnp.swapaxes(b_s, 0, 1)[:, :, None]
    return (u * sv.reshape(b, n, GM_WIDTH)) @ w_out

def natten_latent(q, k, v, k_ctx, v_ctx, rpb):
    b, n, h, d = q.shape
    rows = n // GRID_W
    wr = min(NA_WIN_R, rows)
    n_cb = GRID_W // NA_COL_BLOCK
    qg = q.reshape(b, rows, GRID_W, h, d)
    kg = k.reshape(b, rows, GRID_W, h, d)
    vg = v.reshape(b, rows, GRID_W, h, d)
    band_start = np.clip(np.arange(n_cb) * NA_COL_BLOCK - NA_COL_BLOCK // 2, 0, GRID_W - NA_COL_BAND)
    band_cols = band_start[:, None] + np.arange(NA_COL_BAND)
    q_cols = np.arange(GRID_W).reshape(n_cb, NA_COL_BLOCK)
    win_c0 = np.clip(q_cols - NA_WIN_C // 2, 0, GRID_W - NA_WIN_C)
    kc_b = band_cols[:, None, :]
    col_ok = (kc_b >= win_c0[:, :, None]) & (kc_b < win_c0[:, :, None] + NA_WIN_C)
    dc_idx = np.clip(kc_b - q_cols[:, :, None] + NA_WIN_C - 1, 0, 2 * NA_WIN_C - 2)
    scale = d ** -0.5

    def one_row(r):
        r0 = jnp.clip(r - wr // 2, 0, rows - wr)
        kb = lax.dynamic_slice_in_dim(kg, r0, wr, axis=1)[:, :, band_cols]
        vb = lax.dynamic_slice_in_dim(vg, r0, wr, axis=1)[:, :, band_cols]
        qr = lax.dynamic_index_in_dim(qg, r, axis=1, keepdims=False).reshape(b, n_cb, NA_COL_BLOCK, h, d)
        dr = r0 + jnp.arange(wr) - r
        bias = rpb[:, dr + NA_WIN_R - 1][:, :, dc_idx]
        bias = jnp.transpose(bias, (0, 2, 3, 1, 4))
        s_loc = jnp.einsum('bjqhd,brjkhd->bhjqrk', qr, kb).astype(jnp.float32) * scale + bias
        s_loc = jnp.where(col_ok[:, :, None, :], s_loc, NEG_INF)
        s_ctx = jnp.einsum('bjqhd,bkhd->bhjqk', qr, k_ctx).astype(jnp.float32) * scale
        s = jnp.concatenate([s_loc.reshape(b, h, n_cb, NA_COL_BLOCK, wr * NA_COL_BAND), s_ctx], axis=-1)
        p = jax.nn.softmax(s, axis=-1).astype(v.dtype)
        p_loc = p[..., :wr * NA_COL_BAND].reshape(b, h, n_cb, NA_COL_BLOCK, wr, NA_COL_BAND)
        p_ctx = p[..., wr * NA_COL_BAND:]
        o = (jnp.einsum('bhjqrk,brjkhd->bjqhd', p_loc, vb)
             + jnp.einsum('bhjqk,bkhd->bjqhd', p_ctx, v_ctx))
        return o.reshape(b, GRID_W, h, d)

    out = lax.map(one_row, jnp.arange(rows))
    return jnp.moveaxis(out, 0, 1).reshape(b, n, h, d)

def natten_mixer(hx, hc, w_in, rpb, w_out, ctx_out):
    b, n, _ = hx.shape
    lc = hc.shape[1]
    q, k, v = [t.reshape(b, n, NA_HEADS, NA_HEAD_DIM) for t in jnp.split(hx @ w_in, 3, axis=-1)]
    kc, vc = [t.reshape(b, lc, NA_HEADS, NA_HEAD_DIM) for t in jnp.split(hc @ w_in[:, NA_WIDTH:], 2, axis=-1)]
    y = natten_latent(q, k, v, kc, vc, rpb).reshape(b, n, NA_WIDTH) @ w_out
    yc = None
    if ctx_out:
        qc = (hc @ w_in[:, :NA_WIDTH]).reshape(b, lc, NA_HEADS, NA_HEAD_DIM)
        yc = dense_attention(qc, kc, vc).reshape(b, lc, NA_WIDTH) @ w_out
    return y, yc

def fourier_mix(h, w_out):
    b, n, d = h.shape
    hg = h.astype(jnp.float32).reshape(b, n, FN_GROUPS, d // FN_GROUPS)
    f = jnp.real(jnp.fft.fftn(hg, axes=(1, 3), norm='ortho'))
    return f.reshape(b, n, d).astype(h.dtype) @ w_out

def expert_choice_moe(h, w_router, w_gate, w_up, w_down):
    b, n, d = h.shape
    cap = EC_CAPACITY_FACTOR * n // N_EXPERTS
    aff = jax.nn.softmax((h @ w_router).astype(jnp.float32), axis=-1)
    top_aff, top_idx = lax.top_k(jnp.swapaxes(aff, 1, 2), cap)
    idx = top_idx.reshape(b, N_EXPERTS * cap)
    bidx = jnp.arange(b)[:, None]
    xs = h[bidx, idx].reshape(b, N_EXPERTS, cap, d)
    hid = jax.nn.silu(jnp.einsum('becd,edf->becf', xs, w_gate)) * jnp.einsum('becd,edf->becf', xs, w_up)
    ys = jnp.einsum('becf,efd->becd', hid, w_down) * top_aff[..., None].astype(h.dtype)
    return jnp.zeros_like(h).at[bidx, idx].add(ys.reshape(b, N_EXPERTS * cap, d))

def setup_inputs(seed: int = 0) -> dict:
    key = jax.random.key(seed)
    keys = iter(jax.random.split(key, 40))

    def nrm(shape, scale):
        return jax.random.normal(next(keys), shape, jnp.float32) * scale

    def gain(shape):
        return 1.0 + nrm(shape, 0.02)

    n_a, n_b, n_c, n_d = [len(range(kind, DEPTH, N_MIXERS)) for kind in range(N_MIXERS)]
    d = D_MODEL
    return {
        'x': nrm((BATCH, SEQ, d), 1.0),
        'c': nrm((BATCH, d), 1.0),
        'ctx': nrm((BATCH, CTX_LEN, d), 1.0),
        'c_ctx': nrm((d,), 1.0),
        'ada_w': nrm((DEPTH, d, 6 * d), 0.5 * d ** -0.5),
        'ada_b': nrm((DEPTH, 6 * d), 0.01),
        'mixer_norm_g': gain((DEPTH, d)),
        'moe_norm_g': gain((DEPTH, d)),
        'router_w': nrm((DEPTH, d, N_EXPERTS), d ** -0.5),
        'moe_w_gate': nrm((DEPTH, N_EXPERTS, d, EXPERT_DIM), d ** -0.5),
        'moe_w_up': nrm((DEPTH, N_EXPERTS, d, EXPERT_DIM), d ** -0.5),
        'moe_w_down': nrm((DEPTH, N_EXPERTS, EXPERT_DIM, d), EXPERT_DIM ** -0.5),
        'da_w_in': nrm((n_a, d, 3 * DA_WIDTH), d ** -0.5),
        'da_lambda_q1': nrm((n_a, DA_HEAD_DIM), 0.1),
        'da_lambda_k1': nrm((n_a, DA_HEAD_DIM), 0.1),
        'da_lambda_q2': nrm((n_a, DA_HEAD_DIM), 0.1),
        'da_lambda_k2': nrm((n_a, DA_HEAD_DIM), 0.1),
        'da_subln_g': gain((n_a, DA_V_DIM)),
        'da_w_out': nrm((n_a, DA_WIDTH, d), DA_WIDTH ** -0.5),
        'gm_w_in': nrm((n_b, d, 2 * GM_WIDTH), d ** -0.5),
        'gm_v_g': gain((n_b, GM_WIDTH)),
        'gm_w_s': nrm((n_b, GM_GROUPS, GM_CHUNK, GM_CHUNK), GM_CHUNK ** -0.5),
        'gm_b_s': 1.0 + nrm((n_b, GM_GROUPS, GM_CHUNK), 0.02),
        'gm_w_out': nrm((n_b, GM_WIDTH, d), GM_WIDTH ** -0.5),
        'na_w_in': nrm((n_c, d, 3 * NA_WIDTH), d ** -0.5),
        'na_rpb': nrm((n_c, NA_HEADS, 2 * NA_WIN_R - 1, 2 * NA_WIN_C - 1), 0.1),
        'na_w_out': nrm((n_c, NA_WIDTH, d), NA_WIDTH ** -0.5),
        'fn_w_out': nrm((n_d, d, d), d ** -0.5),
        'final_norm_g': gain((d,)),
    }

def reference(x, c, ctx, c_ctx, ada_w, ada_b, mixer_norm_g, moe_norm_g, router_w,
              moe_w_gate, moe_w_up, moe_w_down,
              da_w_in, da_lambda_q1, da_lambda_k1, da_lambda_q2, da_lambda_k2, da_subln_g, da_w_out,
              gm_w_in, gm_v_g, gm_w_s, gm_b_s, gm_w_out,
              na_w_in, na_rpb, na_w_out, fn_w_out, final_norm_g):
    n_tok = x.shape[1]
    ang_r, ang_c = axial_rope_angles(n_tok, DA_HEAD_DIM)
    readers = [i for i in range(DEPTH) if i % N_MIXERS in CTX_READERS]
    last_reader = max(readers) if readers else -1
    for i in range(DEPTH):
        kind, j = i % N_MIXERS, i // N_MIXERS
        need_ctx = i <= last_reader
        update_ctx = i < last_reader
        sh1, sc1, g1, sh2, sc2, g2 = adaln_params(c, ada_w[i], ada_b[i], 6)
        hx = modulate(rmsnorm(x, mixer_norm_g[i]), sh1, sc1)
        hc = None
        if need_ctx:
            cmod = adaln_params(c_ctx[None, :], ada_w[i], ada_b[i], 6 if update_ctx else 3)
            hc = modulate(rmsnorm(ctx, mixer_norm_g[i]), cmod[0], cmod[1])
        if kind == MIX_DIFF:
            lam_init = 0.8 - 0.6 * math.exp(-0.3 * i)
            y, yc = diff_attention_mixer(hx, hc, da_w_in[j], da_lambda_q1[j], da_lambda_k1[j],
                                         da_lambda_q2[j], da_lambda_k2[j], da_subln_g[j], da_w_out[j],
                                         lam_init, ang_r, ang_c, update_ctx)
        elif kind == MIX_GMLP:
            y = chunk_gmlp(hx, gm_w_in[j], gm_v_g[j], gm_w_s[j], gm_b_s[j], gm_w_out[j])
            yc = chunk_gmlp(hc, gm_w_in[j], gm_v_g[j], gm_w_s[j], gm_b_s[j], gm_w_out[j]) if update_ctx else None
        elif kind == MIX_NATTEN:
            y, yc = natten_mixer(hx, hc, na_w_in[j], na_rpb[j], na_w_out[j], update_ctx)
        else:
            y = fourier_mix(hx, fn_w_out[j])
            yc = fourier_mix(hc, fn_w_out[j]) if update_ctx else None
        x = x + g1 * y
        hx = modulate(rmsnorm(x, moe_norm_g[i]), sh2, sc2)
        x = x + g2 * expert_choice_moe(hx, router_w[i], moe_w_gate[i], moe_w_up[i], moe_w_down[i])
        if update_ctx:
            ctx = ctx + cmod[2] * yc
            hc = modulate(rmsnorm(ctx, moe_norm_g[i]), cmod[3], cmod[4])
            ctx = ctx + cmod[5] * expert_choice_moe(hc, router_w[i], moe_w_gate[i], moe_w_up[i], moe_w_down[i])
    return rmsnorm(x, final_norm_g)


_drawn_inputs = setup_inputs


def setup_inputs(seed=0):
    import zlib

    import numpy as np

    out = dict(_drawn_inputs(seed))
    spreads = {}
    factors = {'ada_b': 3.028,
     'mixer_norm_g': 6.823,
     'moe_norm_g': 6.159,
     'da_lambda_q1': 6.556,
     'da_lambda_k1': 8.0,
     'da_lambda_q2': 6.363,
     'da_lambda_k2': 8.0,
     'da_subln_g': 8.0,
     'gm_v_g': 8.0,
     'gm_b_s': 8.0,
     'final_norm_g': 2.719}
    for name, (base, spread) in spreads.items():
        noise = np.random.default_rng([zlib.crc32(name.encode()), seed]).standard_normal(out[name].shape)
        drawn = base * np.exp(spread * noise) if base else spread * noise
        out[name] = jnp.asarray(drawn.astype(out[name].dtype))
    for name, factor in factors.items():
        out[name] = (out[name] * factor).astype(out[name].dtype)
    return out
```

```python
from contextlib import ExitStack

import numpy as np

import concourse.bass as bass
from concourse import mybir

F32 = mybir.dt.float32
F32R = mybir.dt.float32r
BF16 = mybir.dt.bfloat16
I32 = mybir.dt.int32
ALU = mybir.AluOpType
ACT = mybir.ActivationFunctionType
AX = mybir.AxisListType

P = 128
D = 1024
DT = D // P
SEQ = 512
TT = SEQ // P
CTX = 256
CT = CTX // P
KEYS = CTX + SEQ
KT = KEYS // P
GRID_W = 64
EPS = 1e-6
HEADS = 8
HD = 64
LAM_INIT = 0.2
SUB_SCALE = 1.0 - LAM_INIT
GW = 2048
GROUPS = 8
NE = 16
CAP = 64
KB = 1024

R_C, R_CC, R_MIX, R_MOE, R_FIN, R_SUB, R_VG, R_N = 0, 8, 16, 32, 48, 56, 57, 73


def rope_tables():
    n = HD // 4
    inv = (np.float32(10000.0) ** (-np.arange(n, dtype=np.float32) / np.float32(n))).astype(np.float32)
    t = np.arange(SEQ)
    rows, cols = (t // GRID_W).astype(np.float32), (t % GRID_W).astype(np.float32)
    cos, sin = np.zeros((P, SEQ), np.float32), np.zeros((P, SEQ), np.float32)
    for p in range(P):
        r = p % HD
        ang = ((rows if r < 32 else cols) * inv[r % 16]).astype(np.float32)
        cos[p] = np.cos(ang)
        sin[p] = np.sin(ang) * (-1.0 if r % 32 < 16 else 1.0)
    return cos, sin


def shape_constants():
    cos, sin = rope_tables()
    ident = np.eye(P, dtype=np.float32)
    tri = np.triu(np.ones((P, P), np.float32))
    slots = np.broadcast_to(np.arange(1, CAP + 1, dtype=np.float32), (P, CAP))
    return np.ascontiguousarray(np.concatenate([cos, sin, ident, tri, slots], axis=1))


def build(nc, ctx, t, out):
    base = 16512

    def at(name, kb, shape, dt=F32):
        return nc.alloc_sbuf_tensor_at(name, shape, dt, offset=base + int(kb * KB))

    cursor = [16 * KB]

    def small(name, shape, dt=F32):
        a = nc.alloc_sbuf_tensor_at(name, shape, dt, offset=base + cursor[0])
        size = int(np.prod(shape[1:])) * (2 if dt == BF16 else 4)
        cursor[0] += (size + 31) // 32 * 32
        assert cursor[0] <= 26 * KB
        return a

    def sem(name):
        return ctx.enter_context(nc.semaphore(name))

    XT = at("XT", 0, [P, DT, SEQ])
    ident = small("ident", [P, P])
    ident_r = small("ident_r", [P, P], F32R)
    ones = small("ones", [P, P])
    slots = small("slots", [P, CAP])
    tri = small("tri", [P, P], BF16)
    ones_b = small("ones_b", [P, P], BF16)
    CT1 = small("CT1", [P, R_N])
    CT2 = small("CT2", [P, 96])
    silu_c = small("silu_c", [P, DT, 32])
    MOD = small("MOD", [P, 2, 48])
    MODC = small("MODC", [P, 16])
    coef = small("coef", [P, 5, DT])
    rw = small("rw", [P, 2, DT, NE])
    lam4 = at("lam4", 120, [P, 4, HD])
    lam_s = small("lam_s", [P, 4])
    neg_lam = small("neg_lam", [P, 1])
    subg = small("subg", [P, 1])
    nv = small("nv", [P, HEADS * TT])
    ny = small("ny", [P, HEADS * TT])
    na = small("na", [P, HEADS * TT])
    row_max = small("row_max", [P, 2])
    row_bias = small("row_bias", [P, 2, 2])
    row_sum = small("row_sum", [P, 2, 2])
    row_ratio = small("row_ratio", [P, 2, 2])
    sum_all = small("sum_all", [P, HEADS * TT])
    AFF = small("AFF", [P, TT, NE])
    PM = small("PM", [P, TT, NE])
    MB = small("MB", [P, TT, NE], BF16)
    LG = small("LG", [P, TT, NE])
    st4 = small("st4", [P, 2, TT])
    aff_c = small("aff_c", [P, 2])
    vsq = small("vsq", [P, TT, 4])

    XR = at("XR", 58, [P, TT, D])
    CR = at("CR", 74, [P, CT, D])
    CXT = at("CXT", 82, [P, DT, CTX])
    SQ0 = at("SQ0", 90, [P, DT, SEQ])
    SQC = at("SQC", 111, [P, DT, CTX])
    DGC = at("DGC", 119, [P, CT, P])
    ROWS1 = at("ROWS1", 106, [R_N, P])
    ROWS2 = at("ROWS2", 107, [96, P])
    TRI0 = at("TRI0", 108, [P, P])
    U0 = at("U0", 58, [P, DT, SEQ])
    UC0 = at("UC0", 74, [P, DT, CTX])
    DG0 = at("DG0", 109, [P, TT, P])
    H0h = at("H0h", 122, [P, DT, KEYS], F32R)
    H0l = at("H0l", 146, [P, DT, KEYS], F32R)
    RA, RW_ = 8, 3
    rawa = [at(f"rawa_{i}", 26 + 4 * i, [P, 1024]) for i in range(RA)]
    raww = [at(f"raww_{i}", 186 + 4 * i, [P, 4, 256]) for i in range(RW_)]
    st0h = [at(f"st0h_{i}", 170 + 8 * i, [P, 4, 256], F32R) for i in range(2)]
    st0l = [at(f"st0l_{i}", 174 + 8 * i, [P, 4, 256], F32R) for i in range(2)]
    QF = at("QF", 58, [P, HEADS, SEQ])
    KF = at("KF", 74, [P, HEADS, KEYS])
    VF = at("VF", 98, [P, KT, D])
    COS = at("COS", 198, [P, SEQ])
    SIN = at("SIN", 200, [P, SEQ])
    QT = at("QT", 202, [P, KEYS])
    RT = at("RT", 205, [P, SEQ])
    ADS = small("ADS", [P, SEQ])
    Qh = [at(f"Qh{i}", 122 + 14 * i, [P, 2, SEQ], F32R) for i in range(2)]
    Ql = [at(f"Ql{i}", 126 + 14 * i, [P, 2, SEQ], F32R) for i in range(2)]
    Kh = [at(f"Kh{i}", 130 + 14 * i, [P, KEYS], F32R) for i in range(2)]
    Kl = [at(f"Kl{i}", 133 + 14 * i, [P, KEYS], F32R) for i in range(2)]
    AT = [at(f"AT{i}", 150 + 3 * i, [P, KT, P]) for i in range(2)]
    E = [at(f"E{i}", 162 + 6 * i, [P, 2, KEYS]) for i in range(4)]
    OSQ = [at(f"OSQ{i}", 156 + 0.5 * i, [P, P]) for i in range(2)]
    VB = [at(f"VB{i}", (46, 157)[i], [P, KT, P]) for i in range(2)]
    OF = at("OF", 26, [P, HEADS, SEQ])
    DGA = [at("DGA0", 42, [P, TT, P]), at("DGA1", 44, [P, TT, P])]
    OHh = at("OHh", 122, [P, HEADS, SEQ], F32R)
    OHl = at("OHl", 138, [P, HEADS, SEQ], F32R)
    rawo = [at(f"rawo_{i}", (50, 54, 186, 190, 194, 198, 202, 170)[i], [P, 2, 512]) for i in range(8)]
    stoh = [at(f"stoh_{i}", 154 + 8 * i, [P, 2, 512], F32R) for i in range(2)]
    stol = [at(f"stol_{i}", 158 + 8 * i, [P, 2, 512], F32R) for i in range(2)]
    WR = 6
    ring = [at(f"ring_{i}", 26 + 16 * i, [P, 4, D]) for i in range(WR)]
    HHt = at("HHt", 122, [P, TT, D], F32R)
    HLt = at("HLt", 138, [P, TT, D], F32R)
    HT = at("HT", 154, [P, DT, SEQ])
    ACC = at("ACC", 154, [P, DT, SEQ])
    SQ = at("SQ", 170, [P, DT, SEQ])
    DG = at("DG", 186, [P, TT, P])
    WK = at("WK", 200, [NE, SEQ])
    MKT = at("MKT", 202, [NE, SEQ])
    M8 = at("M8", 204, [NE, 8])
    XS = at("XS", 170, [P, DT, P])
    OH = at("OH", 178, [P, TT, P], F32R)
    SM = at("SM", 180, [P, SEQ], F32R)
    SG = at("SG", 182, [P, SEQ])
    HID = at("HID", 184, [P, SEQ])
    HIDT = at("HIDT", 186, [P, TT, P])
    YS = at("YS", 188, [P, D])
    YH = at("YH", 192, [P, D], F32R)
    YL = at("YL", 196, [P, D], F32R)
    H1h = at("H1h", 26, [P, DT, SEQ], F32R)
    H1l = at("H1l", 42, [P, DT, SEQ], F32R)
    U1 = at("U1", 58, [P, DT, SEQ])
    SQ1 = at("SQ1", 74, [P, DT, SEQ])
    DG1 = at("DG1", 94, [P, TT, P])
    RWh = at("RWh", 58, [P, TT, D], F32R)
    RWl = at("RWl", 74, [P, TT, D], F32R)
    WSR = at("WSR", 90, [P, GROUPS, P])
    UT = at("UT", 90, [P, 4, SEQ])
    WST = at("WST", 98, [P, GROUPS, P])
    BSB = at("BSB", 102, [P, GROUPS, P])
    stgh = [at(f"stgh_{i}", 106 + 8 * i, [P, 2, 512], F32R) for i in range(2)]
    stgl = [at(f"stgl_{i}", 110 + 8 * i, [P, 2, 512], F32R) for i in range(2)]
    VH = at("VH", 122, [P, 16, TT, P], F32R)
    VL = at("VL", 154, [P, 16, TT, P], F32R)
    RAWG = 4
    rawg = [at(f"rawg_{i}", 186 + 4 * i, [P, 2, 512]) for i in range(RAWG)]
    VT = at("VT", 202, [P, 512])
    GT = at("GT", 204, [P, 512])
    SQV = at("SQV", 94, [P, 512])
    FG = at("FG", 26, [P, DT, SEQ])
    FO = at("FO", 42, [P, TT, D])
    FSQ = at("FSQ", 58, [P, DT, SEQ])

    bank = [ctx.enter_context(nc.psum_tensor(f"bank{i}", [P, 512], F32)) for i in range(2)]
    sc_a = ctx.enter_context(nc.psum_tensor("sc_a", [P, 1536], F32))
    sc_b = ctx.enter_context(nc.psum_tensor("sc_b", [P, 1536], F32))
    SCP = [sc_a, sc_b]
    PB = [bank[0][:, :], bank[1][:, :]] + [s[:, 512 * i:512 * i + 512] for s in SCP for i in range(3)]

    s_small = sem("small_loads_landed")
    s_xload = sem("x_landed")
    s_cload = sem("ctx_landed")
    s_const = sem("constants_ready")
    s_rowT = sem("rows_transposed")
    s_ct = sem("columns_copied")
    s_silu = sem("silu_c_ready")
    s_xtT = sem("stream_blocks_transposed")
    s_xtc = sem("stream_blocks_copied")
    s_aland = [sem(f"ada_landed_{i}") for i in range(RA)]
    s_wland = [sem(f"w_landed_{i}") for i in range(RW_)]
    s_ada = sem("ada_piece_used")
    s_ads = sem("ada_sums_copied")
    s_adt = sem("ada_sums_transposed")
    s_mod = sem("modulation_ready")
    s_coef = sem("norm_coefficients_ready")
    s_dve = sem("vector_chain")
    s_act = sem("scalar_chain")

    class Norm:

        TOTAL = dict(squares=DT, sums=1, diag=1, spread=1, scaled=DT, hi=DT, lo=DT)
        sems = {k: sem(f"norm_{k}") for k in TOTAL}

        def __init__(self, before, split_before):
            self.before, self.split_before = before, split_before

        def __getitem__(self, name):
            return self.sems[name]

        def __call__(self, name, n):
            return self.sems[name], n + self.TOTAL[name] * (self.split_before if name == "lo" else self.before)

    nx, nc_, nm0, ng, nm1 = Norm(0, 0), Norm(1, 1), Norm(2, 2), Norm(3, 2), Norm(4, 3)
    s_hi = sem("w_hi_ready")
    s_lo = sem("w_lo_ready")
    s_pw = sem("w_piece_used")
    s_evq = sem("q_sums_copied")
    s_evk = sem("k_sums_copied")
    s_evv = sem("v_sums_copied")
    s_shuf = sem("rope_halves_swapped")
    s_sin = sem("rope_sine_applied")
    s_cos = sem("rope_cosine_applied")
    s_rope = sem("rope_done")
    s_vl = sem("v_lo_ready")
    s_lam = sem("lambda_exponentials_ready")
    s_lamr = sem("lambda_sums_ready")

    def need(eng, s, n):
        if not isinstance(n, int) or n > 0:
            eng.wait_ge(s, n)

    class Chain:

        def __init__(self, eng, s):
            self.eng, self.s, self.n = eng, s, 0

        def link(self, ins):
            ins.then_inc(self.s, 1)
            self.n = self.n + 1
            self.eng.wait_ge(self.s, self.n)

    HEAD_SWEEPS = [(0, 0), (1, 0)]
    HEAD_PIECES = 16 * len(HEAD_SWEEPS)
    STEP = []
    for n, extra in enumerate((3, 3, 3, 3, 4, 0)):
        STEP.append(("w", n // 2, n % 2))
        done = sum(kind == "a" for kind, _, _ in STEP)
        STEP += [("a", done + j, 0) for j in range(extra)]

    SMALL_LOADS = []
    for r0, name in ((R_C, "c"), (R_CC, "c_ctx"), (R_MIX, "mixer_norm_g"), (R_MOE, "moe_norm_g"), (R_FIN, "final_norm_g"),
                     (R_SUB, "da_subln_g"), (R_VG, "gm_v_g")):
        src = t[name] if len(t[name].shape) == 1 else t[name].rearrange("a n -> (a n)")
        rows = src.rearrange("(r p) -> r p", p=P)
        SMALL_LOADS.append((ROWS1[r0:r0 + rows.shape[0], :], rows))
    SMALL_LOADS.append((ROWS2[:, :], t["ada_b"].rearrange("a n -> (a n)").rearrange("(r p) -> r p", p=P)))
    SMALL_LOADS += [(ident[:, :], t["shape_constants"][:, 1024:1152]), (TRI0[:, :], t["shape_constants"][:, 1152:1280]),
                    (slots[:, :], t["shape_constants"][:, 1280:1344]), (COS[:, :], t["shape_constants"][:, 0:512]),
                    (SIN[:, :], t["shape_constants"][:, 512:1024])]
    SMALL_LOADS += [(rw[:, i, :, :], t["router_w"][i].rearrange("(a p) n -> p a n", p=P)) for i in range(2)]
    SMALL_LOADS += [(lam4[:, i, :], t[name].partition_broadcast(P).rearrange("p a n -> p (a n)"))
                    for i, name in enumerate(("da_lambda_q1", "da_lambda_k1", "da_lambda_q2", "da_lambda_k2"))]
    SMALL = 16 * len(SMALL_LOADS)

    def three(out_, wh, wl, xh, xl, first, last, **kw):
        nc.tensor.matmul(out_, wh, xh, start=first, stop=False, **kw)
        nc.tensor.matmul(out_, wh, xl, start=False, stop=False, **kw)
        return nc.tensor.matmul(out_, wl, xh, start=False, stop=last, **kw)

    def pe_sums(pe, N, sq, acc, tokens):
        n = tokens // P
        for d in range(DT):
            pe.wait_ge(*N("squares", d + 1))
            for i in range(n):
                mm = nc.tensor.matmul(acc[:, i:i + 1], sq[:, d, i * P:(i + 1) * P], ones[:, 0:1],
                                      start=(d == 0 and i == 0), stop=(d == DT - 1), skip_group_check=True)
        mm.then_inc(N["sums"], 1)

    def pe_spread(pe, done, dg, acc, n):
        for i in range(n):
            mm = nc.tensor.matmul(acc[:, i * P:(i + 1) * P], ones[:, :], dg[:, i, :], start=True, stop=True)
        mm.then_inc(done, 1)

    def rsqrt(ch, sums, n, scale):
        v, y, a = nv[:, 0:n], ny[:, 0:n], na[:, 0:n]
        ch.link(nc.vector.tensor_scalar(v, sums, scale, EPS, ALU.mult, ALU.add))
        ch.link(nc.vector.tensor_scalar(y.bitcast(I32), v.bitcast(I32), 1, None, ALU.logical_shift_right))
        ch.link(nc.vector.tensor_scalar(y.bitcast(I32), y.bitcast(I32), -1.0, float(0x5F3759DF), ALU.mult, ALU.add))
        for _ in range(3):
            ch.link(nc.vector.tensor_tensor(a, y, y, ALU.mult))
            ch.link(nc.vector.scalar_tensor_tensor(a, a, -0.5, v, ALU.mult, ALU.mult))
            ch.link(nc.vector.scalar_tensor_tensor(y, a, 1.5, y, ALU.add, ALU.mult))

    def diagonal(dg, n, done):
        for i in range(n):
            ins = nc.vector.tensor_scalar(dg[:, i, :], ident[:, :], ny[:, i:i + 1], None, ALU.mult)
        ins.then_inc(done, 1)

    def act_squares(act, N, src, sq, tokens, ready=None):
        for d in range(DT):
            if ready is not None:
                act.wait_ge(ready[0], ready[1](d))
            nc.scalar.activation(sq[:, d, 0:tokens], src[:, d, 0:tokens], ACT.Square).then_inc(N["squares"], 1)

    def sp_projections(sp):
        for n in range(HEAD_PIECES):
            layer, b = HEAD_SWEEPS[n // 16]
            kt, half = n % 16 // 2, n % 2
            if n >= RA:
                sp.wait_ge(s_ada, n - RA + 1)
            c0 = b * 2048 + half * 1024
            sp.dma_start(rawa[n % RA][:, :], t["ada_w"][layer, kt * P:(kt + 1) * P, c0:c0 + 1024]).then_inc(
                s_aland[n % RA], 16)
        with sp.Fori(0, 2) as body:
            for step in range(2):
                for kind, m, half in STEP:
                    if kind == "w":
                        k = step * 6 + m * 2 + half
                        sp.wait_ge(s_lo, body * 12 + (k + 1))
                        src = t["da_w_in"][0, half * 512:half * 512 + 512, :].rearrange("(a p) n -> p a n", p=P)
                        sp.dma_start(raww[k % RW_][:, :, :], src[:, :, bass.ds(body * 512 + (m * D + step * 256), 256)]
                                     ).then_inc(s_wland[k % RW_], 16)
                    else:
                        k = step * 16 + m
                        sp.wait_ge(s_ada, body * 32 + (HEAD_PIECES + k - RA + 1))
                        kt, c0 = m // 2, (step + 1) * 2048 + m % 2 * 1024
                        src = t["ada_w"][bass.ds(body, 1), kt * P:(kt + 1) * P, c0:c0 + 1024]
                        sp.dma_start(rawa[k % RA][:, :], src.rearrange("a p n -> p (a n)")).then_inc(
                            s_aland[k % RA], 16)

    def pe_ada(pe, k, m, landed):
        pe.wait_ge(*landed)
        for j in range(2):
            g = 2 * (m % 2) + j
            mm = nc.tensor.matmul(PB[7][32 * g:32 * g + 32, :], silu_c[:, m // 2, :], rawa[k % RA][:, 512 * j:512 * j + 512],
                                  start=(m < 2), stop=(m >= 14))
        mm.then_inc(s_ada, 1)

    def pe_ada_columns(pe, n):
        pe.wait_ge(s_ads, n + 1)
        for b in range(4):
            mm = nc.tensor.transpose(PB[7][:, b * P:(b + 1) * P], ADS[:, b * P:(b + 1) * P], ident[:, :])
        mm.then_inc(s_adt, 1)

    def pe_head(pe):
        pe.wait_ge(s_small, SMALL)
        pe.wait_ge(s_const, 4)
        nc.tensor.transpose(PB[0][:, 0:R_N], ROWS1[:, :], ident[0:R_N, 0:R_N]).then_inc(s_rowT, 1)
        nc.tensor.transpose(PB[1][:, 0:96], ROWS2[:, :], ident[0:96, 0:96]).then_inc(s_rowT, 1)
        pe.wait_ge(s_silu, 2)
        for n in range(16):
            pe_ada(pe, n, n, (s_aland[n % RA], (n // RA + 1) * 16))
        pe.wait_ge(s_xload, 16)
        pe.wait_ge(s_cload, 16)
        pe.wait_ge(s_ct, 2)
        for n in range(12):
            if n >= 4:
                pe.wait_ge(s_xtc, n - 3)
            for j in range(4):
                src = XR[:, j, n * P:(n + 1) * P] if n < 8 else CR[:, j % 2, ((n - 8) * 2 + j // 2) * P:((n - 8) * 2 + j // 2) * P + P]
                mm = nc.tensor.transpose(PB[n % 4][:, j * P:(j + 1) * P], src, ident[:, :])
            mm.then_inc(s_xtT, 1)
        pe_ada_columns(pe, 0)
        pe.wait_ge(s_xtc, 12)
        pe_sums(pe, nx, SQ0, PB[1], SEQ)
        pe_sums(pe, nc_, SQC, PB[2], CTX)
        pe.wait_ge(*nx("diag", 1))
        pe_spread(pe, nx["spread"], DG0, PB[0], TT)
        pe.wait_ge(*nc_("diag", 1))
        pe_spread(pe, nc_["spread"], DGC, PB[3], CT)
        pe.wait_ge(s_mod, 1)
        for n in range(16, 32):
            pe_ada(pe, n, n - 16, (s_aland[n % RA], (n // RA + 1) * 16))
        pe_ada_columns(pe, 1)

    def pe_projections(pe):
        for N in (nx, nc_):
            pe.wait_ge(*N("hi", DT))
            pe.wait_ge(*N("lo", DT))
        with pe.Fori(0, 2) as body:
            for step in range(2):
                for kind, m, half in STEP:
                    if kind == "a":
                        k = step * 16 + m
                        if m == 0:
                            pe.wait_ge(s_mod, body * 2 + (step + 2))
                        pe_ada(pe, k, m, (s_aland[k % RA], body * 64 + (HEAD_PIECES // RA + k // RA + 1) * 16))
                        continue
                    k = step * 6 + m * 2 + half
                    wh, wl = st0h[k % 2], st0l[k % 2]
                    pe.wait_ge(s_lo, body * 12 + (RW_ + k + 1))
                    for j in range(4):
                        kt, first, last = half * 4 + j, half == 0 and j == 0, half == 1 and j == 3
                        if m == 0:
                            for h in range(2):
                                if first:
                                    pe.wait_ge(s_evv, body * 6 + (step * 3 + 2 + h))
                                w = slice(h * P, h * P + P)
                                mm = three(PB[h], wh[:, j, w], wl[:, j, w], H0h[:, kt, CTX:], H0l[:, kt, CTX:],
                                           first, last)
                        elif m == 1:
                            for h in range(2):
                                if first:
                                    pe.wait_ge(s_evk, body * 4 + (step * 2 + 1 + h))
                                w = slice(h * P, h * P + P)
                                for i in range(2):
                                    c = slice(i * 384, i * 384 + 384)
                                    mm = three(PB[2 + 2 * h + i][:, 0:384], wh[:, j, w], wl[:, j, w], H0h[:, kt, c],
                                               H0l[:, kt, c], first, last)
                        else:
                            for i in range(KT):
                                if first and i == 0:
                                    pe.wait_ge(s_evv, body * 6 + (step * 3 + 1))
                                if first and i in (2, 4):
                                    pe.wait_ge(s_evq, body * 4 + (step * 2 + i // 2))
                                c = slice(i * P, i * P + P)
                                mm = three(PB[(6, 0, 1)[i // 2]][:, i % 2 * 256:i % 2 * 256 + 256], H0h[:, kt, c],
                                           H0l[:, kt, c], wh[:, j, :], wl[:, j, :], first and i % 2 == 0, last,
                                           skip_group_check=True)
                    mm.then_inc(s_pw, 1)
                pe_ada_columns(pe, body * 2 + (step + 2))

    def act_head(act):
        for dst, src in SMALL_LOADS:
            act.dma_start(dst, src).then_inc(s_small, 16)
        act.dma_start(XR[:, :, :], t["x"][0].rearrange("(a p) n -> p a n", p=P)).then_inc(s_xload, 16)
        act.dma_start(CR[:, :, :], t["ctx"][0].rearrange("(a p) n -> p a n", p=P)).then_inc(s_cload, 16)
        act.wait_ge(s_rowT, 1)
        nc.scalar.activation(CT1[:, :], PB[0][:, 0:R_N], ACT.Copy).then_inc(s_ct, 1)
        act.wait_ge(s_rowT, 2)
        nc.scalar.activation(CT2[:, :], PB[1][:, 0:96], ACT.Copy).then_inc(s_ct, 1)
        act.wait_ge(s_const, 4)
        act.wait_ge(s_ct, 1)
        for r in range(2):
            nc.scalar.activation(silu_c[:, :, r], CT1[:, 8 * r:8 * r + 8], ACT.Silu).then_inc(s_silu, 1)
        act.wait_ge(s_lamr, 1)
        nc.scalar.activation(lam_s[:, 2:4], lam_s[:, 0:2], ACT.Exp).then_inc(s_lam, 1)
        act.wait_ge(s_ada, 16)
        nc.scalar.activation(ADS[:, :], PB[7], ACT.Copy).then_inc(s_ads, 1)
        act_squares(act, nx, XT, SQ0, SEQ, (s_xtc, lambda d: d + 1))
        act_squares(act, nc_, CXT, SQC, CTX, (s_xtc, lambda d: 9 + d // 2))
        for d in range(DT):
            act.wait_ge(*nx("scaled", d + 1))
            nc.scalar.activation(H0h[:, d, CTX:], U0[:, d, :], ACT.Identity, bias=MOD[:, 0, d:d + 1]).then_inc(nx["hi"], 1)
        for d in range(DT):
            act.wait_ge(*nc_("scaled", d + 1))
            nc.scalar.activation(H0h[:, d, 0:CTX], UC0[:, d, :], ACT.Identity, bias=MODC[:, d:d + 1]).then_inc(
                nc_["hi"], 1)
        act.wait_ge(s_adt, 1)
        act.wait_ge(s_ada, 32)
        nc.scalar.activation(ADS[:, :], PB[7], ACT.Copy).then_inc(s_ads, 1)

    def act_projections(act):
        def hi(body, k):
            act.wait_ge(s_wland[k % RW_], body * 64 + (k // RW_ + 1) * 16)
            act.wait_ge(s_pw, body * 12 + (k + 1))
            nc.scalar.activation(st0h[k % 2][:, :, :], raww[k % RW_][:, :, :], ACT.Copy).then_inc(s_hi, 1)

        def copy_sums(body, k, r, banks, width, done):
            for i, b in enumerate(banks):
                if i == 0:
                    act.wait_ge(s_pw, body * 12 + (k + 3))
                    act.wait_ge(s_shuf, body * 8 + (r + 1))
                ins = nc.scalar.activation(QT[:, i * width:i * width + width], PB[b][:, 0:width], ACT.Copy)
            ins.then_inc(done, 1)

        with act.Fori(0, 2) as body:
            for step in range(2):
                k = step * 6
                for j in range(3):
                    hi(body, k + j)
                for h in range(2):
                    copy_sums(body, k + 1, step * 4 + h, (h,), SEQ, s_evq)
                for j in range(3, 6):
                    hi(body, k + j)
                for h in range(2):
                    copy_sums(body, k + 3, step * 4 + 2 + h, (2 + 2 * h, 3 + 2 * h), 384, s_evk)
                act.wait_ge(s_ada, body * 32 + (HEAD_PIECES + 16 * (step + 1)))
                nc.scalar.activation(ADS[:, :], PB[7], ACT.Copy).then_inc(s_ads, 1)

    def dve_modulation(dve, n, dst, r, bias):
        src = PB[7].rearrange("p (b g r) -> p g b r", b=4, g=4)[:, :, :, r]
        return nc.vector.tensor_tensor(dst.rearrange("p (g b) -> p g b", g=4), src,
                                       bias.rearrange("p (g b) -> p g b", g=4), ALU.add)

    def dve_coef(ch, n, scale_cols, gain_cols):
        ch.link(nc.vector.scalar_tensor_tensor(coef[:, n, :], scale_cols, 1.0, gain_cols, ALU.add, ALU.mult))

    def dve_head(dve, ch):
        dve.wait_ge(s_small, SMALL)
        nc.vector.tensor_copy(tri[:, :], TRI0[:, :]).then_inc(s_const, 1)
        nc.vector.tensor_copy(ident_r[:, :], ident[:, :]).then_inc(s_const, 1)
        ch.link(nc.vector.tensor_tensor(lam4[:, 0:4:2, :], lam4[:, 0:4:2, :], lam4[:, 1:4:2, :], ALU.mult))
        nc.vector.tensor_reduce(lam_s[:, 0:2], lam4[:, 0:4:2, :], AX.X, ALU.add).then_inc(s_lamr, 1)
        for n in range(12):
            dve.wait_ge(s_xtT, n + 1)
            dst = XT[:, n, :] if n < 8 else CXT[:, 2 * (n - 8):2 * (n - 8) + 2, :].rearrange("p a n -> p (a n)")
            nc.vector.tensor_copy(dst, PB[n % 4]).then_inc(s_xtc, 1)
        dve.wait_ge(s_lam, 1)
        ch.link(nc.vector.scalar_tensor_tensor(neg_lam[:, :], lam_s[:, 3:4], -LAM_INIT, lam_s[:, 2:3], ALU.add,
                                               ALU.subtract))
        dve.wait_ge(s_ct, 2)
        ch.link(nc.vector.tensor_scalar(subg[:, :], CT1[:, R_SUB:R_SUB + 1], SUB_SCALE, None, ALU.mult))
        dve.wait_ge(s_adt, 1)
        dve_modulation(dve, 0, MODC[:, :], 1, CT2[:, 0:16])
        ch.link(dve_modulation(dve, 0, MOD[:, 0, 0:16], 0, CT2[:, 0:16]))
        dve_coef(ch, 0, MOD[:, 0, 8:16], CT1[:, R_MIX:R_MIX + 8])
        nc.vector.scalar_tensor_tensor(coef[:, 1, :], MODC[:, 8:16], 1.0, CT1[:, R_MIX:R_MIX + 8], ALU.add,
                                       ALU.mult).then_inc(s_mod, 1)
        dve.wait_ge(s_mod, 1)
        dve.wait_ge(*nx("sums", 1))
        rsqrt(ch, PB[1][:, 0:TT], TT, 1.0 / D)
        diagonal(DG0, TT, nx["diag"])
        dve.wait_ge(*nc_("sums", 1))
        dve.wait_ge(*nx("diag", 1))
        rsqrt(ch, PB[2][:, 0:CT], CT, 1.0 / D)
        diagonal(DGC, CT, nc_["diag"])
        for N, src, u, b, n, c0, B in ((nx, XT, U0, 0, 0, CTX, MOD[:, 0, :]), (nc_, CXT, UC0, 3, 1, 0, MODC[:, :])):
            tokens = SEQ if n == 0 else CTX
            dve.wait_ge(*N("spread", 1))
            for d in range(DT):
                nc.vector.scalar_tensor_tensor(u[:, d, :], src[:, d, :], coef[:, n, d:d + 1], PB[b][:, 0:tokens],
                                               ALU.mult, ALU.mult).then_inc(N["scaled"], 1)
            for d in range(DT):
                dve.wait_ge(*N("hi", d + 1))
                nc.vector.scalar_tensor_tensor(H0l[:, d, c0:c0 + tokens], u[:, d, :], B[:, d:d + 1],
                                               H0h[:, d, c0:c0 + tokens], ALU.add, ALU.subtract).then_inc(N["lo"], 1)
        dve.wait_ge(s_adt, 2)
        dve_modulation(dve, 1, MOD[:, 1, 0:16], 0, CT2[:, 48:64]).then_inc(s_mod, 1)

    def dve_projections(dve):
        with dve.Fori(0, 2) as body:
            for step in range(2):
                for r in range(4):
                    kind, h = r // 2, r % 2
                    idx = step * 4 + r
                    dve.wait_ge((s_evq, s_evk)[kind], body * 4 + (kind * 2 + step * 2 + h + 1))
                    dve.wait_ge(s_rope, body * 8 + (idx + 1))
                    lat = QT[:, 0:SEQ] if kind == 0 else QT[:, CTX:]
                    head = bass.ds(body * 4 + (step * 2 + h), 1)
                    if kind == 0:
                        dst = QF[:, head, :].rearrange("p a n -> p (a n)")
                    else:
                        dst = KF[:, head, CTX:].rearrange("p a n -> p (a n)")
                        nc.vector.tensor_scalar(KF[:, head, 0:CTX].rearrange("p a n -> p (a n)"), QT[:, 0:CTX], 1.0, None,
                                                ALU.mult)
                    nc.vector.tensor_tensor(dst, lat, COS[:, :], ALU.mult).then_inc(s_cos, 1)
                    nc.vector.stream_shuffle(RT[:, :], lat, [(i + 16) % 32 for i in range(32)]).then_inc(s_shuf, 1)
                    dve.wait_ge(s_cos, body * 8 + (idx + 1))
                    dve.wait_ge(s_sin, body * 8 + (idx + 1))
                    nc.vector.tensor_tensor(dst, dst, RT[:, :], ALU.add).then_inc(s_rope, 1)
                dve.wait_ge(s_pw, body * 12 + (step * 6 + 8))
                for i, b in enumerate((6, 0, 1)):
                    dst = VF[:, 2 * i:2 * i + 2, bass.ds(body * 512 + step * 256, 256)]
                    nc.vector.tensor_scalar(dst, PB[b].rearrange("p (a n) -> p a n", a=2), 1.0, None, ALU.mult).then_inc(
                        s_evv, 1)
                dve.wait_ge(s_adt, body * 2 + (step + 3))
                c = (step + 1) * 16
                dst = MOD[:, bass.ds(body, 1), c:c + 16].rearrange("p a n -> p (a n)")
                dve_modulation(dve, None, dst, 0, CT2[:, bass.ds(body * 48 + c, 16)]).then_inc(s_mod, 1)

    def pool_head(pool):
        nc.gpsimd.memset(ones[:, :], 1.0).then_inc(s_const, 1)
        nc.gpsimd.memset(silu_c[:, :, :], 0.0).then_inc(s_const, 1)
        nc.gpsimd.memset(ones_b[:, 0:32], 1.0).then_inc(s_lo, RW_)
        nc.gpsimd.memset(ones_b[:, 32:64], 1.0).then_inc(s_pw, 2)
        nc.gpsimd.memset(ones_b[:, 64:96], 1.0).then_inc(s_evv, 3)
        nc.gpsimd.memset(ones_b[:, 96:112], 1.0).then_inc(s_evk, 2)
        nc.gpsimd.memset(ones_b[:, 112:120], 1.0).then_inc(s_vl, 8)
        nc.gpsimd.memset(ones_b[:, 120:124], 1.0).then_inc(s_shuf, 1)
        nc.gpsimd.memset(ones_b[:, 124:128], 1.0).then_inc(s_rope, 1)

    def pool_projections(pool):
        def lo(body, k):
            pool.wait_ge(s_hi, body * 12 + (k + 1))
            nc.gpsimd.tensor_tensor(st0l[k % 2][:, :, :], raww[k % RW_][:, :, :], st0h[k % 2][:, :, :],
                                    ALU.subtract).then_inc(s_lo, 1)

        def sine(body, r):
            pool.wait_ge(s_shuf, body * 8 + (r + 2))
            nc.gpsimd.tensor_tensor(RT[:, :], RT[:, :], SIN[:, :], ALU.mult).then_inc(s_sin, 1)

        with pool.Fori(0, 2) as body:
            for step in range(2):
                for j in range(3):
                    lo(body, step * 6 + j)
                for h in range(2):
                    sine(body, step * 4 + h)
                for j in range(3, 6):
                    lo(body, step * 6 + j)
                for h in range(2):
                    sine(body, step * 4 + 2 + h)
    s_zero = sem("q_zeros_written")
    s_qkh = sem("qk_hi_ready")
    s_qkl = sem("qk_lo_ready")
    s_vb = sem("v_of_head_ready")
    s_sc = sem("scores_ready")
    s_bias = sem("maximum_ready")
    s_exp = sem("exponentials_ready")
    s_rat = sem("ratio_chain")
    s_comb = sem("softmaxes_combined")
    s_tra = sem("keys_0_to_3_transposed")
    s_trb = sem("keys_4_and_5_transposed")
    s_at = sem("transposes_copied")
    s_pv = sem("tile_times_v_ready")
    s_osq = sem("tile_output_copied")
    s_sub = sem("tile_squares_summed")
    PROJ_ADA = HEAD_PIECES + 64
    PROJ_PW = 2 + 24
    PV0 = 256
    SUMS0 = 384
    SLOTS = HEADS * TT

    def over_heads(eng, slot):
        for h in range(2):
            for qt in range(TT):
                slot(0, h, qt)
        with eng.Fori(1, HEADS // 2 - 1) as body:
            for h in range(2):
                for qt in range(TT):
                    slot(body * 2, h, qt)
        for h in range(2):
            for qt in range(TT):
                slot(HEADS - 2, h, qt)
        for qt in range(TT):
            slot(HEADS, 0, qt)

    def due(base, h, qt, late):
        if not isinstance(base, int):
            return True
        s = (base + h) * TT + qt - late
        return 0 <= s < SLOTS

    def begun(base, h, qt, late):
        return not isinstance(base, int) or (base + h) * TT + qt >= late

    def pe_attention(pe):
        pe.wait_ge(s_evv, 3 + 12)
        pe.wait_ge(s_evk, 2 + 4 * 2)
        pe.wait_ge(s_mod, 6)
        pe.wait_ge(s_zero, 1)

        def slot(base, h, qt):
            s = base * TT + (TT * h + qt)
            if due(base, h, qt, 0):
                if qt == 0:
                    pe.wait_ge(s_qkh, base * 3 + (3 * h + 3))
                    pe.wait_ge(s_qkl, base * 3 + (3 * h + 3))
                if due(base, h, qt, 2):
                    pe.wait_ge(s_exp, s - 1)
                S = SCP[qt % 2]
                q = slice(qt * P, qt * P + P)
                for j in range(2):
                    for c0, c1 in ((0, 512), (512, 768)) if j == 0 else ((0, 256), (256, 768)):
                        o0 = j * KEYS
                        mm = three(S[:, o0 + c0:o0 + c1], Qh[h][:, j, q], Ql[h][:, j, q], Kh[h][:, c0:c1],
                                   Kl[h][:, c0:c1], (j, c0) != (1, 0), True, skip_group_check=True)
                mm.then_inc(s_sc, 1)
            if due(base, h, qt, 3):
                pe.wait_ge(s_at, s * 2 - 4)
            if due(base, h, qt, 4):
                pe.wait_ge(s_osq, s - 3)
            if due(base, h, qt, 2):
                pe.wait_ge(s_comb, s - 1)
                src = E[(qt - 2) % 4]
                for kt in range(KT):
                    mm = nc.tensor.transpose(PB[kt // 4][:, kt % 4 * P:kt % 4 * P + P], src[:, 0, kt * P:kt * P + P],
                                             ident[:, :])
                    if kt in (3, 5):
                        mm.then_inc((s_tra, s_trb)[kt // 4], 1)
            if due(base, h, qt, 4):
                dst = PB[1][:, bass.ds(s + (SUMS0 - 4), 1)]
                nc.tensor.matmul(dst, OSQ[qt % 2][:, :], ones[:, 0:1], start=True, stop=True,
                                 skip_group_check=True).then_inc(s_sub, 1)
            if due(base, h, qt, 3):
                if qt == 3:
                    pe.wait_ge(s_vb, base + (h + 1))
                v = VB[h] if qt == 3 else VB[1 - h]
                for kt in range(KT):
                    mm = nc.tensor.matmul(PB[1][:, PV0:PV0 + P], v[:, kt, :], AT[(qt - 3) % 2][:, kt, :],
                                          start=(kt == 0), stop=(kt == KT - 1), skip_group_check=True)
                mm.then_inc(s_pv, 1)

        over_heads(pe, slot)

    def act_attention(act):
        act.wait_ge(s_pw, PROJ_PW)
        act.wait_ge(s_ada, PROJ_ADA)

        def slot(base, h, qt):
            s = base * TT + (TT * h + qt)
            if due(base, h, qt, 2):
                if due(base, h, qt, 5):
                    act.wait_ge(s_pv, s - 4)
                act.wait_ge(s_tra, s - 1)
                src = PB[0].rearrange("p (a n) -> p a n", a=4)
                nc.scalar.activation(AT[qt % 2][:, 0:4, :], src, ACT.Copy).then_inc(s_at, 1)
            if due(base, h, qt, 0):
                if due(base, h, qt, 4):
                    act.wait_ge(s_trb, s - 3)
                act.wait_ge(s_bias, s + 1)
                for j in range(2):
                    ins = nc.scalar.activation(E[qt][:, j, :], SCP[qt % 2][:, j * KEYS:(j + 1) * KEYS], ACT.Exp,
                                               bias=row_bias[:, qt % 2, j:j + 1], scale=HD ** -0.5,
                                               accum_out=row_sum[:, qt % 2, j:j + 1])
                ins.then_inc(s_exp, 1)
            if due(base, h, qt, 3):
                if due(base, h, qt, 5):
                    act.wait_ge(s_sub, s - 4)
                act.wait_ge(s_pv, s - 2)
            if due(base, h, qt, 2):
                act.wait_ge(s_trb, s - 1)
                src = PB[1][:, 0:2 * P].rearrange("p (a n) -> p a n", a=2)
                nc.scalar.activation(AT[qt % 2][:, 4:6, :], src, ACT.Copy).then_inc(s_at, 1)
            if due(base, h, qt, 3):
                nc.scalar.activation(OSQ[(qt - 3) % 2][:, :], PB[1][:, PV0:PV0 + P], ACT.Square)
                q = (qt - 3) % TT
                dst = OF[:, bass.ds(base + (h - (qt < 3)), 1), q * P:q * P + P].rearrange("p a n -> p (a n)")
                nc.scalar.activation(dst, PB[1][:, PV0:PV0 + P], ACT.Copy).then_inc(s_osq, 1)

        over_heads(act, slot)

    def dve_split_hi(head, b, parts):
        q = QF[:, head, :].rearrange("p a n -> p (a n)")
        k = KF[:, head, :].rearrange("p a n -> p (a n)")
        steps = ((Qh[b][0:HD, 0, :], q[0:HD, :]), (Qh[b][HD:P, 1, :], q[HD:P, :]), (Kh[b][:, :], k))
        for n in parts:
            nc.vector.tensor_scalar(*steps[n], 1.0, None, ALU.mult).then_inc(s_qkh, 1)

    def dve_attention(dve):
        dve.wait_ge(s_rope, 1 + 16)
        dve.wait_ge(s_pw, PROJ_PW)
        for i in range(2):
            for q in (Qh, Ql):
                nc.vector.memset(q[i][HD:P, 0, :].bitcast(F32), 0.0)
                ins = nc.vector.memset(q[i][0:HD, 1, :].bitcast(F32), 0.0)
        ins.then_inc(s_zero, 1)
        dve_split_hi(slice(0, 1), 0, range(3))

        def slot(base, h, qt):
            s = base * TT + (TT * h + qt)
            par = qt % 2
            live = due(base, h, qt, 0)
            if live:
                dve.wait_ge(s_sc, s + 1)
                need(dve, s_bias, s)
                nc.vector.tensor_reduce(row_max[:, :], SCP[par].rearrange("p (j n) -> p j n", j=2), AX.X, ALU.max
                                        ).then_inc(s_rat, 1)
                dve.wait_ge(s_rat, s * 3 - 1 if begun(base, h, qt, 1) else 1)
                nc.vector.tensor_scalar(row_bias[:, par, :], row_max[:, :], -HD ** -0.5, None, ALU.mult).then_inc(
                    s_bias, 1)
            if due(base, h, qt, 1):
                par = 1 - par
                e = E[(qt - 1) % 4]
                dve.wait_ge(s_exp, s)
                if due(base, h, qt, 2):
                    dve.wait_ge(s_comb, s - 1)
                dst = sum_all[:, bass.ds(s - 1, 1)]
                nc.vector.tensor_scalar(dst, row_sum[:, par, 0:1], 1.0, None, ALU.mult)
                nc.vector.reciprocal(row_ratio[:, par, 0:1], row_sum[:, par, 1:2]).then_inc(s_rat, 1)
                dve.wait_ge(s_rat, s * 3 - (0 if live else 1))
                nc.vector.scalar_tensor_tensor(row_ratio[:, par, 1:2], row_ratio[:, par, 0:1], neg_lam[:, :],
                                               row_sum[:, par, 0:1], ALU.mult, ALU.mult).then_inc(s_rat, 1)
                dve.wait_ge(s_rat, s * 3 + (1 if live else 0))
                nc.vector.scalar_tensor_tensor(e[:, 0, :], e[:, 1, :], row_ratio[:, par, 1:2], e[:, 0, :], ALU.mult,
                                               ALU.add).then_inc(s_comb, 1)
            if qt < 3 and due(base, h, qt, -TT):
                need(dve, s_qkl, base * 3 + 3 * h)
                dve_split_hi(bass.ds(base + (h + 1), 1), 1 - h, (qt,))

        over_heads(dve, slot)

    def pool_attention(pool):
        pool.wait_ge(s_pw, PROJ_PW)
        pool.wait_ge(s_zero, 1)
        pool.wait_ge(s_rope, 1 + 16)
        pool.wait_ge(s_evv, 3 + 12)
        pool.wait_ge(s_ada, PROJ_ADA)
        pool.wait_ge(s_sin, 16)

        def lo(head, count, b):
            q = QF[:, head, :].rearrange("p a n -> p (a n)")
            k = KF[:, head, :].rearrange("p a n -> p (a n)")
            for n, (dst, src, hi) in enumerate(((Ql[b][0:HD, 0, :], q[0:HD, :], Qh[b][0:HD, 0, :]),
                                                (Ql[b][HD:P, 1, :], q[HD:P, :], Qh[b][HD:P, 1, :]),
                                                (Kl[b][:, :], k, Kh[b][:, :]))):
                pool.wait_ge(s_qkh, count + (n + 1))
                if n > 0:
                    pool.wait_ge(s_qkl, count + n)
                nc.gpsimd.tensor_tensor(dst, src, hi, ALU.subtract).then_inc(s_qkl, 1)
            pool.wait_ge(s_qkl, count + 3)

        def v_of_head(b, columns, count):
            nc.gpsimd.tensor_copy(VB[b][:, :, :], VF[:, :, columns]).then_inc(s_vb, 1)
            pool.wait_ge(s_vb, count)

        lo(slice(0, 1), 0, 0)
        v_of_head(0, slice(0, P), 1)
        lo(slice(1, 2), 3, 1)
        v_of_head(1, slice(P, 2 * P), 2)
        with pool.Fori(1, HEADS // 2) as body:
            for h in range(2):
                lo(bass.ds(body * 2 + h, 1), body * 6 + 3 * h, h)
                pool.wait_ge(s_pv, body * (2 * TT) + (TT * h - TT))
                v_of_head(h, bass.ds(body * (2 * P) + h * P, P), body * 2 + (h + 1))
    s_oland = [sem(f"w_out_landed_{i}") for i in range(8)]
    s_ohi = sem("w_out_hi_ready")
    s_olo = sem("w_out_lo_ready")
    s_opw = sem("w_out_piece_used")
    s_dga = sem("head_factors_on_diagonal")
    s_osp = sem("head_factors_spread")
    s_on = sem("head_output_normed")
    s_ohh = sem("head_output_hi_ready")
    s_ohl = sem("head_output_lo_ready")
    s_xo = sem("attention_added_to_stream")

    def split_piece(act, n, src, hi, landed, used, done):
        act.wait_ge(*landed)
        if n >= 2:
            act.wait_ge(used, n - 1)
        nc.scalar.activation(hi, src, ACT.Copy).then_inc(done, 1)

    def sp_out_projection(sp, pieces):
        for n in pieces:
            if n == 0:
                sp.wait_ge(s_ada, PROJ_ADA)
                sp.wait_ge(s_lo, RW_ + 24)
                sp.wait_ge(s_rope, 1 + 16)
            if n == 7:
                sp.wait_ge(s_trb, SLOTS)
            src = t["da_w_out"][0, n % 4 * 256:n % 4 * 256 + 256, n // 4 * 512:n // 4 * 512 + 512]
            sp.dma_start(rawo[n][:, :, :], src.rearrange("(a p) n -> p a n", p=P)).then_inc(s_oland[n], 16)

    def pe_out_projection(pe):
        def spread(h):
            pe.wait_ge(s_dga, h + 1)
            if h >= 2:
                pe.wait_ge(s_on, h - 1)
            pe_spread(pe, s_osp, DGA[h % 2], PB[2 + h % 2], TT)

        pe.wait_ge(s_exp, SLOTS)
        spread(0)
        spread(1)
        for n in range(8):
            chunk, kp = n // 4, n % 4
            pe.wait_ge(s_olo, n + 1)
            if n == 4:
                pe.wait_ge(s_on, HEADS)
            for j in range(2):
                kt = 2 * kp + j
                if chunk == 0:
                    pe.wait_ge(s_ohl, kt + 1)
                for m in range(4):
                    w = slice(m * P, m * P + P)
                    mm = three(PB[4 * (1 - chunk) + m], stoh[n % 2][:, j, w], stol[n % 2][:, j, w], OHh[:, kt, :],
                               OHl[:, kt, :], kt == 0, kt == HEADS - 1)
                if chunk == 0 and kt + 2 < HEADS:
                    if j == 1:
                        mm.then_inc(s_opw, 1)
                    spread(kt + 2)
                elif j == 1:
                    mm.then_inc(s_opw, 1)

    def act_out_projection(act):
        act.wait_ge(s_sub, SLOTS)
        act.wait_ge(s_trb, SLOTS)

        def hi(n):
            split_piece(act, n, rawo[n][:, :, :], stoh[n % 2][:, :, :], (s_oland[n], 16), s_opw, s_ohi)

        hi(0)
        hi(1)
        for h in range(HEADS):
            act.wait_ge(s_on, h + 1)
            nc.scalar.activation(OHh[:, h, :], OF[:, h, :], ACT.Copy).then_inc(s_ohh, 1)
            if h in (3, 5):
                hi(2 + (h - 3) // 2)
        for n in range(4, 8):
            hi(n)

    def pool_out_projection(pool):
        for n in range(8):
            pool.wait_ge(s_ohi, n + 1)
            nc.gpsimd.tensor_tensor(stol[n % 2][:, :, :], rawo[n][:, :, :], stoh[n % 2][:, :, :],
                                    ALU.subtract).then_inc(s_olo, 1)

    def dve_out_projection(dve, ch):
        n = SLOTS
        dve.wait_ge(s_comb, SLOTS)
        ch.link(nc.vector.reciprocal(sum_all[:, :], sum_all[:, :]))
        dve.wait_ge(s_sub, SLOTS)
        ch.link(nc.vector.tensor_tensor(nv[:, :], PB[1][:, SUMS0:SUMS0 + n], sum_all[:, :], ALU.mult))
        ch.link(nc.vector.tensor_tensor(nv[:, :], nv[:, :], sum_all[:, :], ALU.mult))
        rsqrt(ch, nv[:, :], n, 1.0 / P)
        ch.link(nc.vector.tensor_tensor(ny[:, :], ny[:, :], sum_all[:, :], ALU.mult))

        def diag(h):
            if h >= 2:
                dve.wait_ge(s_osp, h - 1)
            for i in range(TT):
                ins = nc.vector.tensor_scalar(DGA[h % 2][:, i, :], ident[:, :], ny[:, TT * h + i:TT * h + i + 1], None,
                                              ALU.mult)
            ins.then_inc(s_dga, 1)

        diag(0)
        diag(1)
        dve.wait_ge(s_osq, SLOTS)
        for h in range(HEADS):
            dve.wait_ge(s_osp, h + 1)
            nc.vector.scalar_tensor_tensor(OF[:, h, :], OF[:, h, :], subg[:, :], PB[2 + h % 2], ALU.mult,
                                           ALU.mult).then_inc(s_on, 1)
            if h + 2 < HEADS:
                diag(h + 2)
            dve.wait_ge(s_ohh, h + 1)
            nc.vector.tensor_tensor(OHl[:, h, :], OF[:, h, :], OHh[:, h, :], ALU.subtract).then_inc(s_ohl, 1)
        dve_add_to_stream(dve, s_opw, 0, 16, (4, 0), s_xo)

    def dve_add_to_stream(dve, used, layer, gate, banks, done):
        for d in range(DT):
            if d % 4 == 0:
                dve.wait_ge(used, 4 * (d // 4 + 1))
            g = MOD[:, layer, gate + d:gate + d + 1]
            nc.vector.scalar_tensor_tensor(XT[:, d, :], PB[banks[d // 4] + d % 4], g, XT[:, d, :], ALU.mult,
                                           ALU.add).then_inc(done, 1)
    PAIRS = NE // 2
    PIECES = 12

    class Signals:

        KINDS = dict(
            router=("router_logits_ready", 1), soft=("router_softmax_chain", 3), aff=("affinities_ready", 1),
            afft=("affinities_turned", 1), wk=("affinities_by_expert", 1), mask=("chosen_ready", 1),
            maskt=("chosen_turned", 1), mb=("chosen_in_bf16", 1), rank=("ranks_summed", 1),
            hb=("token_blocks_turned", 2 * TT), hh=("token_blocks_hi_ready", 2 * TT),
            hl=("token_blocks_lo_ready", 2 * TT), zero=("sums_zeroed", 1), oh=("one_hots_ready", PAIRS),
            smt=("one_hots_turned", PAIRS), sm=("one_hots_by_slot_ready", PAIRS), afm=("slot_affinities_summed", PAIRS),
            afc=("slot_affinities_ready", PAIRS), gath=("tokens_gathered", PAIRS),
            xsa=("gathered_first_half_copied", PAIRS), xsb=("gathered_second_half_copied", PAIRS),
            used=("expert_piece_used", PAIRS * PIECES), sg=("silu_ready", NE), hid=("hidden_ready", NE),
            hidm=("hidden_turned", NE), hidt=("hidden_by_feature_ready", NE), ys=("outputs_scaled", 2 * NE),
            yh=("outputs_hi_ready", PAIRS), yl=("outputs_lo_ready", PAIRS), sc=("outputs_scattered", PAIRS * DT),
            acc=("outputs_added", PAIRS * DT), add=("experts_added_to_stream", DT))
        sems = {k: sem(name) for k, (name, _) in KINDS.items()}
        landed = [sem(f"ring_landed_{i}") for i in range(WR)]

        def __init__(self, layer):
            self.layer = layer

        def __getitem__(self, name):
            return self.landed if name == "land" else self.sems[name]

        def __call__(self, name, n, slot=None):
            if name == "land":
                return self.landed[slot], n + self.layer * (PAIRS * PIECES // WR * 16)
            return self.sems[name], n + self.layer * self.KINDS[name][1]

    ME = [Signals(0), Signals(1)]
    RING = [[ring[(i + 2) % WR] for i in range(WR)], ring]

    def over_pairs(eng, pair):
        pair(0, True, False)
        with eng.Fori(1, PAIRS - 1) as i:
            pair(i, False, False)
        pair(PAIRS - 1, False, True)

    def sp_moe(sp, L, before):
        S = ME[L]

        def load(i, r):
            name = ("moe_w_gate", "moe_w_up", "moe_w_down")[r % 6 // 2]
            src = t[name][L, bass.ds(i * 2 + r // 6, 1), r % 2 * 512:r % 2 * 512 + 512, :]
            sp.dma_start(RING[L][r % WR][:, :, :], src.rearrange("e (a p) n -> p (e a) n", p=P)).then_inc(
                S["land"][r % WR], 16)

        for r in range(WR):
            before(r)
            load(0, r)
        for r in range(WR, PIECES):
            sp.wait_ge(*S("used", r - WR + 1))
            load(0, r)
        with sp.Fori(1, PAIRS) as i:
            for r in range(PIECES):
                sp.wait_ge(*S("used", i * PIECES + (r - WR + 1)))
                load(i, r)

    def pe_moe_head(pe, L, N):
        S = ME[L]
        pe_sums(pe, N, SQ, PB[4 - 4 * L], SEQ)
        pe.wait_ge(*N("diag", 1))
        pe_spread(pe, N["spread"], DG, PB[5 - 4 * L], TT)
        for i in range(TT):
            for d in range(DT):
                if i == 0:
                    pe.wait_ge(*N("hi", d + 1))
                mm = nc.tensor.matmul(PB[2][:, i * NE:i * NE + NE], HT[:, d, i * P:i * P + P], rw[:, L, d, :],
                                      start=(i == 0 and d == 0), stop=(d == DT - 1), skip_group_check=True)
        mm.then_inc(S["router"], 1)

        def tokens(n):
            if n >= 4:
                pe.wait_ge(*S("hl", n - 3))
            i, half = n // 2, n % 2
            for j in range(4):
                mm = nc.tensor.transpose(PB[4 + n % 4][:, j * P:j * P + P], HT[:, half * 4 + j, i * P:i * P + P],
                                         ident[:, :])
            mm.then_inc(S["hb"], 1)

        for n in range(2 * TT):
            tokens(n)
        pe.wait_ge(*S("aff", 1))
        for i in range(TT):
            mm = nc.tensor.transpose(PB[3][0:NE, i * P:i * P + P], AFF[:, i, :], ident[:, :])
        mm.then_inc(S["afft"], 1)
        pe.wait_ge(*S("mask", 1))
        for i in range(TT):
            mm = nc.tensor.transpose(PB[0][:, i * NE:i * NE + NE], MKT[:, i * P:i * P + P], ident[0:NE, 0:NE])
        mm.then_inc(S["maskt"], 1)
        pe.wait_ge(*S("mb", 1))
        for i in range(TT):
            for j in range(i + 1):
                mm = nc.tensor.matmul(PB[1][:, i * NE:i * NE + NE], tri[:, :] if j == i else ones_b[:, :], MB[:, j, :],
                                      start=(i == 0), stop=(j == i), skip_group_check=True)
        mm.then_inc(S["rank"], 1)
        pe.wait_ge(*S("oh", 1))
        pe_gather(S)

    def pe_gather(S):
        for d in range(DT):
            for p, part in enumerate((HHt, HLt)):
                for j in range(TT):
                    mm = nc.tensor.matmul(PB[4 + d // 4][:, d % 4 * P:d % 4 * P + P], part[:, j, d * P:d * P + P],
                                          OH[:, j, :], start=(d % 4 == 0 and p == 0 and j == 0),
                                          stop=(p == 1 and j == TT - 1), skip_group_check=True)
        mm.then_inc(S["gath"], 1)

    def pe_scatter(pe, S, i):
        pe.wait_ge(*S("yl", i))
        for d in range(DT):
            if d == 0:
                pe.wait_ge(*S("afc", i))
            if d >= 2:
                pe.wait_ge(*S("acc", i * DT + (d - DT - 1)))
            w = slice(d * P, d * P + P)
            nc.tensor.matmul(PB[6 + d % 2], YH[:, w], SM[:, :], start=True, stop=False)
            nc.tensor.matmul(PB[6 + d % 2], YL[:, w], SM[:, :], start=False, stop=True).then_inc(S["sc"], 1)

    def pe_moe(pe, L):
        S = ME[L]

        def pair(i, first, last):
            for a in range(2):
                for m in range(3):
                    if m == 2:
                        if a == 0:
                            if not first:
                                pe_scatter(pe, S, i)
                            for j in range(TT):
                                mm = nc.tensor.transpose(PB[3][:, j * P:j * P + P], OH[:, j, :].bitcast(F32),
                                                         ident[:, :])
                            mm.then_inc(S["smt"], 1)
                            if not first:
                                pe.wait_ge(*S("acc", i * DT))
                            for e in range(2):
                                for j in range(TT):
                                    for half in range(2):
                                        mm = nc.tensor.matmul(PB[6][half * 64:half * 64 + 64, e * NE:e * NE + NE],
                                                              OH[:, j, e * 64:e * 64 + 64].bitcast(F32),
                                                              AFF[:, j, :],
                                                              start=(e == 0 and j == 0), stop=(j == TT - 1),
                                                              skip_group_check=True)
                            mm.then_inc(S["afm"], 1)
                            pe.wait_ge(*S("sm", i + 1))
                        elif not last:
                            pe.wait_ge(*S("oh", i + 2))
                            pe.wait_ge(*S("xsa", i + 1))
                            pe.wait_ge(*S("xsb", i + 1))
                            pe_gather(S)
                        pe.wait_ge(*S("hid", i * 2 + (a + 1)))
                        for j in range(4):
                            mm = nc.tensor.transpose(PB[3][:, j * P:j * P + P], HID[:, j * P:j * P + P], ident[:, :])
                        mm.then_inc(S["hidm"], 1)
                        pe.wait_ge(*S("hidt", i * 2 + (a + 1)))
                        if a == 1 or not first:
                            pe.wait_ge(*S("ys", i * 4 + (2 * a)))
                    elif m == 0 and a == 0:
                        pe.wait_ge(*S("xsa", i + 1))
                        pe.wait_ge(*S("xsb", i + 1))
                    elif m == 0:
                        pe.wait_ge(*S("hid", i * 2 + 1))
                    for half in range(2):
                        r = a * 6 + m * 2 + half
                        pe.wait_ge(*S("land", i * 32 + (r // WR + 1) * 16, r % WR))
                        for j in range(4):
                            for n in range(2):
                                k = half * 4 + j
                                if m < 2:
                                    x = XS[:, k, a * 64:a * 64 + 64]
                                else:
                                    x = HIDT[:, j, half * 64:half * 64 + 64]
                                mm = nc.tensor.matmul(PB[m][n * 64:n * 64 + 64, :], x,
                                                      RING[L][r % WR][:, j, n * 512:n * 512 + 512], start=(k == 0),
                                                      stop=(k == DT - 1))
                        mm.then_inc(S["used"], 1)

        over_pairs(pe, pair)
        pe_scatter(pe, S, PAIRS)

    def act_moe_head(act, L, N, added):
        S = ME[L]
        act_squares(act, N, XT, SQ, SEQ, (added, lambda d: max(d, 4) + 1))
        for d in range(DT):
            act.wait_ge(*N("scaled", d + 1))
            nc.scalar.activation(HT[:, d, :], HT[:, d, :], ACT.Identity, bias=MOD[:, L, 24 + d:25 + d]).then_inc(
                N["hi"], 1)
        act.wait_ge(*S("soft", 2))
        nc.scalar.activation(LG[:, :, :], LG[:, :, :], ACT.Exp).then_inc(S["soft"], 1)
        for n in range(2 * TT):
            if n == 4:
                act.wait_ge(*S("afft", 1))
                nc.scalar.activation(WK[:, :], PB[3][0:NE, :], ACT.Copy).then_inc(S["wk"], 1)
            act.wait_ge(*S("hb", n + 1))
            half = n % 2 * 512
            nc.scalar.activation(HHt[:, n // 2, half:half + 512], PB[4 + n % 4], ACT.Copy).then_inc(S["hh"], 1)
        act.wait_ge(*S("gath", 1))
        nc.scalar.activation(XS[:, 0:4, :], PB[4].rearrange("p (a n) -> p a n", a=4), ACT.Copy).then_inc(S["xsa"], 1)

    def act_moe(act, L):
        S = ME[L]

        def pair(i, first, last):
            for a in range(2):
                act.wait_ge(*S("used", i * PIECES + (6 * a + 2)))
                if not first or a == 1:
                    act.wait_ge(*S("hid", i * 2 + a))
                nc.scalar.activation(SG[:, :], PB[0], ACT.Silu).then_inc(S["sg"], 1)
                if a == 0:
                    act.wait_ge(*S("smt", i + 1))
                    nc.scalar.activation(SM[:, :], PB[3], ACT.Copy).then_inc(S["sm"], 1)
                    act.wait_ge(*S("afm", i + 1))
                    if not first:
                        act.wait_ge(*S("ys", i * 4))
                    for e in range(2):
                        column = PB[6][:, bass.ds(i * 2 + (e * NE + e), 1)]
                        ins = nc.scalar.activation(aff_c[:, e:e + 1], column, ACT.Copy)
                    ins.then_inc(S["afc"], 1)
                elif not last:
                    act.wait_ge(*S("gath", i + 2))
                    nc.scalar.activation(XS[:, 0:4, :], PB[4].rearrange("p (a n) -> p a n", a=4), ACT.Copy).then_inc(
                        S["xsa"], 1)
                act.wait_ge(*S("hidm", i * 2 + (a + 1)))
                nc.scalar.activation(HIDT[:, :, :], PB[3].rearrange("p (a n) -> p a n", a=4), ACT.Copy).then_inc(
                    S["hidt"], 1)
                act.wait_ge(*S("used", i * PIECES + (6 * a + 6)))
                if a == 0:
                    act.wait_ge(*S("afc", i + 1))
                    if not first:
                        act.wait_ge(*S("yl", i))
                for half in range(2):
                    rows = slice(half * 64, half * 64 + 64)
                    nc.scalar.activation(YS[a * 64:a * 64 + 64, half * 512:half * 512 + 512], PB[2][rows, :], ACT.Copy,
                                         scale=aff_c[rows, a:a + 1]).then_inc(S["ys"], 1)
            act.wait_ge(*S("ys", i * 4 + 4))
            if not first:
                act.wait_ge(*S("sc", i * DT))
            nc.scalar.activation(YH[:, :], YS[:, :], ACT.Copy).then_inc(S["yh"], 1)

        over_pairs(act, pair)

    def dve_one_hots(S, e):
        for j in range(TT):
            for a in range(2):
                ins = nc.vector.tensor_scalar(OH[:, j, a * CAP:a * CAP + CAP], slots[:, :], PM[:, j, e(a)], None,
                                              ALU.is_equal)
        ins.then_inc(S["oh"], 1)

    def dve_moe_head(dve, ch, L, N, added):
        S = ME[L]
        dve.wait_ge(s_mod, 6)
        dve_coef(ch, 2 + L * 2, MOD[:, L, 32:40], CT1[:, R_MOE + 8 * L:R_MOE + 8 * L + 8])
        dve.wait_ge(*N("sums", 1))
        rsqrt(ch, PB[4 - 4 * L][:, 0:TT], TT, 1.0 / D)
        diagonal(DG, TT, N["diag"])
        dve.wait_ge(*N("spread", 1))
        dve.wait_ge(added, DT)
        for d in range(DT):
            nc.vector.scalar_tensor_tensor(HT[:, d, :], XT[:, d, :], coef[:, 2 + L * 2, d:d + 1], PB[5 - 4 * L],
                                           ALU.mult, ALU.mult).then_inc(N["scaled"], 1)
        dve.wait_ge(*S("router", 1))
        lg = PB[2][:, 0:TT * NE].rearrange("p (a n) -> p a n", a=TT)
        nc.vector.tensor_reduce(st4[:, 0, :], lg, AX.X, ALU.max).then_inc(S["soft"], 1)
        dve.wait_ge(*S("soft", 1))
        for i in range(TT):
            ins = nc.vector.tensor_scalar(LG[:, i, :], lg[:, i, :], st4[:, 0, i:i + 1], None, ALU.subtract)
        ins.then_inc(S["soft"], 1)
        dve.wait_ge(*S("soft", 3))
        ch.link(nc.vector.tensor_reduce(st4[:, 1, :], LG[:, :, :], AX.X, ALU.add))
        ch.link(nc.vector.reciprocal(st4[:, 0, :], st4[:, 1, :]))
        for i in range(TT):
            ins = nc.vector.tensor_scalar(AFF[:, i, :], LG[:, i, :], st4[:, 0, i:i + 1], None, ALU.mult)
        ins.then_inc(S["aff"], 1)

        def lo(n):
            dve.wait_ge(*S("hh", n + 1))
            half = n % 2 * 512
            nc.vector.tensor_tensor(HLt[:, n // 2, half:half + 512], PB[4 + n % 4],
                                    HHt[:, n // 2, half:half + 512], ALU.subtract).then_inc(S["hl"], 1)

        for n in range(4):
            lo(n)
        dve.wait_ge(*S("wk", 1))
        for n in range(CAP // 8):
            ch.link(nc.vector.max(M8[:, :], WK[:, :]))
            ch.link(nc.vector.match_replace(WK[:, :], M8[:, :], WK[:, :], -1.0))
            if n < 4:
                lo(4 + n)
        nc.vector.tensor_scalar(MKT[:, :], WK[:, :], 0.0, None, ALU.is_lt).then_inc(S["mask"], 1)
        dve.wait_ge(*S("hb", 2 * TT))
        nc.vector.memset(ACC[:, :, :], 0.0).then_inc(S["zero"], 1)
        dve.wait_ge(*S("maskt", 1))
        nc.vector.tensor_copy(MB[:, :, :], PB[0][:, 0:TT * NE].rearrange("p (a n) -> p a n", a=TT)).then_inc(S["mb"], 1)
        dve.wait_ge(*S("mb", 1))
        dve.wait_ge(*S("rank", 1))
        ch.link(nc.vector.tensor_tensor(PM[:, :, :], PB[1][:, 0:TT * NE].rearrange("p (a n) -> p a n", a=TT),
                                        MB[:, :, :], ALU.mult))
        dve_one_hots(S, lambda a: slice(a, a + 1))
        dve.wait_ge(*S("gath", 1))
        nc.vector.tensor_copy(XS[:, 4:8, :], PB[5].rearrange("p (a n) -> p a n", a=4)).then_inc(S["xsb"], 1)

    def dve_moe(dve, L):
        S = ME[L]
        dve.wait_ge(*S("zero", 1))

        def add(i):
            for d in range(DT):
                if d == 0 and not (isinstance(i, int) and i == 1):
                    dve.wait_ge(*S("yl", i))
                dve.wait_ge(*S("sc", i * DT + (d - DT + 1)))
                nc.vector.tensor_tensor(ACC[:, d, :], PB[6 + d % 2], ACC[:, d, :], ALU.add).then_inc(S["acc"], 1)

        def pair(i, first, last):
            for a in range(2):
                dve.wait_ge(*S("sg", i * 2 + (a + 1)))
                dve.wait_ge(*S("used", i * PIECES + (6 * a + 4)))
                if not first or a == 1:
                    dve.wait_ge(*S("hidm", i * 2 + a))
                nc.vector.tensor_tensor(HID[:, :], PB[1], SG[:, :], ALU.mult).then_inc(S["hid"], 1)
                if a == 0 and not first:
                    add(i)
                if a == 0 and not last:
                    dve.wait_ge(*S("afm", i + 1))
                    dve_one_hots(S, lambda a: bass.ds(i * 2 + (2 + a), 1))
            if not last:
                dve.wait_ge(*S("gath", i + 2))
                nc.vector.tensor_scalar(XS[:, 4:8, :], PB[5].rearrange("p (a n) -> p a n", a=4), 1.0, None,
                                        ALU.mult).then_inc(S["xsb"], 1)
            dve.wait_ge(*S("yh", i + 1))
            if not first:
                dve.wait_ge(*S("sc", i * DT))
            nc.vector.tensor_tensor(YL[:, :], YS[:, :], YH[:, :], ALU.subtract).then_inc(S["yl"], 1)

        over_pairs(dve, pair)
        add(PAIRS)
        dve.wait_ge(*S("acc", PAIRS * DT))
        for d in range(DT):
            nc.vector.scalar_tensor_tensor(XT[:, d, :], ACC[:, d, :], MOD[:, L, 40 + d:41 + d], XT[:, d, :], ALU.mult,
                                           ALU.add).then_inc(S["add"], 1)
    V_PIECES = U_PIECES = GW // 512 * (DT // 2)
    O_PIECES = D // 512 * (GW // P // 2)
    s_gland = [sem(f"gmlp_w_landed_{i}") for i in range(RAWG)]
    s_ghi = sem("gmlp_w_hi_ready")
    s_glo = sem("gmlp_w_lo_ready")
    s_gused = sem("gmlp_w_piece_used")
    s_gs = sem("spatial_weights_landed")
    s_gel = sem("v_activated")
    s_vsq = sem("v_squared")
    s_vh = sem("v_hi_ready")
    s_ws = sem("spatial_weights_turned")
    s_wc = sem("spatial_weights_copied")
    s_rms = sem("v_factors_ready")
    s_rh = sem("spatial_hi_ready")
    s_rl = sem("spatial_lo_ready")
    s_ut = sem("u_activated")
    s_sv = sem("gates_summed")
    s_gt = sem("gate_chain")
    s_gh = sem("gated_hi_ready")
    s_gl = sem("gated_lo_ready")
    s_xg = sem("gmlp_added_to_stream")
    V_AHEAD = 8

    def sp_gmlp(sp):
        sp.wait_ge(*ME[0]("used", PAIRS * PIECES))
        sp.dma_start(WSR[:, :, :], t["gm_w_s"][0].rearrange("g p q -> p g q")).then_inc(s_gs, 16)
        sp.dma_start(BSB.rearrange("p g n -> p (g n)"), t["gm_b_s"][0].rearrange("g n -> (g n)").partition_broadcast(P)
                     ).then_inc(s_gs, 16)
        sp.wait_ge(*ME[0]("sc", PAIRS * DT))
        sp.wait_ge(*ME[0]("yl", PAIRS))
        for n in range(V_PIECES + U_PIECES + O_PIECES):
            if n >= RAWG:
                sp.wait_ge(s_glo, n - RAWG + 1)
            if n < V_PIECES + U_PIECES:
                c = GW + n // 4 * 512 if n < V_PIECES else (n - V_PIECES) // 4 * 512
                src = t["gm_w_in"][0, n % 4 * 256:n % 4 * 256 + 256, c:c + 512]
            else:
                m = n - V_PIECES - U_PIECES
                src = t["gm_w_out"][0, m % 8 * 256:m % 8 * 256 + 256, m // 8 * 512:m // 8 * 512 + 512]
            sp.dma_start(rawg[n % RAWG][:, :, :], src.rearrange("(a p) n -> p a n", p=P)).then_inc(
                s_gland[n % RAWG], 16)

    def pool_gmlp(pool):
        for n in range(V_PIECES + U_PIECES + O_PIECES):
            pool.wait_ge(s_ghi, n + 1)
            nc.gpsimd.tensor_tensor(stgl[n % 2][:, :, :], rawg[n % RAWG][:, :, :], stgh[n % 2][:, :, :],
                                    ALU.subtract).then_inc(s_glo, 1)

    def pe_gmlp(pe):
        pe_sums(pe, ng, SQ1, PB[0], SEQ)
        pe.wait_ge(*ng("diag", 1))
        pe_spread(pe, ng["spread"], DG1, PB[1], TT)
        pe.wait_ge(s_gs, 32)
        for g in range(GROUPS):
            mm = nc.tensor.transpose(PB[2 + g // 4][:, g % 4 * P:g % 4 * P + P], WSR[:, g, :], ident[:, :])
        mm.then_inc(s_ws, 1)
        pe.wait_ge(s_wc, 2)
        pe.wait_ge(*ng("hi", DT))
        pe.wait_ge(*ng("lo", DT))
        with pe.Fori(0, 2) as body:
            for c in range(2):
                for n in range(4):
                    pe.wait_ge(s_glo, body * 8 + (c * 4 + n + 1))
                    for j in range(2):
                        kt = 2 * n + j
                        for i in range(TT):
                            if kt == 0:
                                pe.wait_ge(s_vl, body * 8 + (c * 4 + i + 1))
                            tok = slice(i * P, i * P + P)
                            mm = three(PB[4 * c + i], H1h[:, kt, tok], H1l[:, kt, tok], stgh[n % 2][:, j, :],
                                       stgl[n % 2][:, j, :], kt == 0, kt == DT - 1)
                    mm.then_inc(s_gused, 1)
        for c in range(4):
            for n in range(4):
                pe.wait_ge(s_glo, V_PIECES + c * 4 + n + 1)
                for j in range(2):
                    kt = 2 * n + j
                    for m in range(4):
                        if kt == 0:
                            if c == 0:
                                pe.wait_ge(s_vl, V_AHEAD + 8 + m + 1)
                            else:
                                pe.wait_ge(s_ut, (c - 1) * 4 + m + 1)
                        w = slice(m * P, m * P + P)
                        mm = three(PB[m], stgh[n % 2][:, j, w], stgl[n % 2][:, j, w], H1h[:, kt, :], H1l[:, kt, :],
                                   kt == 0, kt == DT - 1)
                mm.then_inc(s_gused, 1)
            for m in range(4):
                f = 4 * c + m
                if c == 0:
                    pe.wait_ge(s_vl, V_AHEAD + 16)
                    pe.wait_ge(s_rl, TT)
                else:
                    pe.wait_ge(s_gt, 2 * (f - 4) + 1)
                g = slice(f // 2 * P, f // 2 * P + P)
                for i in range(TT):
                    mm = three(PB[4 + m][:, i * P:i * P + P], VH[:, f, i, :], VL[:, f, i, :], RWh[:, i, g],
                               RWl[:, i, g], i == 0, i == TT - 1, skip_group_check=True)
                mm.then_inc(s_sv, 1)
        for n in range(O_PIECES):
            chunk, kp = n // 8, n % 8
            pe.wait_ge(s_glo, V_PIECES + U_PIECES + n + 1)
            for j in range(2):
                kt = 2 * kp + j
                if chunk == 0:
                    pe.wait_ge(s_gl, kt + 1)
                for m in range(4):
                    if kt == 0:
                        if chunk == 0:
                            pe.wait_ge(s_ut, 12 + m + 1)
                        else:
                            pe.wait_ge(s_gt, 2 * (12 + m) + 1)
                    w = slice(m * P, m * P + P)
                    gh = VH[:, kt, :, :].rearrange("p a n -> p (a n)")
                    gl = VL[:, kt, :, :].rearrange("p a n -> p (a n)")
                    mm = three(PB[4 * chunk + m], stgh[n % 2][:, j, w], stgl[n % 2][:, j, w], gh, gl, kt == 0,
                               kt == GW // P - 1)
            mm.then_inc(s_gused, 1)

    def act_gmlp(act):
        def hi(n):
            split_piece(act, n, rawg[n % RAWG][:, :, :], stgh[n % 2][:, :, :], (s_gland[n % RAWG], (n // RAWG + 1) * 16),
                        s_gused, s_ghi)

        for n in (0, 1):
            hi(n)
        act_squares(act, ng, XT, SQ1, SEQ, (ME[0]["add"], lambda d: d + 1))
        for d in range(DT):
            act.wait_ge(*ng("scaled", d + 1))
            nc.scalar.activation(H1h[:, d, :], U1[:, d, :], ACT.Identity, bias=MOD[:, 1, d:d + 1]).then_inc(ng["hi"], 1)
        act.wait_ge(s_ws, 1)
        for i in range(2):
            src = PB[2 + i].rearrange("p (a n) -> p a n", a=4)
            nc.scalar.activation(WST[:, 4 * i:4 * i + 4, :], src, ACT.Copy).then_inc(s_wc, 1)

        def v_tile(c, i):
            n = 4 * c + i
            buf = (VT, GT)[n % 2]
            act.wait_ge(s_gused, 4 * c + 4)
            need(act, s_vl, V_AHEAD + n - 1 if n >= 2 else 0)
            need(act, s_vsq, n - 1)
            nc.scalar.activation(buf[:, :], PB[4 * (c % 2) + i], ACT.Gelu_apprx_tanh).then_inc(s_gel, 1)
            act.wait_ge(s_gel, n + 1)
            nc.scalar.activation(SQV[:, :], buf[:, :], ACT.Square, accum_out=vsq[:, i, c:c + 1]).then_inc(s_vsq, 1)

        def u_tile(c, m):
            act.wait_ge(s_gused, V_PIECES + 4 * c + 4)
            if c > 0:
                act.wait_ge(s_gt, 2 * (4 * (c - 1) + m) + 2)
            nc.scalar.activation(UT[:, m, :], PB[m], ACT.Gelu_apprx_tanh).then_inc(s_ut, 1)

        for n in range(2, V_PIECES + U_PIECES + O_PIECES):
            c = n // 4 - 1
            if 0 <= c < 4 and n % 4 in (1, 2):
                for i in range(2):
                    v_tile(c, 2 * (n % 4 - 1) + i)
            if 4 <= c < 8 and n % 4 == 1:
                for i in range(4):
                    u_tile(c - 4, i)
            if n == V_PIECES + 3:
                act.wait_ge(s_rms, 1)
                act.wait_ge(*ng("lo", DT))
                for i in range(TT):
                    nc.scalar.activation(RWh[:, i, :], WST.rearrange("p g n -> p (g n)"), ACT.Copy,
                                         scale=ny[:, i:i + 1]).then_inc(s_rh, 1)
            hi(n)

    def dve_gmlp(dve, ch):
        dve_coef(ch, 3, MOD[:, 1, 8:16], CT1[:, R_MIX + 8:R_MIX + 16])
        dve.wait_ge(*ng("sums", 1))
        rsqrt(ch, PB[0][:, 0:TT], TT, 1.0 / D)
        diagonal(DG1, TT, ng["diag"])
        dve.wait_ge(*ng("spread", 1))
        dve.wait_ge(*ME[0]("add", DT))
        for d in range(DT):
            nc.vector.scalar_tensor_tensor(U1[:, d, :], XT[:, d, :], coef[:, 3, d:d + 1], PB[1], ALU.mult,
                                           ALU.mult).then_inc(ng["scaled"], 1)
        for d in range(DT):
            dve.wait_ge(*ng("hi", d + 1))
            nc.vector.scalar_tensor_tensor(H1l[:, d, :], U1[:, d, :], MOD[:, 1, d:d + 1], H1h[:, d, :], ALU.add,
                                           ALU.subtract).then_inc(ng["lo"], 1)
        for n in range(16):
            c, i = n // TT, n % TT
            buf = (VT, GT)[n % 2].rearrange("p (a n) -> p a n", a=4)
            dve.wait_ge(s_gel, n + 1)
            nc.vector.tensor_copy(VH[:, 4 * c:4 * c + 4, i, :], buf).then_inc(s_vh, 1)
            dve.wait_ge(s_vh, n + 1)
            nc.vector.tensor_tensor(VL[:, 4 * c:4 * c + 4, i, :], buf, VH[:, 4 * c:4 * c + 4, i, :],
                                    ALU.subtract).then_inc(s_vl, 1)
        dve.wait_ge(s_vsq, 16)
        ch.link(nc.vector.tensor_reduce(nv[:, 0:TT], vsq[:, :, :], AX.X, ALU.add))
        rsqrt(ch, nv[:, 0:TT], TT, 1.0 / GW)
        nc.vector.tensor_scalar(st4[:, 0, :], ny[:, 0:TT], 1.0, None, ALU.mult).then_inc(s_rms, 1)
        for i in range(TT):
            dve.wait_ge(s_rh, i + 1)
            nc.vector.scalar_tensor_tensor(RWl[:, i, :], WST.rearrange("p g n -> p (g n)"), ny[:, i:i + 1],
                                           RWh[:, i, :], ALU.mult, ALU.subtract).then_inc(s_rl, 1)
        for f in range(GW // P):
            buf = (VT, GT)[f % 2]
            dve.wait_ge(s_sv, f + 1)
            if f >= 2:
                dve.wait_ge(s_gl, f - 1)
            for i in range(TT):
                tok = slice(i * P, i * P + P)
                ins = nc.vector.scalar_tensor_tensor(buf[:, tok], PB[4 + f % 4][:, tok], CT1[:, R_VG + f:R_VG + f + 1],
                                                     BSB[:, f // 2, :], ALU.mult, ALU.add)
            ins.then_inc(s_gt, 1)
            dve.wait_ge(s_gt, 2 * f + 1)
            dve.wait_ge(s_ut, f + 1)
            nc.vector.tensor_tensor(buf[:, :], buf[:, :], UT[:, f % 4, :], ALU.mult).then_inc(s_gt, 1)
            dve.wait_ge(s_gt, 2 * f + 2)
            hi, lo = (v[:, f, :, :].rearrange("p a n -> p (a n)") for v in (VH, VL))
            nc.vector.tensor_copy(hi, buf[:, :]).then_inc(s_gh, 1)
            dve.wait_ge(s_gh, f + 1)
            nc.vector.tensor_tensor(lo, buf[:, :], hi, ALU.subtract).then_inc(s_gl, 1)
        for d in range(DT):
            if d % 4 == 0:
                dve.wait_ge(s_gused, V_PIECES + U_PIECES + 8 * (d // 4 + 1))
            nc.vector.scalar_tensor_tensor(XT[:, d, :], PB[d], MOD[:, 1, 16 + d:17 + d], XT[:, d, :], ALU.mult,
                                           ALU.add).then_inc(s_xg, 1)

    s_fsq = sem("final_squares_ready")
    s_fsum = sem("final_squares_summed")
    s_fg = sem("stream_times_gain_ready")
    s_fny = sem("final_factors_ready")
    s_ft = sem("final_blocks_turned")
    s_fo = sem("final_second_halves_ready")
    s_fo2 = sem("final_first_halves_ready")
    s_out = sem("output_written")

    def act_final(act):
        for d in range(DT):
            act.wait_ge(*ME[1]("add", d + 1))
            nc.scalar.activation(FSQ[:, d, :], XT[:, d, :], ACT.Square).then_inc(s_fsq, 1)
        act.wait_ge(s_fny, 1)
        for n in range(1, 2 * TT, 2):
            act.wait_ge(s_ft, n + 1)
            nc.scalar.activation(FO[:, n // 2, 512:1024], PB[n], ACT.Copy, scale=ny[:, n // 2:n // 2 + 1]).then_inc(
                s_fo, 1)

    def dve_final(dve, ch):
        for d in range(DT):
            dve.wait_ge(*ME[1]("add", d + 1))
            nc.vector.tensor_scalar(FG[:, d, :], XT[:, d, :], CT1[:, R_FIN + d:R_FIN + d + 1], None, ALU.mult).then_inc(
                s_fg, 1)
        dve.wait_ge(s_fsum, 1)
        rsqrt(ch, PB[1][:, 0:TT], TT, 1.0 / D)
        nc.vector.tensor_copy(st4[:, 0, :], ny[:, 0:TT]).then_inc(s_fny, 1)
        for n in range(0, 2 * TT, 2):
            dve.wait_ge(s_ft, n + 1)
            nc.vector.tensor_scalar(FO[:, n // 2, 0:512], PB[n], ny[:, n // 2:n // 2 + 1], None, ALU.mult).then_inc(
                s_fo2, 1)

    def pe_final(pe):
        for d in range(DT):
            pe.wait_ge(s_fsq, d + 1)
            for i in range(TT):
                mm = nc.tensor.matmul(PB[1][:, i:i + 1], FSQ[:, d, i * P:i * P + P], ones[:, 0:1],
                                      start=(d == 0 and i == 0), stop=(d == DT - 1), skip_group_check=True)
        mm.then_inc(s_fsum, 1)
        pe.wait_ge(s_fg, DT)
        for n in range(2 * TT):
            if n == 1:
                pe.wait_ge(s_fny, 1)
            for j in range(4):
                mm = nc.tensor.transpose(PB[n][:, j * P:j * P + P], FG[:, n % 2 * 4 + j, n // 2 * P:n // 2 * P + P],
                                         ident[:, :])
            mm.then_inc(s_ft, 1)

    def sp_final(sp):
        for i in range(TT):
            sp.wait_ge(s_fo, i + 1)
            sp.wait_ge(s_fo2, i + 1)
            sp.dma_start(out[0, i * P:i * P + P, :], FO[:, i, :]).then_inc(s_out, 16)
        sp.wait_ge(s_out, TT * 16)

    def before_experts_0(sp):
        def before(r):
            if r == 0:
                sp.wait_ge(s_qkl, 3 * HEADS)
                sp.wait_ge(s_vb, HEADS)
            elif r == 4:
                sp_out_projection(sp, (7,))
                sp.wait_ge(s_ohl, HEADS)
            elif r == 5:
                sp.wait_ge(s_osp, HEADS)
                sp.wait_ge(s_olo, 2)
        return before

    def before_experts_1(sp):
        def before(r):
            if r == 0:
                sp.wait_ge(s_gused, V_PIECES + U_PIECES)
            elif r == 2:
                sp.wait_ge(s_sv, GW // P)
            elif r == 4:
                sp.wait_ge(s_gl, GW // P)
            elif r == 5:
                sp.wait_ge(s_gused, V_PIECES + U_PIECES + O_PIECES)
        return before

    block = ctx.enter_context(nc.Block())

    @block.sync
    def _(sp):
        sp_projections(sp)
        sp_out_projection(sp, range(7))
        sp_moe(sp, 0, before_experts_0(sp))
        sp_gmlp(sp)
        sp_moe(sp, 1, before_experts_1(sp))
        sp_final(sp)

    @block.tensor
    def _(pe):
        pe_head(pe)
        pe_projections(pe)
        pe_attention(pe)
        pe_out_projection(pe)
        pe_moe_head(pe, 0, nm0)
        pe_moe(pe, 0)
        pe_gmlp(pe)
        pe_moe_head(pe, 1, nm1)
        pe_moe(pe, 1)
        pe_final(pe)

    @block.scalar
    def _(act):
        act_head(act)
        act_projections(act)
        act_attention(act)
        act_out_projection(act)
        act_moe_head(act, 0, nm0, s_xo)
        act_moe(act, 0)
        act_gmlp(act)
        act_moe_head(act, 1, nm1, s_xg)
        act_moe(act, 1)
        act_final(act)

    @block.vector
    def _(dve):
        ch = Chain(dve, s_dve)
        dve_head(dve, ch)
        dve_projections(dve)
        dve_attention(dve)
        dve_out_projection(dve, ch)
        dve_moe_head(dve, ch, 0, nm0, s_xo)
        dve_moe(dve, 0)
        dve_gmlp(dve, ch)
        dve_moe_head(dve, ch, 1, nm1, s_xg)
        dve_moe(dve, 1)
        dve_final(dve, ch)

    @block.gpsimd
    def _(pool):
        pool_head(pool)
        pool_projections(pool)
        pool_attention(pool)
        pool_out_projection(pool)
        pool_gmlp(pool)


def bass_hybrid_trunk(nc, t, out):
    with ExitStack() as ctx:
        build(nc, ctx, t, out)


_INS = ['x', 'c', 'ctx', 'c_ctx', 'ada_w', 'ada_b', 'mixer_norm_g', 'moe_norm_g', 'router_w', 'moe_w_gate', 'moe_w_up',
        'moe_w_down', 'da_w_in', 'da_lambda_q1', 'da_lambda_k1', 'da_lambda_q2', 'da_lambda_k2', 'da_subln_g',
        'da_w_out', 'gm_w_in', 'gm_v_g', 'gm_w_s', 'gm_b_s', 'gm_w_out', 'final_norm_g']


def kernel(**inputs):
    import numpy as _np
    import concourse.bacc as _bacc
    from concourse import mybir as _mybir
    from concourse.bass_utils import run_bass_kernel_spmd as _run

    nc = _bacc.Bacc("TRN2", target_bir_lowering=False, num_devices=1)
    arrays = {f"in_{name}_dram": _np.ascontiguousarray(inputs[name]) for name in _INS}
    arrays["in_shape_constants_dram"] = shape_constants()
    tensors = {}
    for name, a in arrays.items():
        dtype = _mybir.dt.from_np(a.dtype)
        tensors[name[3:-5]] = nc.dram_tensor(name, a.shape, dtype, kind="ExternalInput").ap()
    out = nc.dram_tensor("out_0_dram", (1, SEQ, D), _mybir.dt.from_np(_np.dtype("float32")), kind="ExternalOutput").ap()
    bass_hybrid_trunk(nc, tensors, out)
    return _run(nc, [arrays], core_ids=[0]).results[0]["out_0_dram"]
```

```python
from contextlib import ExitStack

import numpy as np

import concourse.bass as bass
from concourse import mybir

F32 = mybir.dt.float32
F32R = mybir.dt.float32r
BF16 = mybir.dt.bfloat16
I32 = mybir.dt.int32
ALU = mybir.AluOpType
ACT = mybir.ActivationFunctionType
AX = mybir.AxisListType

P = 128
D = 1024
DT = D // P
SEQ = 512
TT = SEQ // P
CTX = 256
CT = CTX // P
KEYS = CTX + SEQ
KT = KEYS // P
GRID_W = 64
EPS = 1e-6
HEADS = 8
HD = 64
LAM_INIT = 0.2
SUB_SCALE = 1.0 - LAM_INIT
GW = 2048
GROUPS = 8
NE = 16
CAP = 64
KB = 1024

R_C, R_CC, R_MIX, R_MOE, R_FIN, R_SUB, R_VG, R_N = 0, 8, 16, 32, 48, 56, 57, 73


def rope_tables():
    n = HD // 4
    inv = (np.float32(10000.0) ** (-np.arange(n, dtype=np.float32) / np.float32(n))).astype(np.float32)
    t = np.arange(SEQ)
    rows, cols = (t // GRID_W).astype(np.float32), (t % GRID_W).astype(np.float32)
    cos, sin = np.zeros((P, SEQ), np.float32), np.zeros((P, SEQ), np.float32)
    for p in range(P):
        r = p % HD
        ang = ((rows if r < 32 else cols) * inv[r % 16]).astype(np.float32)
        cos[p] = np.cos(ang)
        sin[p] = np.sin(ang) * (-1.0 if r % 32 < 16 else 1.0)
    return cos, sin


def shape_constants():
    cos, sin = rope_tables()
    ident = np.eye(P, dtype=np.float32)
    tri = np.triu(np.ones((P, P), np.float32))
    slots = np.broadcast_to(np.arange(1, CAP + 1, dtype=np.float32), (P, CAP))
    select = np.tile(np.eye(32, dtype=np.float32), (4, 1))
    return np.ascontiguousarray(np.concatenate([cos, sin, ident, tri, slots, select], axis=1))


def build(nc, ctx, t, out):
    base = 16512

    def at(name, kb, shape, dt=F32):
        return nc.alloc_sbuf_tensor_at(name, shape, dt, offset=base + int(kb * KB))

    cursor = [16 * KB]

    def small(name, shape, dt=F32):
        a = nc.alloc_sbuf_tensor_at(name, shape, dt, offset=base + cursor[0])
        size = int(np.prod(shape[1:])) * (2 if dt == BF16 else 4)
        cursor[0] += (size + 31) // 32 * 32
        assert cursor[0] <= 26 * KB
        return a

    def sem(name):
        return ctx.enter_context(nc.semaphore(name))

    XT = at("XT", 0, [P, DT, SEQ])
    ident = small("ident", [P, P])
    ident_r = small("ident_r", [P, P], F32R)
    ones = small("ones", [P, P])
    slots = small("slots", [P, CAP])
    select = small("select", [P, 32])
    tri = small("tri", [P, P], BF16)
    ones_b = small("ones_b", [P, P], BF16)
    CT1 = small("CT1", [P, R_N])
    CT2 = small("CT2", [P, 96])
    silu_c = small("silu_c", [P, DT, 32])
    MOD = small("MOD", [P, 2, 48])
    MODC = small("MODC", [P, 16])
    coef = small("coef", [P, 5, DT])
    rw = small("rw", [P, 2, DT, NE])
    lam4 = at("lam4", 120, [P, 4, HD])
    shift_rw = small("shift_rw", [P, DT, NE])
    const_lg = small("const_lg", [P, NE])
    lam_s = small("lam_s", [P, 4])
    neg_lam = small("neg_lam", [P, 1])
    subg = small("subg", [P, 1])
    nv = small("nv", [P, HEADS * TT])
    ny = small("ny", [P, HEADS * TT])
    na = small("na", [P, HEADS * TT])
    row_max = small("row_max", [P, 2])
    row_bias = small("row_bias", [P, 2, 2])
    row_sum = small("row_sum", [P, 2, 2])
    row_ratio = small("row_ratio", [P, 2, 2])
    sum_all = small("sum_all", [P, HEADS * TT])
    AFF = small("AFF", [P, TT, NE])
    PM = small("PM", [P, TT, NE])
    MB = small("MB", [P, TT, NE], BF16)
    LG = small("LG", [P, TT, NE])
    st4 = small("st4", [P, 2, TT])
    aff_c = small("aff_c", [P, 2])
    vsq = small("vsq", [P, TT, 4])

    XR = at("XR", 58, [P, TT, D])
    CR = at("CR", 74, [P, CT, D])
    CXT = at("CXT", 82, [P, DT, CTX])
    SQ0 = at("SQ0", 90, [P, DT, SEQ])
    SQC = at("SQC", 111, [P, DT, CTX])
    DGC = at("DGC", 119, [P, CT, P])
    ROWS1 = at("ROWS1", 106, [R_N, P])
    ROWS2 = at("ROWS2", 107, [96, P])
    TRI0 = at("TRI0", 108, [P, P])
    U0 = at("U0", 58, [P, DT, SEQ])
    UC0 = at("UC0", 74, [P, DT, CTX])
    DG0 = at("DG0", 109, [P, TT, P])
    H0h = at("H0h", 122, [P, DT, KEYS], F32R)
    H0l = at("H0l", 146, [P, DT, KEYS], F32R)
    RA, RW_ = 8, 3
    rawa = [at(f"rawa_{i}", 26 + 4 * i, [P, 1024]) for i in range(RA)]
    raww = [at(f"raww_{i}", 186 + 4 * i, [P, 4, 256]) for i in range(RW_)]
    st0h = [at(f"st0h_{i}", 170 + 8 * i, [P, 4, 256], F32R) for i in range(2)]
    st0l = [at(f"st0l_{i}", 174 + 8 * i, [P, 4, 256], F32R) for i in range(2)]
    QF = at("QF", 58, [P, HEADS, SEQ])
    KF = at("KF", 74, [P, HEADS, KEYS])
    VF = at("VF", 98, [P, KT, D])
    COS = at("COS", 198, [P, SEQ])
    SIN = at("SIN", 200, [P, SEQ])
    QT = at("QT", 202, [P, KEYS])
    RT = at("RT", 205, [P, SEQ])
    ADS = small("ADS", [P, SEQ])
    Qh = [at(f"Qh{i}", 122 + 14 * i, [P, 2, SEQ], F32R) for i in range(2)]
    Ql = [at(f"Ql{i}", 126 + 14 * i, [P, 2, SEQ], F32R) for i in range(2)]
    Kh = [at(f"Kh{i}", 130 + 14 * i, [P, KEYS], F32R) for i in range(2)]
    Kl = [at(f"Kl{i}", 133 + 14 * i, [P, KEYS], F32R) for i in range(2)]
    AT = [at(f"AT{i}", 150 + 3 * i, [P, KT, P]) for i in range(2)]
    E = [at(f"E{i}", 162 + 6 * i, [P, 2, KEYS]) for i in range(4)]
    OSQ = [at(f"OSQ{i}", 156 + 0.5 * i, [P, P]) for i in range(2)]
    VB = [at(f"VB{i}", (46, 157)[i], [P, KT, P]) for i in range(2)]
    OF = at("OF", 26, [P, HEADS, SEQ])
    DGA = [at("DGA0", 42, [P, TT, P]), at("DGA1", 44, [P, TT, P])]
    OHh = at("OHh", 122, [P, HEADS, SEQ], F32R)
    OHl = at("OHl", 138, [P, HEADS, SEQ], F32R)
    rawo = [at(f"rawo_{i}", (50, 54, 186, 190, 194, 198, 202, 186)[i], [P, 2, 512]) for i in range(8)]
    stoh = [at(f"stoh_{i}", 154 + 8 * i, [P, 2, 512], F32R) for i in range(2)]
    stol = [at(f"stol_{i}", 158 + 8 * i, [P, 2, 512], F32R) for i in range(2)]
    WR = 6
    ring = [at(f"ring_{i}", 26 + 16 * i, [P, 4, D]) for i in range(WR)]
    XTM = at("XTM", 122, [P, TT, D])
    ACC = at("ACC", 154, [P, DT, SEQ])
    SQ = at("SQ", 170, [P, DT, SEQ])
    SUMC = at("SUMC", 186, [P, SEQ])
    LOGC = at("LOGC", 188, [P, SEQ])
    rw_pad = at("rw_pad", 206, [P, DT, 32])
    WK = at("WK", 200, [NE, SEQ])
    MKT = at("MKT", 202, [NE, SEQ])
    M8 = at("M8", 204, [NE, 8])
    XS = at("XS", 170, [P, DT, P])
    OH = at("OH", 178, [P, TT, P])
    SM = at("SM", 180, [P, SEQ], F32R)
    SG = at("SG", 182, [P, SEQ])
    HID = at("HID", 184, [P, SEQ])
    HIDT = at("HIDT", 186, [P, TT, P])
    YS = at("YS", 188, [P, D])
    YH = at("YH", 192, [P, D], F32R)
    YL = at("YL", 196, [P, D], F32R)
    H1h = at("H1h", 26, [P, DT, SEQ], F32R)
    H1l = at("H1l", 42, [P, DT, SEQ], F32R)
    U1 = at("U1", 58, [P, DT, SEQ])
    SQ1 = at("SQ1", 74, [P, DT, SEQ])
    DG1 = at("DG1", 94, [P, TT, P])
    RW1 = at("RW1", 58, [P, TT, D])
    WSR = at("WSR", 90, [P, GROUPS, P])
    UT = at("UT", 90, [P, 4, SEQ])
    WST = at("WST", 98, [P, GROUPS, P])
    BSB = at("BSB", 102, [P, GROUPS, P])
    stgh = [at(f"stgh_{i}", 106 + 8 * i, [P, 2, 512], F32R) for i in range(2)]
    stgl = [at(f"stgl_{i}", 110 + 8 * i, [P, 2, 512], F32R) for i in range(2)]
    V1 = at("V1", 122, [P, 16, TT, P])
    GH = at("GH", 122, [P, 16, SEQ], F32R)
    GL = at("GL", 154, [P, 16, SEQ], F32R)
    RAWG = 4
    rawg = [at(f"rawg_{i}", 186 + 4 * i, [P, 2, 512]) for i in range(RAWG)]
    VT = at("VT", 202, [P, 512])
    GT = at("GT", 204, [P, 512])
    FG = at("FG", 26, [P, DT, SEQ])
    FO = at("FO", 42, [P, TT, D])
    FSQ = at("FSQ", 58, [P, DT, SEQ])

    bank = [ctx.enter_context(nc.psum_tensor(f"bank{i}", [P, 512], F32)) for i in range(2)]
    sc_a = ctx.enter_context(nc.psum_tensor("sc_a", [P, 1536], F32))
    sc_b = ctx.enter_context(nc.psum_tensor("sc_b", [P, 1536], F32))
    SCP = [sc_a, sc_b]
    PB = [bank[0][:, :], bank[1][:, :]] + [s[:, 512 * i:512 * i + 512] for s in SCP for i in range(3)]

    s_small = sem("small_loads_landed")
    s_xload = sem("x_landed")
    s_cload = sem("ctx_landed")
    s_unit = sem("streams_normed")
    s_const = sem("constants_ready")
    s_rowT = sem("rows_transposed")
    s_ct = sem("columns_copied")
    s_silu = sem("silu_c_ready")
    s_xtT = sem("stream_blocks_transposed")
    s_xtc = sem("stream_blocks_copied")
    s_aland = [sem(f"ada_landed_{i}") for i in range(RA)]
    s_wland = [sem(f"w_landed_{i}") for i in range(RW_)]
    s_ada = sem("ada_piece_used")
    s_ads = sem("ada_sums_copied")
    s_adt = sem("ada_sums_transposed")
    s_mod = sem("modulation_ready")
    s_coef = sem("norm_coefficients_ready")
    s_dve = sem("vector_chain")
    s_act = sem("scalar_chain")

    class Norm:

        TOTAL = dict(squares=DT, sums=1, diag=1, spread=1, scaled=DT, hi=DT, lo=DT)
        sems = {k: sem(f"norm_{k}") for k in TOTAL}

        def __init__(self, before, applied_before):
            self.before, self.applied_before = before, applied_before

        def __getitem__(self, name):
            return self.sems[name]

        def __call__(self, name, n):
            summed = name in ("squares", "sums")
            return self.sems[name], n + self.TOTAL[name] * (self.before if summed else self.applied_before)

    nx, nc_, nm0, ng, nm1 = Norm(0, 0), Norm(1, 1), Norm(2, 2), Norm(3, 2), Norm(4, 3)
    s_hi = sem("w_hi_ready")
    s_lo = sem("w_lo_ready")
    s_pw = sem("w_piece_used")
    s_evq = sem("q_sums_copied")
    s_evk = sem("k_sums_copied")
    s_evv = sem("v_sums_copied")
    s_shuf = sem("rope_halves_swapped")
    s_sin = sem("rope_sine_applied")
    s_cos = sem("rope_cosine_applied")
    s_rope = sem("rope_done")
    s_gel = sem("v_activated")
    s_lam = sem("lambda_exponentials_ready")
    s_lamr = sem("lambda_sums_ready")

    def need(eng, s, n):
        if not isinstance(n, int) or n > 0:
            eng.wait_ge(s, n)

    class Chain:

        def __init__(self, eng, s):
            self.eng, self.s, self.n = eng, s, 0

        def link(self, ins):
            ins.then_inc(self.s, 1)
            self.n = self.n + 1
            self.eng.wait_ge(self.s, self.n)

    HEAD_PIECES = 16
    STEP = []
    for n, extra in enumerate((3, 3, 3, 3, 4, 0)):
        STEP.append(("w", n // 2, n % 2))
        done = sum(kind == "a" for kind, _, _ in STEP)
        STEP += [("a", done + j, 0) for j in range(extra)]

    SMALL_LOADS = []
    for r0, name in ((R_C, "c"), (R_CC, "c_ctx"), (R_MIX, "mixer_norm_g"), (R_MOE, "moe_norm_g"), (R_FIN, "final_norm_g"),
                     (R_SUB, "da_subln_g"), (R_VG, "gm_v_g")):
        src = t[name] if len(t[name].shape) == 1 else t[name].rearrange("a n -> (a n)")
        rows = src.rearrange("(r p) -> r p", p=P)
        SMALL_LOADS.append((ROWS1[r0:r0 + rows.shape[0], :], rows))
    SMALL_LOADS.append((ROWS2[:, :], t["ada_b"].rearrange("a n -> (a n)").rearrange("(r p) -> r p", p=P)))
    SMALL_LOADS += [(ident[:, :], t["shape_constants"][:, 1024:1152]), (TRI0[:, :], t["shape_constants"][:, 1152:1280]),
                    (slots[:, :], t["shape_constants"][:, 1280:1344]), (select[:, :], t["shape_constants"][:, 1344:1376]), (COS[:, :], t["shape_constants"][:, 0:512]),
                    (SIN[:, :], t["shape_constants"][:, 512:1024])]
    SMALL_LOADS += [(rw[:, i, :, :], t["router_w"][i].rearrange("(a p) n -> p a n", p=P)) for i in range(2)]
    SMALL_LOADS += [(lam4[:, i, :], t[name].partition_broadcast(P).rearrange("p a n -> p (a n)"))
                    for i, name in enumerate(("da_lambda_q1", "da_lambda_k1", "da_lambda_q2", "da_lambda_k2"))]
    SMALL = 16 * len(SMALL_LOADS)

    def three(out_, wh, wl, xh, xl, first, last, **kw):
        nc.tensor.matmul(out_, wh, xh, start=first, stop=False, **kw)
        nc.tensor.matmul(out_, wh, xl, start=False, stop=False, **kw)
        return nc.tensor.matmul(out_, wl, xh, start=False, stop=last, **kw)

    def pe_sums(pe, N, sq, acc, tokens):
        n = tokens // P
        for d in range(DT):
            pe.wait_ge(*N("squares", d + 1))
            for i in range(n):
                mm = nc.tensor.matmul(acc[:, i:i + 1], sq[:, d, i * P:(i + 1) * P], ones[:, 0:1],
                                      start=(d == 0 and i == 0), stop=(d == DT - 1), skip_group_check=True)
        mm.then_inc(N["sums"], 1)

    def pe_spread(pe, done, dg, acc, n):
        for i in range(n):
            mm = nc.tensor.matmul(acc[:, i * P:(i + 1) * P], ones[:, :], dg[:, i, :], start=True, stop=True)
        mm.then_inc(done, 1)

    def rsqrt(ch, sums, n, scale):
        v, y, a = nv[:, 0:n], ny[:, 0:n], na[:, 0:n]
        ch.link(nc.vector.tensor_scalar(v, sums, scale, EPS, ALU.mult, ALU.add))
        ch.link(nc.vector.tensor_scalar(y.bitcast(I32), v.bitcast(I32), 1, None, ALU.logical_shift_right))
        ch.link(nc.vector.tensor_scalar(y.bitcast(I32), y.bitcast(I32), -1.0, float(0x5F3759DF), ALU.mult, ALU.add))
        for _ in range(3):
            ch.link(nc.vector.tensor_tensor(a, y, y, ALU.mult))
            ch.link(nc.vector.scalar_tensor_tensor(a, a, -0.5, v, ALU.mult, ALU.mult))
            ch.link(nc.vector.scalar_tensor_tensor(y, a, 1.5, y, ALU.add, ALU.mult))

    def diagonal(dg, n, done):
        for i in range(n):
            ins = nc.vector.tensor_scalar(dg[:, i, :], ident[:, :], ny[:, i:i + 1], None, ALU.mult)
        ins.then_inc(done, 1)

    def act_squares(act, N, src, sq, tokens, ready=None):
        for d in range(DT):
            if ready is not None:
                act.wait_ge(ready[0], ready[1](d))
            nc.scalar.activation(sq[:, d, 0:tokens], src[:, d, 0:tokens], ACT.Square).then_inc(N["squares"], 1)

    def sp_projections(sp):
        sp.dma_start(XR[:, :, :], t["x"][0].rearrange("(a p) n -> p a n", p=P)).then_inc(s_xload, 16)
        sp.dma_start(CR[:, :, :], t["ctx"][0].rearrange("(a p) n -> p a n", p=P)).then_inc(s_cload, 16)

        def first_sweep(layer, m, used):
            if m + used >= RA:
                sp.wait_ge(s_ada, m + used - RA + 1)
            c0 = m % 2 * 1024
            sp.dma_start(rawa[m % RA][:, :], t["ada_w"][layer, m // 2 * P:m // 2 * P + P, c0:c0 + 1024]).then_inc(
                s_aland[m % RA], 16)

        sp.wait_ge(s_cload, 16)
        for m in range(16):
            first_sweep(0, m, 0)
        with sp.Fori(0, 2) as body:
            for step in range(2):
                for kind, m, half in STEP:
                    if kind == "w":
                        k = step * 6 + m * 2 + half
                        sp.wait_ge(s_lo, body * 12 + (k + 1))
                        src = t["da_w_in"][0, half * 512:half * 512 + 512, :].rearrange("(a p) n -> p a n", p=P)
                        sp.dma_start(raww[k % RW_][:, :, :], src[:, :, bass.ds(body * 512 + (m * D + step * 256), 256)]
                                     ).then_inc(s_wland[k % RW_], 16)
                    else:
                        k = step * 16 + m
                        sp.wait_ge(s_ada, body * 32 + (HEAD_PIECES + k - RA + 1))
                        kt, c0 = m // 2, (step + 1) * 2048 + m % 2 * 1024
                        src = t["ada_w"][bass.ds(body, 1), kt * P:(kt + 1) * P, c0:c0 + 1024]
                        sp.dma_start(rawa[k % RA][:, :], src.rearrange("a p n -> p (a n)")).then_inc(
                            s_aland[k % RA], 16)
        for m in range(16):
            first_sweep(1, m, HEAD_PIECES + 64)

    def pe_ada(pe, k, m, landed):
        pe.wait_ge(*landed)
        for j in range(2):
            g = 2 * (m % 2) + j
            mm = nc.tensor.matmul(PB[7][32 * g:32 * g + 32, :], silu_c[:, m // 2, :], rawa[k % RA][:, 512 * j:512 * j + 512],
                                  start=(m < 2), stop=(m >= 14))
        mm.then_inc(s_ada, 1)

    def pe_ada_columns(pe, n):
        pe.wait_ge(s_ads, n + 1)
        for b in range(4):
            mm = nc.tensor.transpose(PB[7][:, b * P:(b + 1) * P], ADS[:, b * P:(b + 1) * P], ident[:, :])
        mm.then_inc(s_adt, 1)

    def pe_head(pe):
        pe.wait_ge(s_small, SMALL)
        pe.wait_ge(s_const, 4)
        nc.tensor.transpose(PB[0][:, 0:R_N], ROWS1[:, :], ident[0:R_N, 0:R_N]).then_inc(s_rowT, 1)
        nc.tensor.transpose(PB[1][:, 0:96], ROWS2[:, :], ident[0:96, 0:96]).then_inc(s_rowT, 1)
        pe.wait_ge(s_ct, 2)
        pe.wait_ge(s_xload, 16)
        for n in range(12):
            if n == 8:
                pe.wait_ge(s_cload, 16)
            if n >= 4:
                pe.wait_ge(s_xtc, n - 3)
            for j in range(4):
                c = (n - 8) * 2 + j // 2
                src = XR[:, j, n * P:(n + 1) * P] if n < 8 else CR[:, j % 2, c * P:c * P + P]
                mm = nc.tensor.transpose(PB[n % 4][:, j * P:(j + 1) * P], src, ident[:, :])
            mm.then_inc(s_xtT, 1)
        pe.wait_ge(s_silu, 2)
        for n in range(16):
            pe_ada(pe, n, n, (s_aland[n % RA], (n // RA + 1) * 16))
            if n == 3:
                pe.wait_ge(s_xtc, 12)
                pe_sums(pe, nx, SQ0, PB[1], SEQ)
            if n == 5:
                pe_sums(pe, nc_, SQC, PB[2], CTX)
            if n == 7:
                pe.wait_ge(*nx("diag", 1))
                pe_spread(pe, nx["spread"], DG0, PB[0], TT)
            if n == 9:
                pe.wait_ge(*nc_("diag", 1))
                pe_spread(pe, nc_["spread"], DGC, PB[3], CT)
        pe_ada_columns(pe, 0)

    def pe_projections(pe):
        with pe.Fori(0, 2) as body:
            for step in range(2):
                for kind, m, half in STEP:
                    if kind == "a":
                        k = step * 16 + m
                        if m == 0:
                            pe.wait_ge(s_mod, body * 2 + (step + 1))
                        pe_ada(pe, k, m, (s_aland[k % RA], body * 64 + (HEAD_PIECES // RA + k // RA + 1) * 16))
                        continue
                    k = step * 6 + m * 2 + half
                    wh, wl = st0h[k % 2], st0l[k % 2]
                    pe.wait_ge(s_lo, body * 12 + (RW_ + k + 1))
                    for j in range(4):
                        kt, first, last = half * 4 + j, half == 0 and j == 0, half == 1 and j == 3
                        if m == 0:
                            pe.wait_ge(*nx("lo", kt + 1))
                            for h in range(2):
                                if first:
                                    pe.wait_ge(s_evv, body * 6 + (step * 3 + 2 + h))
                                w = slice(h * P, h * P + P)
                                mm = three(PB[h], wh[:, j, w], wl[:, j, w], H0h[:, kt, CTX:], H0l[:, kt, CTX:],
                                           first, last)
                        elif m == 1:
                            pe.wait_ge(*nc_("lo", kt + 1))
                            for h in range(2):
                                if first:
                                    pe.wait_ge(s_evk, body * 4 + (step * 2 + 1 + h))
                                w = slice(h * P, h * P + P)
                                for i in range(2):
                                    c = slice(i * 384, i * 384 + 384)
                                    mm = three(PB[2 + 2 * h + i][:, 0:384], wh[:, j, w], wl[:, j, w], H0h[:, kt, c],
                                               H0l[:, kt, c], first, last)
                        else:
                            for i in range(KT):
                                if first and i == 0:
                                    pe.wait_ge(s_evv, body * 6 + (step * 3 + 1))
                                if first and i in (2, 4):
                                    pe.wait_ge(s_evq, body * 4 + (step * 2 + i // 2))
                                c = slice(i * P, i * P + P)
                                mm = three(PB[(6, 0, 1)[i // 2]][:, i % 2 * 256:i % 2 * 256 + 256], H0h[:, kt, c],
                                           H0l[:, kt, c], wh[:, j, :], wl[:, j, :], first and i % 2 == 0, last,
                                           skip_group_check=True)
                    mm.then_inc(s_pw, 1)
                pe_ada_columns(pe, body * 2 + (step + 1))
        pe.wait_ge(s_mod, 5)
        for m in range(16):
            pe_ada(pe, m, m, (s_aland[m % RA], ((HEAD_PIECES + 64 + m) // RA + 1) * 16))
        pe_ada_columns(pe, 5)

    def act_head(act):
        for dst, src in SMALL_LOADS:
            act.dma_start(dst, src).then_inc(s_small, 16)
        act.wait_ge(s_rowT, 1)
        nc.scalar.activation(CT1[:, :], PB[0][:, 0:R_N], ACT.Copy).then_inc(s_ct, 1)
        act.wait_ge(s_rowT, 2)
        nc.scalar.activation(CT2[:, :], PB[1][:, 0:96], ACT.Copy).then_inc(s_ct, 1)
        act.wait_ge(s_const, 4)
        act.wait_ge(s_ct, 1)
        for r in range(2):
            nc.scalar.activation(silu_c[:, :, r], CT1[:, 8 * r:8 * r + 8], ACT.Silu).then_inc(s_silu, 1)
        act.wait_ge(s_lamr, 1)
        nc.scalar.activation(lam_s[:, 2:4], lam_s[:, 0:2], ACT.Exp).then_inc(s_lam, 1)
        act_squares(act, nx, XT, SQ0, SEQ, (s_xtc, lambda d: d + 1))
        act_squares(act, nc_, CXT, SQC, CTX, (s_xtc, lambda d: 9 + d // 2))
        act.wait_ge(s_ada, 16)
        nc.scalar.activation(ADS[:, :], PB[7], ACT.Copy).then_inc(s_ads, 1)
        for N, u, c0 in ((nx, U0, CTX), (nc_, UC0, 0)):
            for d in range(DT):
                act.wait_ge(*N("scaled", d + 1))
                nc.scalar.activation(H0h[:, d, c0:c0 + u.shape[2]], u[:, d, :], ACT.Copy).then_inc(N["hi"], 1)

    def act_projections(act):
        def hi(body, k):
            act.wait_ge(s_wland[k % RW_], body * 64 + (k // RW_ + 1) * 16)
            act.wait_ge(s_pw, body * 12 + (k + 1))
            nc.scalar.activation(st0h[k % 2][:, :, :], raww[k % RW_][:, :, :], ACT.Copy).then_inc(s_hi, 1)

        def copy_sums(body, k, r, banks, width, done):
            for i, b in enumerate(banks):
                if i == 0:
                    act.wait_ge(s_pw, body * 12 + (k + 3))
                    act.wait_ge(s_shuf, body * 8 + (r + 1))
                ins = nc.scalar.activation(QT[:, i * width:i * width + width], PB[b][:, 0:width], ACT.Copy)
            ins.then_inc(done, 1)

        with act.Fori(0, 2) as body:
            for step in range(2):
                k = step * 6
                for j in range(3):
                    hi(body, k + j)
                for h in range(2):
                    copy_sums(body, k + 1, step * 4 + h, (h,), SEQ, s_evq)
                for j in range(3, 6):
                    hi(body, k + j)
                for h in range(2):
                    copy_sums(body, k + 3, step * 4 + 2 + h, (2 + 2 * h, 3 + 2 * h), 384, s_evk)
                act.wait_ge(s_ada, body * 32 + (HEAD_PIECES + 16 * (step + 1)))
                nc.scalar.activation(ADS[:, :], PB[7], ACT.Copy).then_inc(s_ads, 1)

    def dve_modulation(dve, n, dst, r, bias):
        src = PB[7].rearrange("p (b g r) -> p g b r", b=4, g=4)[:, :, :, r]
        return nc.vector.tensor_tensor(dst.rearrange("p (g b) -> p g b", g=4), src,
                                       bias.rearrange("p (g b) -> p g b", g=4), ALU.add)

    def dve_coef(ch, n, scale_cols, gain_cols):
        ch.link(nc.vector.scalar_tensor_tensor(coef[:, n, :], scale_cols, 1.0, gain_cols, ALU.add, ALU.mult))

    def dve_head(dve, ch):
        dve.wait_ge(s_small, SMALL)
        nc.vector.tensor_copy(tri[:, :], TRI0[:, :]).then_inc(s_const, 1)
        nc.vector.tensor_copy(ident_r[:, :], ident[:, :]).then_inc(s_const, 1)
        ch.link(nc.vector.tensor_tensor(lam4[:, 0:4:2, :], lam4[:, 0:4:2, :], lam4[:, 1:4:2, :], ALU.mult))
        nc.vector.tensor_reduce(lam_s[:, 0:2], lam4[:, 0:4:2, :], AX.X, ALU.add).then_inc(s_lamr, 1)
        for n in range(12):
            dve.wait_ge(s_xtT, n + 1)
            dst = XT[:, n, :] if n < 8 else CXT[:, 2 * (n - 8):2 * (n - 8) + 2, :].rearrange("p a n -> p (a n)")
            nc.vector.tensor_copy(dst, PB[n % 4]).then_inc(s_xtc, 1)
        dve.wait_ge(s_lam, 1)
        ch.link(nc.vector.scalar_tensor_tensor(neg_lam[:, :], lam_s[:, 3:4], -LAM_INIT, lam_s[:, 2:3], ALU.add,
                                               ALU.subtract))
        dve.wait_ge(s_ct, 2)
        ch.link(nc.vector.tensor_scalar(subg[:, :], CT1[:, R_SUB:R_SUB + 1], SUB_SCALE, None, ALU.mult))
        dve.wait_ge(*nx("sums", 1))
        rsqrt(ch, PB[1][:, 0:TT], TT, 1.0 / D)
        diagonal(DG0, TT, nx["diag"])
        dve.wait_ge(*nc_("sums", 1))
        dve.wait_ge(*nx("diag", 1))
        rsqrt(ch, PB[2][:, 0:CT], CT, 1.0 / D)
        diagonal(DGC, CT, nc_["diag"])
        for N, src, u, b in ((nx, XT, U0, 0), (nc_, CXT, UC0, 3)):
            dve.wait_ge(*N("spread", 1))
            for d in range(DT):
                nc.vector.tensor_tensor(u[:, d, :], src[:, d, :], PB[b][:, 0:u.shape[2]], ALU.mult).then_inc(s_unit, 1)
        dve.wait_ge(s_adt, 1)
        dve_modulation(dve, 0, MODC[:, :], 1, CT2[:, 0:16])
        ch.link(dve_modulation(dve, 0, MOD[:, 0, 0:16], 0, CT2[:, 0:16]))
        dve_coef(ch, 0, MOD[:, 0, 8:16], CT1[:, R_MIX:R_MIX + 8])
        nc.vector.scalar_tensor_tensor(coef[:, 1, :], MODC[:, 8:16], 1.0, CT1[:, R_MIX:R_MIX + 8], ALU.add,
                                       ALU.mult).then_inc(s_mod, 1)
        dve.wait_ge(s_mod, 1)
        dve.wait_ge(s_unit, 2 * DT)
        for N, u, n, c0, B in ((nx, U0, 0, CTX, MOD[:, 0, :]), (nc_, UC0, 1, 0, MODC[:, :])):
            for d in range(DT + 1):
                if d < DT:
                    nc.vector.tensor_scalar(u[:, d, :], u[:, d, :], coef[:, n, d:d + 1], B[:, d:d + 1], ALU.mult,
                                            ALU.add).then_inc(N["scaled"], 1)
                if d > 0:
                    c = slice(c0, c0 + u.shape[2])
                    dve.wait_ge(*N("hi", d))
                    nc.vector.tensor_tensor(H0l[:, d - 1, c], u[:, d - 1, :], H0h[:, d - 1, c], ALU.subtract).then_inc(
                        N["lo"], 1)

    def dve_projections(dve):
        with dve.Fori(0, 2) as body:
            for step in range(2):
                for r in range(4):
                    kind, h = r // 2, r % 2
                    idx = step * 4 + r
                    dve.wait_ge((s_evq, s_evk)[kind], body * 4 + (kind * 2 + step * 2 + h + 1))
                    dve.wait_ge(s_rope, body * 8 + (idx + 1))
                    lat = QT[:, 0:SEQ] if kind == 0 else QT[:, CTX:]
                    head = bass.ds(body * 4 + (step * 2 + h), 1)
                    if kind == 0:
                        dst = QF[:, head, :].rearrange("p a n -> p (a n)")
                    else:
                        dst = KF[:, head, CTX:].rearrange("p a n -> p (a n)")
                        nc.vector.tensor_scalar(KF[:, head, 0:CTX].rearrange("p a n -> p (a n)"), QT[:, 0:CTX], 1.0, None,
                                                ALU.mult)
                    nc.vector.tensor_tensor(dst, lat, COS[:, :], ALU.mult).then_inc(s_cos, 1)
                    nc.vector.stream_shuffle(RT[:, :], lat, [(i + 16) % 32 for i in range(32)]).then_inc(s_shuf, 1)
                    dve.wait_ge(s_cos, body * 8 + (idx + 1))
                    dve.wait_ge(s_sin, body * 8 + (idx + 1))
                    nc.vector.tensor_tensor(dst, dst, RT[:, :], ALU.add).then_inc(s_rope, 1)
                dve.wait_ge(s_pw, body * 12 + (step * 6 + 8))
                for i, b in enumerate((6, 0, 1)):
                    dst = VF[:, 2 * i:2 * i + 2, bass.ds(body * 512 + step * 256, 256)]
                    nc.vector.tensor_scalar(dst, PB[b].rearrange("p (a n) -> p a n", a=2), 1.0, None, ALU.mult).then_inc(
                        s_evv, 1)
                dve.wait_ge(s_adt, body * 2 + (step + 2))
                c = (step + 1) * 16
                dst = MOD[:, bass.ds(body, 1), c:c + 16].rearrange("p a n -> p (a n)")
                dve_modulation(dve, None, dst, 0, CT2[:, bass.ds(body * 48 + c, 16)]).then_inc(s_mod, 1)

    def pool_head(pool):
        nc.gpsimd.memset(ones[:, :], 1.0).then_inc(s_const, 1)
        nc.gpsimd.memset(silu_c[:, :, :], 0.0).then_inc(s_const, 1)
        nc.gpsimd.memset(ones_b[:, 0:32], 1.0).then_inc(s_lo, RW_)
        nc.gpsimd.memset(ones_b[:, 32:64], 1.0).then_inc(s_pw, 2)
        nc.gpsimd.memset(ones_b[:, 64:96], 1.0).then_inc(s_evv, 3)
        nc.gpsimd.memset(ones_b[:, 96:112], 1.0).then_inc(s_evk, 2)
        nc.gpsimd.memset(ones_b[:, 112:120], 1.0).then_inc(s_gel, 8)
        nc.gpsimd.memset(ones_b[:, 120:124], 1.0).then_inc(s_shuf, 1)
        nc.gpsimd.memset(ones_b[:, 124:128], 1.0).then_inc(s_rope, 1)

    def pool_projections(pool):
        def lo(body, k):
            pool.wait_ge(s_hi, body * 12 + (k + 1))
            nc.gpsimd.tensor_tensor(st0l[k % 2][:, :, :], raww[k % RW_][:, :, :], st0h[k % 2][:, :, :],
                                    ALU.subtract).then_inc(s_lo, 1)

        def sine(body, r):
            pool.wait_ge(s_shuf, body * 8 + (r + 2))
            nc.gpsimd.tensor_tensor(RT[:, :], RT[:, :], SIN[:, :], ALU.mult).then_inc(s_sin, 1)

        with pool.Fori(0, 2) as body:
            for step in range(2):
                for j in range(3):
                    lo(body, step * 6 + j)
                for h in range(2):
                    sine(body, step * 4 + h)
                for j in range(3, 6):
                    lo(body, step * 6 + j)
                for h in range(2):
                    sine(body, step * 4 + 2 + h)
    s_zero = sem("q_zeros_written")
    s_qkh = sem("qk_hi_ready")
    s_qkl = sem("qk_lo_ready")
    s_vb = sem("v_of_head_ready")
    s_sc = sem("scores_ready")
    s_bias = sem("maximum_ready")
    s_exp = sem("exponentials_ready")
    s_rat = sem("ratio_chain")
    s_comb = sem("softmaxes_combined")
    s_tra = sem("keys_0_to_3_transposed")
    s_trb = sem("keys_4_and_5_transposed")
    s_at = sem("transposes_copied")
    s_pv = sem("tile_times_v_ready")
    s_osq = sem("tile_output_copied")
    s_sub = sem("tile_squares_summed")
    PROJ_ADA = HEAD_PIECES + 64 + 16
    PROJ_PW = 2 + 24
    PV0 = 256
    SUMS0 = 384
    SLOTS = HEADS * TT

    def over_heads(eng, slot):
        for h in range(2):
            for qt in range(TT):
                slot(0, h, qt)
        with eng.Fori(1, HEADS // 2 - 1) as body:
            for h in range(2):
                for qt in range(TT):
                    slot(body * 2, h, qt)
        for h in range(2):
            for qt in range(TT):
                slot(HEADS - 2, h, qt)
        for qt in range(TT):
            slot(HEADS, 0, qt)

    def due(base, h, qt, late):
        if not isinstance(base, int):
            return True
        s = (base + h) * TT + qt - late
        return 0 <= s < SLOTS

    def begun(base, h, qt, late):
        return not isinstance(base, int) or (base + h) * TT + qt >= late

    def pe_attention(pe):
        pe.wait_ge(s_evv, 3 + 12)
        pe.wait_ge(s_evk, 2 + 4 * 2)
        pe.wait_ge(s_mod, 6)
        pe.wait_ge(s_zero, 1)

        def slot(base, h, qt):
            s = base * TT + (TT * h + qt)
            if due(base, h, qt, 0):
                if qt == 0:
                    pe.wait_ge(s_qkh, base * 3 + (3 * h + 3))
                    pe.wait_ge(s_qkl, base * 3 + (3 * h + 3))
                if due(base, h, qt, 2):
                    pe.wait_ge(s_exp, s - 1)
                S = SCP[qt % 2]
                q = slice(qt * P, qt * P + P)
                for j in range(2):
                    for c0, c1 in ((0, 512), (512, 768)) if j == 0 else ((0, 256), (256, 768)):
                        o0 = j * KEYS
                        mm = three(S[:, o0 + c0:o0 + c1], Qh[h][:, j, q], Ql[h][:, j, q], Kh[h][:, c0:c1],
                                   Kl[h][:, c0:c1], (j, c0) != (1, 0), True, skip_group_check=True)
                mm.then_inc(s_sc, 1)
            if due(base, h, qt, 3):
                pe.wait_ge(s_at, s * 2 - 4)
            if due(base, h, qt, 4):
                pe.wait_ge(s_osq, s - 3)
            if due(base, h, qt, 2):
                pe.wait_ge(s_comb, s - 1)
                src = E[(qt - 2) % 4]
                for kt in range(KT):
                    mm = nc.tensor.transpose(PB[kt // 4][:, kt % 4 * P:kt % 4 * P + P], src[:, 0, kt * P:kt * P + P],
                                             ident[:, :])
                    if kt in (3, 5):
                        mm.then_inc((s_tra, s_trb)[kt // 4], 1)
            if due(base, h, qt, 4):
                dst = PB[1][:, bass.ds(s + (SUMS0 - 4), 1)]
                nc.tensor.matmul(dst, OSQ[qt % 2][:, :], ones[:, 0:1], start=True, stop=True,
                                 skip_group_check=True).then_inc(s_sub, 1)
            if due(base, h, qt, 3):
                if qt == 3:
                    pe.wait_ge(s_vb, base + (h + 1))
                v = VB[h] if qt == 3 else VB[1 - h]
                for kt in range(KT):
                    mm = nc.tensor.matmul(PB[1][:, PV0:PV0 + P], v[:, kt, :], AT[(qt - 3) % 2][:, kt, :],
                                          start=(kt == 0), stop=(kt == KT - 1), skip_group_check=True)
                mm.then_inc(s_pv, 1)

        over_heads(pe, slot)

    def act_attention(act):
        act.wait_ge(s_pw, PROJ_PW)
        act.wait_ge(s_ada, PROJ_ADA)
        nc.scalar.activation(ADS[:, :], PB[7], ACT.Copy).then_inc(s_ads, 1)

        def slot(base, h, qt):
            s = base * TT + (TT * h + qt)
            if due(base, h, qt, 2):
                if due(base, h, qt, 5):
                    act.wait_ge(s_pv, s - 4)
                act.wait_ge(s_tra, s - 1)
                src = PB[0].rearrange("p (a n) -> p a n", a=4)
                nc.scalar.activation(AT[qt % 2][:, 0:4, :], src, ACT.Copy).then_inc(s_at, 1)
            if due(base, h, qt, 0):
                if due(base, h, qt, 4):
                    act.wait_ge(s_trb, s - 3)
                act.wait_ge(s_bias, s + 1)
                for j in range(2):
                    ins = nc.scalar.activation(E[qt][:, j, :], SCP[qt % 2][:, j * KEYS:(j + 1) * KEYS], ACT.Exp,
                                               bias=row_bias[:, qt % 2, j:j + 1], scale=HD ** -0.5,
                                               accum_out=row_sum[:, qt % 2, j:j + 1])
                ins.then_inc(s_exp, 1)
            if due(base, h, qt, 3):
                if due(base, h, qt, 5):
                    act.wait_ge(s_sub, s - 4)
                act.wait_ge(s_pv, s - 2)
            if due(base, h, qt, 2):
                act.wait_ge(s_trb, s - 1)
                src = PB[1][:, 0:2 * P].rearrange("p (a n) -> p a n", a=2)
                nc.scalar.activation(AT[qt % 2][:, 4:6, :], src, ACT.Copy).then_inc(s_at, 1)
            if due(base, h, qt, 3):
                nc.scalar.activation(OSQ[(qt - 3) % 2][:, :], PB[1][:, PV0:PV0 + P], ACT.Square)
                q = (qt - 3) % TT
                dst = OF[:, bass.ds(base + (h - (qt < 3)), 1), q * P:q * P + P].rearrange("p a n -> p (a n)")
                nc.scalar.activation(dst, PB[1][:, PV0:PV0 + P], ACT.Copy).then_inc(s_osq, 1)

        over_heads(act, slot)

    def dve_split_hi(head, b, parts):
        q = QF[:, head, :].rearrange("p a n -> p (a n)")
        k = KF[:, head, :].rearrange("p a n -> p (a n)")
        steps = ((Qh[b][0:HD, 0, :], q[0:HD, :]), (Qh[b][HD:P, 1, :], q[HD:P, :]), (Kh[b][:, :], k))
        for n in parts:
            nc.vector.tensor_scalar(*steps[n], 1.0, None, ALU.mult).then_inc(s_qkh, 1)

    def dve_attention(dve):
        dve.wait_ge(s_rope, 1 + 16)
        dve.wait_ge(s_pw, PROJ_PW)
        for i in range(2):
            for q in (Qh, Ql):
                nc.vector.memset(q[i][HD:P, 0, :].bitcast(F32), 0.0)
                ins = nc.vector.memset(q[i][0:HD, 1, :].bitcast(F32), 0.0)
        ins.then_inc(s_zero, 1)
        dve_split_hi(slice(0, 1), 0, range(3))
        dve.wait_ge(s_adt, 6)
        dve_modulation(dve, 5, MOD[:, 1, 0:16], 0, CT2[:, 48:64]).then_inc(s_mod, 1)

        def slot(base, h, qt):
            s = base * TT + (TT * h + qt)
            par = qt % 2
            live = due(base, h, qt, 0)
            if live:
                dve.wait_ge(s_sc, s + 1)
                need(dve, s_bias, s)
                nc.vector.tensor_reduce(row_max[:, :], SCP[par].rearrange("p (j n) -> p j n", j=2), AX.X, ALU.max
                                        ).then_inc(s_rat, 1)
                dve.wait_ge(s_rat, s * 3 - 1 if begun(base, h, qt, 1) else 1)
                nc.vector.tensor_scalar(row_bias[:, par, :], row_max[:, :], -HD ** -0.5, None, ALU.mult).then_inc(
                    s_bias, 1)
            if due(base, h, qt, 1):
                par = 1 - par
                e = E[(qt - 1) % 4]
                dve.wait_ge(s_exp, s)
                if due(base, h, qt, 2):
                    dve.wait_ge(s_comb, s - 1)
                dst = sum_all[:, bass.ds(s - 1, 1)]
                nc.vector.tensor_scalar(dst, row_sum[:, par, 0:1], 1.0, None, ALU.mult)
                nc.vector.reciprocal(row_ratio[:, par, 0:1], row_sum[:, par, 1:2]).then_inc(s_rat, 1)
                dve.wait_ge(s_rat, s * 3 - (0 if live else 1))
                nc.vector.scalar_tensor_tensor(row_ratio[:, par, 1:2], row_ratio[:, par, 0:1], neg_lam[:, :],
                                               row_sum[:, par, 0:1], ALU.mult, ALU.mult).then_inc(s_rat, 1)
                dve.wait_ge(s_rat, s * 3 + (1 if live else 0))
                nc.vector.scalar_tensor_tensor(e[:, 0, :], e[:, 1, :], row_ratio[:, par, 1:2], e[:, 0, :], ALU.mult,
                                               ALU.add).then_inc(s_comb, 1)
            if qt < 3 and due(base, h, qt, -TT):
                need(dve, s_qkl, base * 3 + 3 * h)
                dve_split_hi(bass.ds(base + (h + 1), 1), 1 - h, (qt,))

        over_heads(dve, slot)

    def pool_attention(pool):
        pool.wait_ge(s_pw, PROJ_PW)
        pool.wait_ge(s_zero, 1)
        pool.wait_ge(s_rope, 1 + 16)
        pool.wait_ge(s_evv, 3 + 12)
        pool.wait_ge(s_ada, PROJ_ADA)
        pool.wait_ge(s_sin, 16)

        def lo(head, count, b):
            q = QF[:, head, :].rearrange("p a n -> p (a n)")
            k = KF[:, head, :].rearrange("p a n -> p (a n)")
            for n, (dst, src, hi) in enumerate(((Ql[b][0:HD, 0, :], q[0:HD, :], Qh[b][0:HD, 0, :]),
                                                (Ql[b][HD:P, 1, :], q[HD:P, :], Qh[b][HD:P, 1, :]),
                                                (Kl[b][:, :], k, Kh[b][:, :]))):
                pool.wait_ge(s_qkh, count + (n + 1))
                if n > 0:
                    pool.wait_ge(s_qkl, count + n)
                nc.gpsimd.tensor_tensor(dst, src, hi, ALU.subtract).then_inc(s_qkl, 1)
            pool.wait_ge(s_qkl, count + 3)

        def v_of_head(b, columns, count):
            nc.gpsimd.tensor_copy(VB[b][:, :, :], VF[:, :, columns]).then_inc(s_vb, 1)
            pool.wait_ge(s_vb, count)

        lo(slice(0, 1), 0, 0)
        v_of_head(0, slice(0, P), 1)
        lo(slice(1, 2), 3, 1)
        v_of_head(1, slice(P, 2 * P), 2)
        with pool.Fori(1, HEADS // 2) as body:
            for h in range(2):
                lo(bass.ds(body * 2 + h, 1), body * 6 + 3 * h, h)
                pool.wait_ge(s_pv, body * (2 * TT) + (TT * h - TT))
                v_of_head(h, bass.ds(body * (2 * P) + h * P, P), body * 2 + (h + 1))
    s_oland = [sem(f"w_out_landed_{i}") for i in range(8)]
    s_ohi = sem("w_out_hi_ready")
    s_olo = sem("w_out_lo_ready")
    s_opw = sem("w_out_piece_used")
    s_dga = sem("head_factors_on_diagonal")
    s_osp = sem("head_factors_spread")
    s_on = sem("head_output_normed")
    s_ohh = sem("head_output_hi_ready")
    s_ohl = sem("head_output_lo_ready")
    s_xo = sem("attention_added_to_stream")

    def split_piece(act, n, src, hi, landed, used, done):
        act.wait_ge(*landed)
        if n >= 2:
            act.wait_ge(used, n - 1)
        nc.scalar.activation(hi, src, ACT.Copy).then_inc(done, 1)

    def sp_out_projection(sp, pieces):
        for n in pieces:
            if n == 0:
                sp.wait_ge(s_ada, PROJ_ADA)
                sp.wait_ge(s_lo, RW_ + 24)
                sp.wait_ge(s_rope, 1 + 16)
            if n == 7:
                sp.wait_ge(s_olo, 3)
            src = t["da_w_out"][0, n % 4 * 256:n % 4 * 256 + 256, n // 4 * 512:n // 4 * 512 + 512]
            sp.dma_start(rawo[n][:, :, :], src.rearrange("(a p) n -> p a n", p=P)).then_inc(s_oland[n], 16)

    def pe_out_projection(pe):
        def spread(h):
            pe.wait_ge(s_dga, h + 1)
            if h >= 2:
                pe.wait_ge(s_on, h - 1)
            pe_spread(pe, s_osp, DGA[h % 2], PB[2 + h % 2], TT)

        pe.wait_ge(s_exp, SLOTS)
        spread(0)
        spread(1)
        for n in range(8):
            chunk, kp = n // 4, n % 4
            pe.wait_ge(s_olo, n + 1)
            if n == 4:
                pe.wait_ge(s_on, HEADS)
            for j in range(2):
                kt = 2 * kp + j
                if chunk == 0:
                    pe.wait_ge(s_ohl, kt + 1)
                for m in range(4):
                    w = slice(m * P, m * P + P)
                    mm = three(PB[4 * (1 - chunk) + m], stoh[n % 2][:, j, w], stol[n % 2][:, j, w], OHh[:, kt, :],
                               OHl[:, kt, :], kt == 0, kt == HEADS - 1)
                if chunk == 0 and kt + 2 < HEADS:
                    if j == 1:
                        mm.then_inc(s_opw, 1)
                    spread(kt + 2)
                elif j == 1:
                    mm.then_inc(s_opw, 1)

    def act_out_projection(act):
        act.wait_ge(s_sub, SLOTS)
        act.wait_ge(s_trb, SLOTS)

        def hi(n):
            split_piece(act, n, rawo[n][:, :, :], stoh[n % 2][:, :, :], (s_oland[n], 16), s_opw, s_ohi)

        hi(0)
        hi(1)
        for h in range(HEADS):
            act.wait_ge(s_on, h + 1)
            nc.scalar.activation(OHh[:, h, :], OF[:, h, :], ACT.Copy).then_inc(s_ohh, 1)
            if h in (3, 5):
                hi(2 + (h - 3) // 2)
        for n in range(4, 8):
            hi(n)

    def pool_out_projection(pool):
        for n in range(8):
            pool.wait_ge(s_ohi, n + 1)
            nc.gpsimd.tensor_tensor(stol[n % 2][:, :, :], rawo[n][:, :, :], stoh[n % 2][:, :, :],
                                    ALU.subtract).then_inc(s_olo, 1)

    def dve_out_projection(dve, ch):
        n = SLOTS
        dve.wait_ge(s_comb, SLOTS)
        ch.link(nc.vector.reciprocal(sum_all[:, :], sum_all[:, :]))
        dve.wait_ge(s_sub, SLOTS)
        ch.link(nc.vector.tensor_tensor(nv[:, :], PB[1][:, SUMS0:SUMS0 + n], sum_all[:, :], ALU.mult))
        ch.link(nc.vector.tensor_tensor(nv[:, :], nv[:, :], sum_all[:, :], ALU.mult))
        rsqrt(ch, nv[:, :], n, 1.0 / P)
        ch.link(nc.vector.tensor_tensor(ny[:, :], ny[:, :], sum_all[:, :], ALU.mult))

        def diag(h):
            if h >= 2:
                dve.wait_ge(s_osp, h - 1)
            for i in range(TT):
                ins = nc.vector.tensor_scalar(DGA[h % 2][:, i, :], ident[:, :], ny[:, TT * h + i:TT * h + i + 1], None,
                                              ALU.mult)
            ins.then_inc(s_dga, 1)

        diag(0)
        diag(1)
        dve.wait_ge(s_osq, SLOTS)
        for h in range(HEADS):
            dve.wait_ge(s_osp, h + 1)
            nc.vector.scalar_tensor_tensor(OF[:, h, :], OF[:, h, :], subg[:, :], PB[2 + h % 2], ALU.mult,
                                           ALU.mult).then_inc(s_on, 1)
            if h + 2 < HEADS:
                diag(h + 2)
            dve.wait_ge(s_ohh, h + 1)
            nc.vector.tensor_tensor(OHl[:, h, :], OF[:, h, :], OHh[:, h, :], ALU.subtract).then_inc(s_ohl, 1)
        dve_router_weights(ch, 0)
        dve_add_to_stream(dve, s_opw, 0, 16, (4, 0), s_xo)

    def dve_add_to_stream(dve, used, layer, gate, banks, done):
        for d in range(DT):
            if d % 4 == 0:
                dve.wait_ge(used, 4 * (d // 4 + 1))
            g = MOD[:, layer, gate + d:gate + d + 1]
            nc.vector.scalar_tensor_tensor(XT[:, d, :], PB[banks[d // 4] + d % 4], g, XT[:, d, :], ALU.mult,
                                           ALU.add).then_inc(done, 1)
    PAIRS = NE // 2
    PIECES = 12

    class Signals:

        KINDS = dict(
            rwc=("router_weights_ready", 3), fac=("token_factors_ready", 1), soft=("router_softmax_chain", 3), aff=("affinities_ready", 1),
            afft=("affinities_turned", 1), wk=("affinities_by_expert", 1), mask=("chosen_ready", 1),
            maskt=("chosen_turned", 1), mb=("chosen_in_bf16", 1), rank=("ranks_summed", 1),
            hb=("token_blocks_turned", 2 * TT), tm=("token_blocks_ready", 2 * TT), parts=("row_parts_summed", 1),
            pc0=("square_sums_copied", 1), pc1=("logit_parts_copied", 1), zero=("sums_zeroed", 1), oh=("one_hots_ready", PAIRS),
            smt=("one_hots_turned", PAIRS), sm=("one_hots_by_slot_ready", PAIRS), afm=("slot_affinities_summed", PAIRS),
            afc=("slot_affinities_ready", PAIRS), gath=("tokens_gathered", PAIRS),
            xsa=("gathered_first_half_copied", PAIRS), xsb=("gathered_second_half_copied", PAIRS),
            used=("expert_piece_used", PAIRS * PIECES), sg=("silu_ready", NE), hid=("hidden_ready", NE),
            hidm=("hidden_turned", NE), hidt=("hidden_by_feature_ready", NE), ys=("outputs_scaled", 2 * NE),
            yh=("outputs_hi_ready", PAIRS), yl=("outputs_lo_ready", PAIRS), sc=("outputs_scattered", PAIRS * DT),
            acc=("outputs_added", (PAIRS - 1) * DT), add=("experts_added_to_stream", DT))
        sems = {k: sem(name) for k, (name, _) in KINDS.items()}
        landed = [sem(f"ring_landed_{i}") for i in range(WR)]

        def __init__(self, layer):
            self.layer = layer

        def __getitem__(self, name):
            return self.landed if name == "land" else self.sems[name]

        def __call__(self, name, n, slot=None):
            if name == "land":
                return self.landed[slot], n + self.layer * (PAIRS * PIECES // WR * 16)
            return self.sems[name], n + self.layer * self.KINDS[name][1]

    ME = [Signals(0), Signals(1)]
    RING = [[ring[(i + 2) % WR] for i in range(WR)], ring]

    def over_pairs(eng, pair):
        pair(0, True, False)
        with eng.Fori(1, PAIRS - 1) as i:
            pair(i, False, False)
        pair(PAIRS - 1, False, True)

    def sp_moe(sp, L, before):
        S = ME[L]

        def load(i, r):
            name = ("moe_w_gate", "moe_w_up", "moe_w_down")[r % 6 // 2]
            src = t[name][L, bass.ds(i * 2 + r // 6, 1), r % 2 * 512:r % 2 * 512 + 512, :]
            sp.dma_start(RING[L][r % WR][:, :, :], src.rearrange("e (a p) n -> p (e a) n", p=P)).then_inc(
                S["land"][r % WR], 16)

        for r in range(WR):
            before(r)
            load(0, r)
        for r in range(WR, PIECES):
            sp.wait_ge(*S("used", r - WR + 1))
            load(0, r)
        with sp.Fori(1, PAIRS) as i:
            for r in range(PIECES):
                sp.wait_ge(*S("used", i * PIECES + (r - WR + 1)))
                load(i, r)

    FREE = [(4, 5, 6, 7, 0, 1, 2, 3), (0, 1, 2, 3, 4, 5, 6, 7)]
    CONST0 = TT * NE
    SUM0 = CONST0 + NE
    BLOCK = (2, 3, 4, 0)

    def pe_moe_head(pe, L, N, added):
        S, F = ME[L], FREE[L]
        pe.wait_ge(*S("rwc", 3))
        for d in range(DT):
            pe.wait_ge(added, max(d, 1) + 1)
            g, h = d % 4 * 32, (d + 2) % 4 * 32
            nc.tensor.matmul(PB[F[1]][g:g + 32, :], rw_pad[:, d, :], XT[:, d, :], start=(d < 4), stop=(d >= 4))
            pe.wait_ge(*N("squares", d + 1))
            mm = nc.tensor.matmul(PB[F[0]][h:h + 32, :], ones[:, 0:32], SQ[:, d, :], start=(d < 4), stop=(d >= 4))
        mm.then_inc(S["parts"], 1)
        small = PB[F[5]]
        nc.tensor.matmul(small[:, CONST0:CONST0 + NE], ones[:, :], const_lg[:, :], start=True, stop=True,
                         skip_group_check=True)
        pe.wait_ge(*S("pc0", 1))
        for i in range(TT):
            nc.tensor.matmul(small[:, SUM0 + i:SUM0 + i + 1], SUMC[:, i * P:i * P + P], select[:, 0:1], start=False,
                             stop=True, skip_group_check=True)
        pe.wait_ge(*S("pc1", 1))
        for i in range(TT):
            mm = nc.tensor.matmul(small[:, i * NE:i * NE + NE], LOGC[:, i * P:i * P + P], select[:, 0:NE],
                                  start=False, stop=True, skip_group_check=True)
        mm.then_inc(N["sums"], 1)

        def tokens(n):
            i, half = n % TT, n // TT
            if n >= 4:
                pe.wait_ge(*S("tm", n - 3))
            for j in range(4):
                mm = nc.tensor.transpose(PB[F[BLOCK[n % 4]]][:, j * P:j * P + P],
                                         XT[:, half * 4 + j, i * P:i * P + P], ident[:, :])
            mm.then_inc(S["hb"], 1)

        for n in range(4):
            tokens(n)
        pe.wait_ge(*S("aff", 1))
        for i in range(TT):
            mm = nc.tensor.transpose(PB[F[6]][0:NE, i * P:i * P + P], AFF[:, i, :], ident[:, :])
        mm.then_inc(S["afft"], 1)
        for n in range(4, 8):
            tokens(n)
        pe.wait_ge(*S("mask", 1))
        for i in range(TT):
            mm = nc.tensor.transpose(PB[F[7]][:, i * NE:i * NE + NE], MKT[:, i * P:i * P + P], ident[0:NE, 0:NE])
        mm.then_inc(S["maskt"], 1)
        pe.wait_ge(*S("mb", 1))
        for i in range(TT):
            for j in range(i + 1):
                mm = nc.tensor.matmul(PB[F[5]][:, i * NE:i * NE + NE], tri[:, :] if j == i else ones_b[:, :],
                                      MB[:, j, :], start=(i == 0), stop=(j == i), skip_group_check=True)
        mm.then_inc(S["rank"], 1)
        pe.wait_ge(*S("oh", 1))
        pe.wait_ge(*S("tm", 2 * TT))
        pe_gather(S)

    def pe_gather(S):
        for d in range(DT):
            for j in range(TT):
                mm = nc.tensor.matmul(PB[4 + d // 4][:, d % 4 * P:d % 4 * P + P], XTM[:, j, d * P:d * P + P],
                                      OH[:, j, :], start=(d % 4 == 0 and j == 0), stop=(j == TT - 1),
                                      skip_group_check=True)
        mm.then_inc(S["gath"], 1)

    def pe_scatter(pe, S, i):
        pe.wait_ge(*S("yl", i))
        for d in range(DT):
            if d == 0:
                pe.wait_ge(*S("afc", i))
            if d >= 2:
                if isinstance(i, int) and i == PAIRS:
                    pe.wait_ge(*S("add", d - 1))
                else:
                    pe.wait_ge(*S("acc", i * DT + (d - DT - 1)))
            w = slice(d * P, d * P + P)
            nc.tensor.matmul(PB[6 + d % 2], YH[:, w], SM[:, :], start=True, stop=False)
            nc.tensor.matmul(PB[6 + d % 2], YL[:, w], SM[:, :], start=False, stop=True).then_inc(S["sc"], 1)

    def pe_moe(pe, L):
        S = ME[L]

        def pair(i, first, last):
            for a in range(2):
                for m in range(3):
                    if m == 2:
                        if a == 0:
                            if not first:
                                pe_scatter(pe, S, i)
                            for j in range(TT):
                                mm = nc.tensor.transpose(PB[3][:, j * P:j * P + P], OH[:, j, :],
                                                         ident[:, :])
                            mm.then_inc(S["smt"], 1)
                            if not first:
                                pe.wait_ge(*S("acc", i * DT))
                            for e in range(2):
                                for j in range(TT):
                                    for half in range(2):
                                        mm = nc.tensor.matmul(PB[6][half * 64:half * 64 + 64, e * NE:e * NE + NE],
                                                              OH[:, j, e * 64:e * 64 + 64],
                                                              AFF[:, j, :],
                                                              start=(e == 0 and j == 0), stop=(j == TT - 1),
                                                              skip_group_check=True)
                            mm.then_inc(S["afm"], 1)
                            pe.wait_ge(*S("sm", i + 1))
                        elif not last:
                            pe.wait_ge(*S("oh", i + 2))
                            pe.wait_ge(*S("xsa", i + 1))
                            pe.wait_ge(*S("xsb", i + 1))
                            pe_gather(S)
                        pe.wait_ge(*S("hid", i * 2 + (a + 1)))
                        for j in range(4):
                            mm = nc.tensor.transpose(PB[3][:, j * P:j * P + P], HID[:, j * P:j * P + P], ident[:, :])
                        mm.then_inc(S["hidm"], 1)
                        pe.wait_ge(*S("hidt", i * 2 + (a + 1)))
                        if a == 1 or not first:
                            pe.wait_ge(*S("ys", i * 4 + (2 * a)))
                    elif m == 0 and a == 0:
                        pe.wait_ge(*S("xsa", i + 1))
                        pe.wait_ge(*S("xsb", i + 1))
                    elif m == 0:
                        pe.wait_ge(*S("hid", i * 2 + 1))
                    for half in range(2):
                        r = a * 6 + m * 2 + half
                        pe.wait_ge(*S("land", i * 32 + (r // WR + 1) * 16, r % WR))
                        for j in range(4):
                            for n in range(2):
                                k = half * 4 + j
                                if m < 2:
                                    x = XS[:, k, a * 64:a * 64 + 64]
                                else:
                                    x = HIDT[:, j, half * 64:half * 64 + 64]
                                mm = nc.tensor.matmul(PB[m][n * 64:n * 64 + 64, :], x,
                                                      RING[L][r % WR][:, j, n * 512:n * 512 + 512], start=(k == 0),
                                                      stop=(k == DT - 1))
                        mm.then_inc(S["used"], 1)

        over_pairs(pe, pair)
        pe_scatter(pe, S, PAIRS)

    def act_moe_head(act, L, N, added):
        S, F = ME[L], FREE[L]
        act_squares(act, N, XT, SQ, SEQ, (added, lambda d: d + 1))

        act.wait_ge(*S("parts", 1))
        nc.scalar.activation(LOGC[:, :], PB[F[1]], ACT.Copy).then_inc(S["pc1"], 1)

        def tokens(n):
            act.wait_ge(*S("hb", n + 1))
            i, half = n % TT, n // TT * 512
            nc.scalar.activation(XTM[:, i, half:half + 512], PB[F[BLOCK[n % 4]]], ACT.Copy,
                                 scale=ny[:, i:i + 1]).then_inc(S["tm"], 1)

        act.wait_ge(*S("soft", 2))
        nc.scalar.activation(LG[:, :, :], LG[:, :, :], ACT.Exp).then_inc(S["soft"], 1)
        act.wait_ge(*S("fac", 1))
        tokens(0)
        act.wait_ge(*S("afft", 1))
        nc.scalar.activation(WK[:, :], PB[F[6]][0:NE, :], ACT.Copy).then_inc(S["wk"], 1)
        for n in range(1, 2 * TT):
            tokens(n)
        act_gathered(act, L, 1)

    def act_gathered(act, L, count):
        S = ME[L]
        act.wait_ge(*S("gath", count))
        for d in range(4):
            ins = nc.scalar.activation(XS[:, d, :], PB[4][:, d * P:d * P + P], ACT.Identity,
                                       bias=MOD[:, L, 24 + d:25 + d], scale=coef[:, 2 + 2 * L, d:d + 1])
        ins.then_inc(S["xsa"], 1)

    def act_moe(act, L):
        S = ME[L]

        def pair(i, first, last):
            for a in range(2):
                act.wait_ge(*S("used", i * PIECES + (6 * a + 2)))
                if not first or a == 1:
                    act.wait_ge(*S("hid", i * 2 + a))
                nc.scalar.activation(SG[:, :], PB[0], ACT.Silu).then_inc(S["sg"], 1)
                if a == 0:
                    act.wait_ge(*S("smt", i + 1))
                    nc.scalar.activation(SM[:, :], PB[3], ACT.Copy).then_inc(S["sm"], 1)
                    act.wait_ge(*S("afm", i + 1))
                    if not first:
                        act.wait_ge(*S("ys", i * 4))
                    for e in range(2):
                        column = PB[6][:, bass.ds(i * 2 + (e * NE + e), 1)]
                        ins = nc.scalar.activation(aff_c[:, e:e + 1], column, ACT.Copy)
                    ins.then_inc(S["afc"], 1)
                elif not last:
                    act_gathered(act, L, i + 2)
                act.wait_ge(*S("hidm", i * 2 + (a + 1)))
                nc.scalar.activation(HIDT[:, :, :], PB[3].rearrange("p (a n) -> p a n", a=4), ACT.Copy).then_inc(
                    S["hidt"], 1)
                act.wait_ge(*S("used", i * PIECES + (6 * a + 6)))
                if a == 0:
                    act.wait_ge(*S("afc", i + 1))
                    if not first:
                        act.wait_ge(*S("yl", i))
                for half in range(2):
                    rows = slice(half * 64, half * 64 + 64)
                    nc.scalar.activation(YS[a * 64:a * 64 + 64, half * 512:half * 512 + 512], PB[2][rows, :], ACT.Copy,
                                         scale=aff_c[rows, a:a + 1]).then_inc(S["ys"], 1)
            act.wait_ge(*S("ys", i * 4 + 4))
            if not first:
                act.wait_ge(*S("sc", i * DT))
            nc.scalar.activation(YH[:, :], YS[:, :], ACT.Copy).then_inc(S["yh"], 1)

        over_pairs(act, pair)

    def dve_one_hots(S, e):
        for j in range(TT):
            for a in range(2):
                ins = nc.vector.tensor_scalar(OH[:, j, a * CAP:a * CAP + CAP], slots[:, :], PM[:, j, e(a)], None,
                                              ALU.is_equal)
        ins.then_inc(S["oh"], 1)

    def dve_router_weights(ch, L):
        S = ME[L]
        n = 2 + 2 * L
        dve_coef(ch, n, MOD[:, L, 32:40], CT1[:, R_MOE + 8 * L:R_MOE + 8 * L + 8])
        for d in range(DT):
            ins = nc.vector.tensor_scalar(shift_rw[:, d, :], rw[:, L, d, :], MOD[:, L, 24 + d:25 + d], None, ALU.mult)
        ins.then_inc(S["rwc"], 1)
        nc.vector.memset(rw_pad[:, :, NE:32], 0.0)
        for d in range(DT):
            ins = nc.vector.tensor_scalar(rw_pad[:, d, 0:NE], rw[:, L, d, :], coef[:, n, d:d + 1], None, ALU.mult)
        ins.then_inc(S["rwc"], 1)
        ch.eng.wait_ge(*S("rwc", 1))
        nc.vector.tensor_reduce(const_lg[:, :], shift_rw.rearrange("p a n -> p n a"), AX.X, ALU.add).then_inc(
            S["rwc"], 1)

    def dve_moe_head(dve, ch, L, N, added):
        S, F = ME[L], FREE[L]
        dve.wait_ge(*S("parts", 1))
        nc.vector.tensor_copy(SUMC[:, :], PB[F[0]]).then_inc(S["pc0"], 1)
        sums = PB[F[5]]
        dve.wait_ge(*N("sums", 1))
        rsqrt(ch, sums[:, SUM0:SUM0 + TT], TT, 1.0 / D)
        ch.link(nc.vector.tensor_copy(const_lg[:, :], sums[:, CONST0:CONST0 + NE]))
        for i in range(TT):
            lg = sums[:, i * NE:i * NE + NE]
            ins = nc.vector.scalar_tensor_tensor(LG[:, i, :], lg, ny[:, i:i + 1], const_lg[:, :], ALU.mult, ALU.add)
        ch.link(ins)
        nc.vector.tensor_reduce(st4[:, 0, :], LG[:, :, :], AX.X, ALU.max).then_inc(S["soft"], 1)
        dve.wait_ge(*S("soft", 1))
        for i in range(TT):
            ins = nc.vector.tensor_scalar(LG[:, i, :], LG[:, i, :], st4[:, 0, i:i + 1], None, ALU.subtract)
        ins.then_inc(S["soft"], 1)
        nc.vector.tensor_copy(na[:, 0:TT], ny[:, 0:TT]).then_inc(S["fac"], 1)
        dve.wait_ge(*S("soft", 3))
        ch.link(nc.vector.tensor_reduce(st4[:, 1, :], LG[:, :, :], AX.X, ALU.add))
        ch.link(nc.vector.reciprocal(st4[:, 0, :], st4[:, 1, :]))
        for i in range(TT):
            ins = nc.vector.tensor_scalar(AFF[:, i, :], LG[:, i, :], st4[:, 0, i:i + 1], None, ALU.mult)
        ins.then_inc(S["aff"], 1)

        dve.wait_ge(*S("wk", 1))
        for n in range(CAP // 8):
            ch.link(nc.vector.max(M8[:, :], WK[:, :]))
            ch.link(nc.vector.match_replace(WK[:, :], M8[:, :], WK[:, :], -1.0))
        nc.vector.tensor_scalar(MKT[:, :], WK[:, :], 0.0, None, ALU.is_lt).then_inc(S["mask"], 1)
        dve.wait_ge(*S("maskt", 1))
        nc.vector.tensor_copy(MB[:, :, :], PB[F[7]][:, 0:TT * NE].rearrange("p (a n) -> p a n", a=TT)).then_inc(
            S["mb"], 1)
        dve.wait_ge(*S("mb", 1))
        dve.wait_ge(*S("rank", 1))
        ch.link(nc.vector.tensor_tensor(PM[:, :, :], PB[F[5]][:, 0:TT * NE].rearrange("p (a n) -> p a n", a=TT),
                                        MB[:, :, :], ALU.mult))
        dve_one_hots(S, lambda a: slice(a, a + 1))
        nc.vector.memset(ACC[:, :, :], 0.0).then_inc(S["zero"], 1)
        dve_gathered(dve, L, 1)

    def dve_gathered(dve, L, count):
        S = ME[L]
        dve.wait_ge(*S("gath", count))
        for d in range(4, DT):
            ins = nc.vector.tensor_scalar(XS[:, d, :], PB[5][:, (d - 4) * P:(d - 3) * P], coef[:, 2 + 2 * L, d:d + 1],
                                          MOD[:, L, 24 + d:25 + d], ALU.mult, ALU.add)
        ins.then_inc(S["xsb"], 1)

    def dve_moe(dve, L):
        S = ME[L]
        dve.wait_ge(*S("zero", 1))

        def add(i):
            for d in range(DT):
                if d == 0 and not (isinstance(i, int) and i == 1):
                    dve.wait_ge(*S("yl", i))
                dve.wait_ge(*S("sc", i * DT + (d - DT + 1)))
                nc.vector.tensor_tensor(ACC[:, d, :], PB[6 + d % 2], ACC[:, d, :], ALU.add).then_inc(S["acc"], 1)

        def pair(i, first, last):
            for a in range(2):
                dve.wait_ge(*S("sg", i * 2 + (a + 1)))
                dve.wait_ge(*S("used", i * PIECES + (6 * a + 4)))
                if not first or a == 1:
                    dve.wait_ge(*S("hidm", i * 2 + a))
                nc.vector.tensor_tensor(HID[:, :], PB[1], SG[:, :], ALU.mult).then_inc(S["hid"], 1)
                if a == 0 and not first:
                    add(i)
                if a == 0 and last:
                    dve.wait_ge(*S("acc", i * DT))
                    for d in range(DT):
                        nc.vector.scalar_tensor_tensor(XT[:, d, :], ACC[:, d, :], MOD[:, L, 40 + d:41 + d],
                                                       XT[:, d, :], ALU.mult, ALU.add)
                if a == 0 and not last:
                    dve.wait_ge(*S("afm", i + 1))
                    dve_one_hots(S, lambda a: bass.ds(i * 2 + (2 + a), 1))
            if not last:
                dve_gathered(dve, L, i + 2)
            dve.wait_ge(*S("yh", i + 1))
            if not first:
                dve.wait_ge(*S("sc", i * DT))
            nc.vector.tensor_tensor(YL[:, :], YS[:, :], YH[:, :], ALU.subtract).then_inc(S["yl"], 1)

        over_pairs(dve, pair)
        for d in range(DT):
            dve.wait_ge(*S("sc", (PAIRS - 1) * DT + d + 1))
            nc.vector.scalar_tensor_tensor(XT[:, d, :], PB[6 + d % 2], MOD[:, L, 40 + d:41 + d], XT[:, d, :], ALU.mult,
                                           ALU.add).then_inc(S["add"], 1)
    V_PIECES = U_PIECES = GW // 512 * (DT // 2)
    O_PIECES = D // 512 * (GW // P // 2)
    s_gland = [sem(f"gmlp_w_landed_{i}") for i in range(RAWG)]
    s_ghi = sem("gmlp_w_hi_ready")
    s_glo = sem("gmlp_w_lo_ready")
    s_gused = sem("gmlp_w_piece_used")
    s_gs = sem("spatial_weights_landed")
    s_vsq = sem("v_squared")
    s_ws = sem("spatial_weights_turned")
    s_wc = sem("spatial_weights_copied")
    s_rl = sem("scaled_spatial_weights_ready")
    s_ut = sem("u_activated")
    s_sv = sem("gates_summed")
    s_gt = sem("gate_chain")
    s_gh = sem("gated_hi_ready")
    s_gl = sem("gated_lo_ready")
    s_xg = sem("gmlp_added_to_stream")
    V_AHEAD = 8

    def sp_gmlp(sp):
        sp.wait_ge(*ME[0]("used", PAIRS * PIECES))
        sp.dma_start(WSR[:, :, :], t["gm_w_s"][0].rearrange("g p q -> p g q")).then_inc(s_gs, 16)
        sp.dma_start(BSB.rearrange("p g n -> p (g n)"), t["gm_b_s"][0].rearrange("g n -> (g n)").partition_broadcast(P)
                     ).then_inc(s_gs, 16)
        sp.wait_ge(*ME[0]("sc", PAIRS * DT))
        sp.wait_ge(*ME[0]("yl", PAIRS))
        for n in range(V_PIECES + U_PIECES + O_PIECES):
            if n >= RAWG:
                sp.wait_ge(s_glo, n - RAWG + 1)
            if n < V_PIECES + U_PIECES:
                c = GW + n // 4 * 512 if n < V_PIECES else (n - V_PIECES) // 4 * 512
                src = t["gm_w_in"][0, n % 4 * 256:n % 4 * 256 + 256, c:c + 512]
            else:
                m = n - V_PIECES - U_PIECES
                src = t["gm_w_out"][0, m % 8 * 256:m % 8 * 256 + 256, m // 8 * 512:m // 8 * 512 + 512]
            sp.dma_start(rawg[n % RAWG][:, :, :], src.rearrange("(a p) n -> p a n", p=P)).then_inc(
                s_gland[n % RAWG], 16)

    def pool_gmlp(pool):
        for n in range(V_PIECES + U_PIECES + O_PIECES):
            pool.wait_ge(s_ghi, n + 1)
            nc.gpsimd.tensor_tensor(stgl[n % 2][:, :, :], rawg[n % RAWG][:, :, :], stgh[n % 2][:, :, :],
                                    ALU.subtract).then_inc(s_glo, 1)

    def pe_gmlp(pe):
        pe_sums(pe, ng, SQ1, PB[0], SEQ)
        pe.wait_ge(*ng("diag", 1))
        pe_spread(pe, ng["spread"], DG1, PB[1], TT)
        pe.wait_ge(s_gs, 32)
        for g in range(GROUPS):
            mm = nc.tensor.transpose(PB[2 + g // 4][:, g % 4 * P:g % 4 * P + P], WSR[:, g, :], ident[:, :])
        mm.then_inc(s_ws, 1)
        pe.wait_ge(s_wc, 2)
        with pe.Fori(0, 2) as body:
            for c in range(2):
                for n in range(4):
                    pe.wait_ge(s_glo, body * 8 + (c * 4 + n + 1))
                    for j in range(2):
                        kt = 2 * n + j
                        pe.wait_ge(*ng("lo", kt + 1))
                        for i in range(TT):
                            if kt == 0:
                                pe.wait_ge(s_gel, body * 8 + (c * 4 + i + 1))
                            tok = slice(i * P, i * P + P)
                            mm = three(PB[4 * c + i], H1h[:, kt, tok], H1l[:, kt, tok], stgh[n % 2][:, j, :],
                                       stgl[n % 2][:, j, :], kt == 0, kt == DT - 1)
                    mm.then_inc(s_gused, 1)
        for c in range(4):
            for n in range(4):
                pe.wait_ge(s_glo, V_PIECES + c * 4 + n + 1)
                for j in range(2):
                    kt = 2 * n + j
                    for m in range(4):
                        if kt == 0:
                            if c == 0:
                                pe.wait_ge(s_gel, V_AHEAD + 8 + m + 1)
                            else:
                                pe.wait_ge(s_ut, (c - 1) * 4 + m + 1)
                        w = slice(m * P, m * P + P)
                        mm = three(PB[m], stgh[n % 2][:, j, w], stgl[n % 2][:, j, w], H1h[:, kt, :], H1l[:, kt, :],
                                   kt == 0, kt == DT - 1)
                mm.then_inc(s_gused, 1)
            for m in range(4):
                f = 4 * c + m
                if c == 0:
                    pe.wait_ge(s_gel, V_AHEAD + 16)
                    pe.wait_ge(s_rl, TT)
                else:
                    pe.wait_ge(s_gt, 2 * (f - 4) + 1)
                g = slice(f // 2 * P, f // 2 * P + P)
                for i in range(TT):
                    mm = nc.tensor.matmul(PB[4 + m][:, i * P:i * P + P], V1[:, f, i, :], RW1[:, i, g], start=(i == 0),
                                          stop=True, skip_group_check=True)
                mm.then_inc(s_sv, 1)
        for n in range(O_PIECES):
            chunk, kp = n // 8, n % 8
            pe.wait_ge(s_glo, V_PIECES + U_PIECES + n + 1)
            for j in range(2):
                kt = 2 * kp + j
                if chunk == 0:
                    pe.wait_ge(s_gl, kt + 1)
                for m in range(4):
                    if kt == 0:
                        if chunk == 0:
                            pe.wait_ge(s_ut, 12 + m + 1)
                        else:
                            pe.wait_ge(s_gt, 2 * (12 + m) + 1)
                    w = slice(m * P, m * P + P)
                    mm = three(PB[4 * chunk + m], stgh[n % 2][:, j, w], stgl[n % 2][:, j, w], GH[:, kt, :],
                               GL[:, kt, :], kt == 0, kt == GW // P - 1)
            mm.then_inc(s_gused, 1)

    def act_gmlp(act):
        def hi(n):
            split_piece(act, n, rawg[n % RAWG][:, :, :], stgh[n % 2][:, :, :], (s_gland[n % RAWG], (n // RAWG + 1) * 16),
                        s_gused, s_ghi)

        for n in (0, 1):
            hi(n)
        act_squares(act, ng, XT, SQ1, SEQ, (ME[0]["add"], lambda d: d + 1))
        for d in range(DT):
            act.wait_ge(*ng("scaled", d + 1))
            nc.scalar.activation(H1h[:, d, :], U1[:, d, :], ACT.Identity, bias=MOD[:, 1, d:d + 1]).then_inc(ng["hi"], 1)
        act.wait_ge(s_ws, 1)
        for i in range(2):
            src = PB[2 + i].rearrange("p (a n) -> p a n", a=4)
            nc.scalar.activation(WST[:, 4 * i:4 * i + 4, :], src, ACT.Copy).then_inc(s_wc, 1)

        def v_tile(c, i):
            n = 4 * c + i
            act.wait_ge(s_gused, 4 * c + 4)
            v = V1[:, 4 * c:4 * c + 4, i, :]
            src = PB[4 * (c % 2) + i].rearrange("p (a n) -> p a n", a=4)
            nc.scalar.activation(v, src, ACT.Gelu_apprx_tanh).then_inc(s_gel, 1)
            act.wait_ge(s_gel, V_AHEAD + n + 1)
            need(act, s_vsq, n)
            nc.scalar.activation(VT.rearrange("p (a n) -> p a n", a=4), v, ACT.Square,
                                 accum_out=vsq[:, i, c:c + 1]).then_inc(s_vsq, 1)

        def u_tile(c, m):
            act.wait_ge(s_gused, V_PIECES + 4 * c + 4)
            if c > 0:
                act.wait_ge(s_gt, 2 * (4 * (c - 1) + m) + 2)
            nc.scalar.activation(UT[:, m, :], PB[m], ACT.Gelu_apprx_tanh).then_inc(s_ut, 1)

        for n in range(2, V_PIECES + U_PIECES + O_PIECES):
            c = n // 4 - 1
            if 0 <= c < 4 and n % 4 in (1, 2):
                for i in range(2):
                    v_tile(c, 2 * (n % 4 - 1) + i)
            if 4 <= c < 8 and n % 4 == 1:
                for i in range(4):
                    u_tile(c - 4, i)
            hi(n)

    def dve_gmlp(dve, ch):
        dve_coef(ch, 3, MOD[:, 1, 8:16], CT1[:, R_MIX + 8:R_MIX + 16])
        dve.wait_ge(*ng("sums", 1))
        rsqrt(ch, PB[0][:, 0:TT], TT, 1.0 / D)
        diagonal(DG1, TT, ng["diag"])
        dve.wait_ge(*ng("spread", 1))
        dve.wait_ge(*ME[0]("add", DT))
        for d in range(DT + 1):
            if d < DT:
                nc.vector.scalar_tensor_tensor(U1[:, d, :], XT[:, d, :], coef[:, 3, d:d + 1], PB[1], ALU.mult,
                                               ALU.mult).then_inc(ng["scaled"], 1)
            if d > 0:
                dve.wait_ge(*ng("hi", d))
                nc.vector.scalar_tensor_tensor(H1l[:, d - 1, :], U1[:, d - 1, :], MOD[:, 1, d - 1:d],
                                               H1h[:, d - 1, :], ALU.add, ALU.subtract).then_inc(ng["lo"], 1)
        dve.wait_ge(s_vsq, 16)
        ch.link(nc.vector.tensor_reduce(nv[:, 0:TT], vsq[:, :, :], AX.X, ALU.add))
        rsqrt(ch, nv[:, 0:TT], TT, 1.0 / GW)
        for i in range(TT):
            nc.vector.tensor_scalar(RW1[:, i, :], WST.rearrange("p g n -> p (g n)"), ny[:, i:i + 1], None,
                                    ALU.mult).then_inc(s_rl, 1)
        for f in range(GW // P):
            buf = (VT, GT)[f % 2]
            dve.wait_ge(s_sv, f + 1)
            if f >= 2:
                dve.wait_ge(s_gl, f - 1)
            for i in range(TT):
                tok = slice(i * P, i * P + P)
                ins = nc.vector.scalar_tensor_tensor(buf[:, tok], PB[4 + f % 4][:, tok], CT1[:, R_VG + f:R_VG + f + 1],
                                                     BSB[:, f // 2, :], ALU.mult, ALU.add)
            ins.then_inc(s_gt, 1)
            dve.wait_ge(s_gt, 2 * f + 1)
            dve.wait_ge(s_ut, f + 1)
            nc.vector.tensor_tensor(buf[:, :], buf[:, :], UT[:, f % 4, :], ALU.mult).then_inc(s_gt, 1)
            dve.wait_ge(s_gt, 2 * f + 2)
            nc.vector.tensor_copy(GH[:, f, :], buf[:, :]).then_inc(s_gh, 1)
            dve.wait_ge(s_gh, f + 1)
            nc.vector.tensor_tensor(GL[:, f, :], buf[:, :], GH[:, f, :], ALU.subtract).then_inc(s_gl, 1)
        dve_router_weights(ch, 1)
        for d in range(DT):
            if d % 4 == 0:
                dve.wait_ge(s_gused, V_PIECES + U_PIECES + 8 * (d // 4 + 1))
            nc.vector.scalar_tensor_tensor(XT[:, d, :], PB[d], MOD[:, 1, 16 + d:17 + d], XT[:, d, :], ALU.mult,
                                           ALU.add).then_inc(s_xg, 1)

    s_fsq = sem("final_squares_ready")
    s_fsum = sem("final_squares_summed")
    s_fg = sem("stream_times_gain_ready")
    s_fny = sem("final_factors_ready")
    s_ft = sem("final_blocks_turned")
    s_fo = sem("final_second_halves_ready")
    s_fo2 = sem("final_first_halves_ready")
    s_out = sem("output_written")

    def act_final(act):
        for d in range(DT):
            act.wait_ge(*ME[1]("add", d + 1))
            nc.scalar.activation(FSQ[:, d, :], XT[:, d, :], ACT.Square).then_inc(s_fsq, 1)
        act.wait_ge(s_fny, 1)
        for n in range(1, 2 * TT, 2):
            act.wait_ge(s_ft, n + 1)
            nc.scalar.activation(FO[:, n // 2, 512:1024], PB[n], ACT.Copy, scale=ny[:, n // 2:n // 2 + 1]).then_inc(
                s_fo, 1)

    def dve_final(dve, ch):
        for d in range(DT):
            dve.wait_ge(*ME[1]("add", d + 1))
            nc.vector.tensor_scalar(FG[:, d, :], XT[:, d, :], CT1[:, R_FIN + d:R_FIN + d + 1], None, ALU.mult).then_inc(
                s_fg, 1)
        dve.wait_ge(s_fsum, 1)
        rsqrt(ch, PB[1][:, 0:TT], TT, 1.0 / D)
        nc.vector.tensor_copy(st4[:, 0, :], ny[:, 0:TT]).then_inc(s_fny, 1)
        for n in range(0, 2 * TT, 2):
            dve.wait_ge(s_ft, n + 1)
            nc.vector.tensor_scalar(FO[:, n // 2, 0:512], PB[n], ny[:, n // 2:n // 2 + 1], None, ALU.mult).then_inc(
                s_fo2, 1)

    def pe_final(pe):
        for d in range(DT):
            pe.wait_ge(s_fsq, d + 1)
            for i in range(TT):
                mm = nc.tensor.matmul(PB[1][:, i:i + 1], FSQ[:, d, i * P:i * P + P], ones[:, 0:1],
                                      start=(d == 0 and i == 0), stop=(d == DT - 1), skip_group_check=True)
        mm.then_inc(s_fsum, 1)
        pe.wait_ge(s_fg, DT)
        for n in range(2 * TT):
            if n == 1:
                pe.wait_ge(s_fny, 1)
            for j in range(4):
                mm = nc.tensor.transpose(PB[n][:, j * P:j * P + P], FG[:, n % 2 * 4 + j, n // 2 * P:n // 2 * P + P],
                                         ident[:, :])
            mm.then_inc(s_ft, 1)

    def sp_final(sp):
        for i in range(TT):
            sp.wait_ge(s_fo, i + 1)
            sp.wait_ge(s_fo2, i + 1)
            sp.dma_start(out[0, i * P:i * P + P, :], FO[:, i, :]).then_inc(s_out, 16)
        sp.wait_ge(s_out, TT * 16)

    def before_experts_0(sp):
        def before(r):
            if r == 0:
                sp.wait_ge(s_qkl, 3 * HEADS)
                sp.wait_ge(s_vb, HEADS)
            elif r == 4:
                sp_out_projection(sp, (7,))
                sp.wait_ge(s_ohl, HEADS)
            elif r == 5:
                sp.wait_ge(s_osp, HEADS)
                sp.wait_ge(s_olo, 2)
        return before

    def before_experts_1(sp):
        def before(r):
            if r == 0:
                sp.wait_ge(s_gused, V_PIECES + U_PIECES)
            elif r == 2:
                sp.wait_ge(s_sv, GW // P)
            elif r == 4:
                sp.wait_ge(s_gl, GW // P)
            elif r == 5:
                sp.wait_ge(s_gused, V_PIECES + U_PIECES + O_PIECES)
        return before

    block = ctx.enter_context(nc.Block())

    @block.sync
    def _(sp):
        sp_projections(sp)
        sp_out_projection(sp, range(7))
        sp_moe(sp, 0, before_experts_0(sp))
        sp_gmlp(sp)
        sp_moe(sp, 1, before_experts_1(sp))
        sp_final(sp)

    @block.tensor
    def _(pe):
        pe_head(pe)
        pe_projections(pe)
        pe_attention(pe)
        pe_out_projection(pe)
        pe_moe_head(pe, 0, nm0, s_xo)
        pe_moe(pe, 0)
        pe_gmlp(pe)
        pe_moe_head(pe, 1, nm1, s_xg)
        pe_moe(pe, 1)
        pe_final(pe)

    @block.scalar
    def _(act):
        act_head(act)
        act_projections(act)
        act_attention(act)
        act_out_projection(act)
        act_moe_head(act, 0, nm0, s_xo)
        act_moe(act, 0)
        act_gmlp(act)
        act_moe_head(act, 1, nm1, s_xg)
        act_moe(act, 1)
        act_final(act)

    @block.vector
    def _(dve):
        ch = Chain(dve, s_dve)
        dve_head(dve, ch)
        dve_projections(dve)
        dve_attention(dve)
        dve_out_projection(dve, ch)
        dve_moe_head(dve, ch, 0, nm0, s_xo)
        dve_moe(dve, 0)
        dve_gmlp(dve, ch)
        dve_moe_head(dve, ch, 1, nm1, s_xg)
        dve_moe(dve, 1)
        dve_final(dve, ch)

    @block.gpsimd
    def _(pool):
        pool_head(pool)
        pool_projections(pool)
        pool_attention(pool)
        pool_out_projection(pool)
        pool_gmlp(pool)


def bass_hybrid_trunk(nc, t, out):
    with ExitStack() as ctx:
        build(nc, ctx, t, out)


_INS = ['x', 'c', 'ctx', 'c_ctx', 'ada_w', 'ada_b', 'mixer_norm_g', 'moe_norm_g', 'router_w', 'moe_w_gate', 'moe_w_up',
        'moe_w_down', 'da_w_in', 'da_lambda_q1', 'da_lambda_k1', 'da_lambda_q2', 'da_lambda_k2', 'da_subln_g',
        'da_w_out', 'gm_w_in', 'gm_v_g', 'gm_w_s', 'gm_b_s', 'gm_w_out', 'final_norm_g']


def kernel(**inputs):
    import numpy as _np
    import concourse.bacc as _bacc
    from concourse import mybir as _mybir
    from concourse.bass_utils import run_bass_kernel_spmd as _run

    nc = _bacc.Bacc("TRN2", target_bir_lowering=False, num_devices=1)
    arrays = {f"in_{name}_dram": _np.ascontiguousarray(inputs[name]) for name in _INS}
    arrays["in_shape_constants_dram"] = shape_constants()
    tensors = {}
    for name, a in arrays.items():
        dtype = _mybir.dt.from_np(a.dtype)
        tensors[name[3:-5]] = nc.dram_tensor(name, a.shape, dtype, kind="ExternalInput").ap()
    out = nc.dram_tensor("out_0_dram", (1, SEQ, D), _mybir.dt.from_np(_np.dtype("float32")), kind="ExternalOutput").ap()
    bass_hybrid_trunk(nc, tensors, out)
    return _run(nc, [arrays], core_ids=[0]).results[0]["out_0_dram"]
```

```python
from contextlib import ExitStack

import numpy as np

import concourse.bass as bass
from concourse import mybir

F32 = mybir.dt.float32
F32R = mybir.dt.float32r
BF16 = mybir.dt.bfloat16
I32 = mybir.dt.int32
ALU = mybir.AluOpType
ACT = mybir.ActivationFunctionType
AX = mybir.AxisListType

P = 128
D = 1024
DT = D // P
SEQ = 512
TT = SEQ // P
CTX = 256
CT = CTX // P
KEYS = CTX + SEQ
KT = KEYS // P
GRID_W = 64
EPS = 1e-6
HEADS = 8
HD = 64
LAM_INIT = 0.2
SUB_SCALE = 1.0 - LAM_INIT
GW = 2048
GROUPS = 8
NE = 16
CAP = 64
KB = 1024

R_C, R_CC, R_MIX, R_MOE, R_FIN, R_SUB, R_VG, R_N = 0, 8, 16, 32, 48, 56, 57, 73


def rope_tables():
    n = HD // 4
    inv = (np.float32(10000.0) ** (-np.arange(n, dtype=np.float32) / np.float32(n))).astype(np.float32)
    t = np.arange(SEQ)
    rows, cols = (t // GRID_W).astype(np.float32), (t % GRID_W).astype(np.float32)
    cos, sin = np.zeros((P, SEQ), np.float32), np.zeros((P, SEQ), np.float32)
    for p in range(P):
        r = p % HD
        ang = ((rows if r < 32 else cols) * inv[r % 16]).astype(np.float32)
        cos[p] = np.cos(ang)
        sin[p] = np.sin(ang) * (-1.0 if r % 32 < 16 else 1.0)
    return cos, sin


def shape_constants():
    cos, sin = rope_tables()
    ident = np.eye(P, dtype=np.float32)
    tri = np.triu(np.ones((P, P), np.float32))
    slots = np.broadcast_to(np.arange(1, CAP + 1, dtype=np.float32), (P, CAP))
    select = np.tile(np.eye(32, dtype=np.float32), (4, 1))
    return np.ascontiguousarray(np.concatenate([cos, sin, ident, tri, slots, select], axis=1))


def build(nc, ctx, t, out):
    base = 16512

    def at(name, kb, shape, dt=F32):
        return nc.alloc_sbuf_tensor_at(name, shape, dt, offset=base + int(kb * KB))

    cursor = [16 * KB]

    def small(name, shape, dt=F32):
        a = nc.alloc_sbuf_tensor_at(name, shape, dt, offset=base + cursor[0])
        size = int(np.prod(shape[1:])) * (2 if dt == BF16 else 4)
        cursor[0] += (size + 31) // 32 * 32
        assert cursor[0] <= 26 * KB
        return a

    def sem(name):
        return ctx.enter_context(nc.semaphore(name))

    XT = at("XT", 0, [P, DT, SEQ])
    ident = small("ident", [P, P])
    ones = small("ones", [P, P])
    slots = small("slots", [P, CAP])
    select = small("select", [P, 32])
    tri = small("tri", [P, P], BF16)
    ones_b = small("ones_b", [P, P], BF16)
    CT1 = small("CT1", [P, R_N])
    CT2 = small("CT2", [P, 96])
    silu_c = small("silu_c", [P, DT, 32])
    MOD = small("MOD", [P, 2, 48])
    MODC = small("MODC", [P, 16])
    coef = small("coef", [P, 5, DT])
    rw = small("rw", [P, 2, DT, NE])
    lam4 = at("lam4", 120, [P, 4, HD])
    shift_rw = small("shift_rw", [P, DT, NE])
    const_lg = small("const_lg", [P, NE])
    lam_s = small("lam_s", [P, 4])
    neg_lam = small("neg_lam", [P, 1])
    subg = small("subg", [P, 1])
    nv = small("nv", [P, HEADS * TT])
    ny = small("ny", [P, HEADS * TT])
    na = small("na", [P, HEADS * TT])
    fv = small("fv", [P, HEADS * TT])
    head_f = small("head_f", [P, HEADS * TT])
    row_max = small("row_max", [P, 2])
    row_bias = small("row_bias", [P, 2, 2])
    row_sum = small("row_sum", [P, 2, 2])
    row_ratio = small("row_ratio", [P, 2, 2])
    sum_all = small("sum_all", [P, HEADS * TT])
    AFF = small("AFF", [P, TT, NE])
    PM = small("PM", [P, TT, NE])
    MB = small("MB", [P, TT, NE], BF16)
    LG = small("LG", [P, TT, NE])
    st4 = small("st4", [P, 2, TT])
    aff_c = small("aff_c", [P, 2])
    M8 = small("M8", [NE, 8])
    vsq = small("vsq", [P, TT, 4])

    XR = at("XR", 58, [P, TT, D])
    CR = at("CR", 74, [P, CT, D])
    CXT = at("CXT", 82, [P, DT, CTX])
    SQ0 = at("SQ0", 90, [P, DT, SEQ])
    SQC = at("SQC", 111, [P, DT, CTX])
    DGC = at("DGC", 119, [P, CT, P])
    ROWS1 = at("ROWS1", 106, [R_N, P])
    ROWS2 = at("ROWS2", 107, [96, P])
    TRI0 = at("TRI0", 108, [P, P])
    ROWX = at("ROWX", 202, [P, SEQ])
    ROWC = at("ROWC", 204, [P, CTX])
    U0 = at("U0", 58, [P, DT, SEQ])
    UC0 = at("UC0", 74, [P, DT, CTX])
    DG0 = at("DG0", 109, [P, TT, P])
    H0h = at("H0h", 122, [P, DT, KEYS], F32R)
    H0l = at("H0l", 146, [P, DT, KEYS], F32R)
    RA, RW_ = 8, 3
    rawa = [at(f"rawa_{i}", 26 + 4 * i, [P, 1024]) for i in range(RA)]
    raww = [at(f"raww_{i}", 186 + 4 * i, [P, 4, 256]) for i in range(RW_)]
    st0h = [at(f"st0h_{i}", 170 + 8 * i, [P, 4, 256], F32R) for i in range(2)]
    st0l = [at(f"st0l_{i}", 174 + 8 * i, [P, 4, 256], F32R) for i in range(2)]
    QF = at("QF", 58, [P, HEADS, SEQ])
    KF = at("KF", 74, [P, HEADS, KEYS])
    VF = at("VF", 98, [P, KT, D])
    COS = at("COS", 198, [P, SEQ])
    SIN = at("SIN", 200, [P, SEQ])
    QT = at("QT", 202, [P, KEYS])
    RT = at("RT", 205, [P, SEQ])
    ADS = small("ADS", [P, SEQ])
    QP = [at(f"QP{i}", 122 + 16 * i, [P, 2, SEQ], F32R) for i in range(2)]
    KA = [at(f"KA{i}", 126 + 16 * i, [P, 2, KEYS], F32R) for i in range(2)]
    KB_ = [at(f"KB{i}", 132 + 16 * i, [P, 2, KEYS], F32R) for i in range(2)]
    AT = [at(f"AT{i}", 154 + 3 * i, [P, KT, P]) for i in range(2)]
    QD = at("QD", 42, [P, 2, SEQ])
    KD = at("KD", 201.5, [P, 2, KEYS])
    E = [at(f"E{i}", 162 + 6 * i, [P, 2, KEYS]) for i in range(4)]
    OSQ = [at(f"OSQ{i}", (160, 201)[i], [P, P]) for i in range(2)]
    VB = [at(f"VB{i}", (46, 198)[i], [P, KT, P]) for i in range(2)]
    OF = at("OF", 26, [P, HEADS, SEQ])
    DGA = [at("DGA0", 42, [P, TT, P]), at("DGA1", 44, [P, TT, P])]
    OHh = at("OHh", 122, [P, HEADS, SEQ], F32R)
    OHl = at("OHl", 138, [P, HEADS, SEQ], F32R)
    rawo = [at(f"rawo_{i}", (50, 54, 186, 190, 194, 50, 54, 186)[i], [P, 2, 512]) for i in range(8)]
    stoh = [at(f"stoh_{i}", 162 - 8 * i, [P, 2, 512], F32R) for i in range(2)]
    stol = [at(f"stol_{i}", 166 - 8 * i, [P, 2, 512], F32R) for i in range(2)]
    WR = 8
    ring = [at(f"ring_{i}", 26 + 16 * i, [P, 4, D]) for i in range(WR)]
    XTM = at("XTM", 154, [P, TT, D])
    SQ = at("SQ", 170, [P, DT, SEQ])
    SUMC = at("SUMC", 186, [P, SEQ])
    LOGC = at("LOGC", 188, [P, SEQ])
    adap = [at(f"adap_{i}", (190, 194, 198, 174)[i], [P, 1024]) for i in range(4)]
    rw_pad = at("rw_pad", 206, [P, DT, 32])
    WK = at("WK", 202, [NE, SEQ])
    MKT = at("MKT", 204, [NE, SEQ])
    XS = at("XS", 170, [P, DT, P])
    OH = at("OH", 178, [P, TT, P])
    SM = at("SM", 180, [P, SEQ], F32R)
    SG = at("SG", 182, [P, SEQ])
    HID = at("HID", 184, [P, SEQ])
    HIDT = at("HIDT", 186, [P, TT, P])
    YS = at("YS", 188, [P, D])
    YH = at("YH", 192, [P, D], F32R)
    YL = at("YL", 196, [P, D], F32R)
    H1h = at("H1h", 26, [P, DT, SEQ], F32R)
    H1l = at("H1l", 42, [P, DT, SEQ], F32R)
    U1 = at("U1", 58, [P, DT, SEQ])
    SQ1 = at("SQ1", 78, [P, DT, SEQ])
    DG1 = at("DG1", 94, [P, TT, P])
    ROWG = at("ROWG", 96, [P, SEQ])
    RW1 = at("RW1", 58, [P, TT, D])
    WSR = at("WSR", 74, [P, GROUPS, P])
    UT = at("UT", 90, [P, 4, SEQ])
    WST = at("WST", 98, [P, GROUPS, P])
    BSB = at("BSB", 102, [P, GROUPS, P])
    stgh = [at(f"stgh_{i}", 106 + 8 * i, [P, 2, 512], F32R) for i in range(2)]
    stgl = [at(f"stgl_{i}", 110 + 8 * i, [P, 2, 512], F32R) for i in range(2)]
    V1 = at("V1", 122, [P, 16, TT, P])
    GH = at("GH", 122, [P, 16, SEQ], F32R)
    GL = at("GL", 154, [P, 16, SEQ], F32R)
    RAWG = 4
    rawg = [at(f"rawg_{i}", 186 + 4 * i, [P, 2, 512]) for i in range(RAWG)]
    VT = at("VT", 202, [P, 512])
    GT = at("GT", 204, [P, 512])
    FG = at("FG", 26, [P, DT, SEQ])
    FO = at("FO", 42, [P, TT, D])
    FSQ = at("FSQ", 58, [P, DT, SEQ])
    ROWF = at("ROWF", 74, [P, SEQ])

    bank = [ctx.enter_context(nc.psum_tensor(f"bank{i}", [P, 512], F32)) for i in range(2)]
    sc_a = ctx.enter_context(nc.psum_tensor("sc_a", [P, 1536], F32))
    sc_b = ctx.enter_context(nc.psum_tensor("sc_b", [P, 1536], F32))
    SCP = [sc_a, sc_b]
    PB = [bank[0][:, :], bank[1][:, :]] + [s[:, 512 * i:512 * i + 512] for s in SCP for i in range(3)]

    s_small = sem("small_loads_landed")
    s_later = sem("later_small_loads_landed")
    s_xload = sem("x_landed")
    s_cload = sem("ctx_landed")
    s_unit = sem("streams_normed")
    s_const = sem("constants_ready")
    s_rowT = sem("rows_transposed")
    s_ct = sem("columns_copied")
    s_silu = sem("silu_c_ready")
    s_xtT = sem("stream_blocks_transposed")
    s_xtc = sem("stream_blocks_copied")
    s_aland = [sem(f"ada_landed_{i}") for i in range(RA)]
    s_wland = [sem(f"w_landed_{i}") for i in range(RW_)]
    s_ada = sem("ada_piece_used")
    s_ads = sem("ada_sums_copied")
    s_adt = sem("ada_sums_transposed")
    s_mod = sem("modulation_ready")
    s_coef = sem("norm_coefficients_ready")
    s_dve = sem("vector_chain")
    s_act = sem("scalar_chain")

    class Norm:

        TOTAL = dict(squares=DT, parts=1, copied=1, sums=1, diag=1, spread=1, scaled=DT, hi=DT, lo=DT)
        sems = {k: sem(f"norm_{k}") for k in TOTAL}

        def __init__(self, before, applied_before):
            self.before, self.applied_before = before, applied_before

        def __getitem__(self, name):
            return self.sems[name]

        def __call__(self, name, n):
            summed = name in ("squares", "sums")
            return self.sems[name], n + self.TOTAL[name] * (self.before if summed else self.applied_before)

    nx, nc_, nm0, ng, nm1, nf = Norm(0, 0), Norm(1, 1), Norm(2, 2), Norm(3, 2), Norm(4, 3), Norm(5, 3)
    s_hi = sem("w_hi_ready")
    s_lo = sem("w_lo_ready")
    s_pw = sem("w_piece_used")
    s_evq = sem("q_sums_copied")
    s_evk = sem("k_sums_copied")
    s_evv = sem("v_sums_copied")
    s_shuf = sem("rope_halves_swapped")
    s_sin = sem("rope_sine_applied")
    s_cos = sem("rope_cosine_applied")
    s_rope = sem("rope_done")
    s_gel = sem("v_activated")
    s_lam = sem("lambda_exponentials_ready")
    s_lamr = sem("lambda_sums_ready")

    def need(eng, s, n):
        if not isinstance(n, int) or n > 0:
            eng.wait_ge(s, n)

    class Chain:

        def __init__(self, eng, s):
            self.eng, self.s, self.n = eng, s, 0

        def link(self, ins):
            ins.then_inc(self.s, 1)
            self.n = self.n + 1
            self.eng.wait_ge(self.s, self.n)

    HEAD_PIECES = 16
    STEP = []
    for n, extra in enumerate((3, 3, 3, 3, 4, 0)):
        STEP.append(("w", n // 2, n % 2))
        done = sum(kind == "a" for kind, _, _ in STEP)
        STEP += [("a", done + j, 0) for j in range(extra)]

    SMALL_LOADS = []
    for r0, name in ((R_C, "c"), (R_CC, "c_ctx"), (R_MIX, "mixer_norm_g"), (R_MOE, "moe_norm_g"), (R_FIN, "final_norm_g"),
                     (R_SUB, "da_subln_g"), (R_VG, "gm_v_g")):
        src = t[name] if len(t[name].shape) == 1 else t[name].rearrange("a n -> (a n)")
        rows = src.rearrange("(r p) -> r p", p=P)
        SMALL_LOADS.append((ROWS1[r0:r0 + rows.shape[0], :], rows))
    SMALL_LOADS.append((ROWS2[:, :], t["ada_b"].rearrange("a n -> (a n)").rearrange("(r p) -> r p", p=P)))
    SMALL_LOADS += [(ident[:, :], t["shape_constants"][:, 1024:1152]), (TRI0[:, :], t["shape_constants"][:, 1152:1280]),
                    (select[:, :], t["shape_constants"][:, 1344:1376])]
    LATER_LOADS = [(slots[:, :], t["shape_constants"][:, 1280:1344]), (COS[:, :], t["shape_constants"][:, 0:512]),
                   (SIN[:, :], t["shape_constants"][:, 512:1024])]
    LATER_LOADS += [(rw[:, i, :, :], t["router_w"][i].rearrange("(a p) n -> p a n", p=P)) for i in range(2)]
    LATER_LOADS += [(lam4[:, i, :], t[name].partition_broadcast(P).rearrange("p a n -> p (a n)"))
                    for i, name in enumerate(("da_lambda_q1", "da_lambda_k1", "da_lambda_q2", "da_lambda_k2"))]
    SMALL, LATER = 16 * len(SMALL_LOADS), 16 * len(LATER_LOADS)

    def three(out_, wh, wl, xh, xl, first, last, **kw):
        nc.tensor.matmul(out_, wh, xh, start=first, stop=False, **kw)
        nc.tensor.matmul(out_, wh, xl, start=False, stop=False, **kw)
        return nc.tensor.matmul(out_, wl, xh, start=False, stop=last, **kw)

    def pe_sums(pe, N, sq, rows):
        for d in range(DT):
            pe.wait_ge(*N("squares", d + 1))
            g = d % 4 * 32
            mm = nc.tensor.matmul(rows[g:g + 32, 0:sq.shape[2]], ones[:, 0:32], sq[:, d, :], start=(d < 4),
                                  stop=(d >= 4))
        mm.then_inc(N["parts"], 1)

    def pe_sums_by_token(pe, N, rows, out_):
        pe.wait_ge(*N("copied", 1))
        for i in range(rows.shape[1] // P):
            mm = nc.tensor.matmul(out_[:, i:i + 1], rows[:, i * P:i * P + P], select[:, 0:1], start=True, stop=True,
                                  skip_group_check=True)
        mm.then_inc(N["sums"], 1)

    def dve_copy_sums(dve, N, bank_, rows):
        dve.wait_ge(*N("parts", 1))
        nc.vector.tensor_copy(rows[:, :], bank_[:, 0:rows.shape[1]]).then_inc(N["copied"], 1)

    def pe_spread(pe, done, dg, acc, n):
        for i in range(n):
            mm = nc.tensor.matmul(acc[:, i * P:(i + 1) * P], ones[:, :], dg[:, i, :], start=True, stop=True)
        mm.then_inc(done, 1)

    def rsqrt(ch, sums, n, scale):
        v, y, a = nv[:, 0:n], ny[:, 0:n], na[:, 0:n]
        ch.link(nc.vector.tensor_scalar(v, sums, scale, EPS, ALU.mult, ALU.add))
        ch.link(nc.vector.tensor_scalar(y.bitcast(I32), v.bitcast(I32), 1, None, ALU.logical_shift_right))
        ch.link(nc.vector.tensor_scalar(y.bitcast(I32), y.bitcast(I32), -1.0, float(0x5F3759DF), ALU.mult, ALU.add))
        for _ in range(3):
            ch.link(nc.vector.tensor_tensor(a, y, y, ALU.mult))
            ch.link(nc.vector.scalar_tensor_tensor(a, a, -0.5, v, ALU.mult, ALU.mult))
            ch.link(nc.vector.scalar_tensor_tensor(y, a, 1.5, y, ALU.add, ALU.mult))

    def diagonal(dg, n, done, first=0):
        for i in range(n):
            y = ny[:, first + i:first + i + 1]
            ins = nc.vector.tensor_scalar(dg[:, i, :], ident[:, :], y, None, ALU.mult)
        ins.then_inc(done, 1)

    def act_squares(act, N, src, sq, tokens, ready=None):
        for d in range(DT):
            if ready is not None:
                act.wait_ge(ready[0], ready[1](d))
            nc.scalar.activation(sq[:, d, 0:tokens], src[:, d, 0:tokens], ACT.Square).then_inc(N["squares"], 1)

    def sp_projections(sp):
        sp.dma_start(XR[:, :, :], t["x"][0].rearrange("(a p) n -> p a n", p=P)).then_inc(s_xload, 16)
        sp.dma_start(CR[:, :, :], t["ctx"][0].rearrange("(a p) n -> p a n", p=P)).then_inc(s_cload, 16)

        sp.wait_ge(s_cload, 16)
        for m in range(16):
            if m >= RA:
                sp.wait_ge(s_ada, m - RA + 1)
            c0 = m % 2 * 1024
            sp.dma_start(rawa[m % RA][:, :], t["ada_w"][0, m // 2 * P:m // 2 * P + P, c0:c0 + 1024]).then_inc(
                s_aland[m % RA], 16)
        with sp.Fori(0, 2) as body:
            for step in range(2):
                for kind, m, half in STEP:
                    if kind == "w":
                        k = step * 6 + m * 2 + half
                        sp.wait_ge(s_lo, body * 12 + (k + 1))
                        src = t["da_w_in"][0, half * 512:half * 512 + 512, :].rearrange("(a p) n -> p a n", p=P)
                        sp.dma_start(raww[k % RW_][:, :, :], src[:, :, bass.ds(body * 512 + (m * D + step * 256), 256)]
                                     ).then_inc(s_wland[k % RW_], 16)
                    else:
                        k = step * 16 + m
                        sp.wait_ge(s_ada, body * 32 + (HEAD_PIECES + k - RA + 1))
                        kt, c0 = m // 2, (step + 1) * 2048 + m % 2 * 1024
                        src = t["ada_w"][bass.ds(body, 1), kt * P:(kt + 1) * P, c0:c0 + 1024]
                        sp.dma_start(rawa[k % RA][:, :], src.rearrange("a p n -> p (a n)")).then_inc(
                            s_aland[k % RA], 16)

    def pe_ada(pe, piece, m, landed, bank_=PB[7]):
        pe.wait_ge(*landed)
        for j in range(2):
            g = 2 * (m % 2) + j
            mm = nc.tensor.matmul(bank_[32 * g:32 * g + 32, :], silu_c[:, m // 2, :], piece[:, 512 * j:512 * j + 512],
                                  start=(m < 2), stop=(m >= 14))
        mm.then_inc(s_ada, 1)

    def pe_ada_columns(pe, n, bank_=PB[7]):
        pe.wait_ge(s_ads, n + 1)
        for b in range(4):
            mm = nc.tensor.transpose(bank_[:, b * P:(b + 1) * P], ADS[:, b * P:(b + 1) * P], ident[:, :])
        mm.then_inc(s_adt, 1)

    def pe_head(pe):
        pe.wait_ge(s_small, SMALL)
        pe.wait_ge(s_const, 3)
        nc.tensor.transpose(PB[0][:, 0:R_N], ROWS1[:, :], ident[0:R_N, 0:R_N]).then_inc(s_rowT, 1)
        nc.tensor.transpose(PB[1][:, 0:96], ROWS2[:, :], ident[0:96, 0:96]).then_inc(s_rowT, 1)
        pe.wait_ge(s_ct, 2)
        pe.wait_ge(s_xload, 16)
        for n in range(12):
            if n == 8:
                pe.wait_ge(s_cload, 16)
            if n >= 4:
                pe.wait_ge(s_xtc, n - 3)
            for j in range(4):
                c = (n - 8) * 2 + j // 2
                src = XR[:, j, n * P:(n + 1) * P] if n < 8 else CR[:, j % 2, c * P:c * P + P]
                mm = nc.tensor.transpose(PB[n % 4][:, j * P:(j + 1) * P], src, ident[:, :])
            mm.then_inc(s_xtT, 1)
        pe.wait_ge(s_silu, 2)
        for n in range(16):
            if n == 0:
                pe_sums(pe, nx, SQ0, PB[5])
            if n == 0:
                pe_sums(pe, nc_, SQC, PB[6])
            pe_ada(pe, rawa[n % RA], n, (s_aland[n % RA], (n // RA + 1) * 16))
            if n == 0:
                pe_sums_by_token(pe, nx, ROWX, PB[4])
                pe_sums_by_token(pe, nc_, ROWC, PB[4][:, TT:])
            if n == 3:
                pe.wait_ge(*nx("diag", 1))
                pe_spread(pe, nx["spread"], DG0, PB[0], TT)
                pe.wait_ge(*nc_("diag", 1))
                pe_spread(pe, nc_["spread"], DGC, PB[3], CT)
        pe_ada_columns(pe, 0)

    def pe_projections(pe):
        with pe.Fori(0, 2) as body:
            for step in range(2):
                for kind, m, half in STEP:
                    if kind == "a":
                        k = step * 16 + m
                        if m == 0:
                            pe.wait_ge(s_mod, body * 2 + (step + 1))
                        pe_ada(pe, rawa[k % RA], m, (s_aland[k % RA], body * 64 + (HEAD_PIECES // RA + k // RA + 1) * 16))
                        continue
                    k = step * 6 + m * 2 + half
                    wh, wl = st0h[k % 2], st0l[k % 2]
                    pe.wait_ge(s_lo, body * 12 + (RW_ + k + 1))
                    for j in range(4):
                        kt, first, last = half * 4 + j, half == 0 and j == 0, half == 1 and j == 3
                        if m == 0:
                            pe.wait_ge(*nx("lo", kt + 1))
                            for h in range(2):
                                if first:
                                    pe.wait_ge(s_evv, body * 6 + (step * 3 + 2 + h))
                                w = slice(h * P, h * P + P)
                                mm = three(PB[h], wh[:, j, w], wl[:, j, w], H0h[:, kt, CTX:], H0l[:, kt, CTX:],
                                           first, last)
                        elif m == 1:
                            pe.wait_ge(*nc_("lo", kt + 1))
                            for h in range(2):
                                if first:
                                    pe.wait_ge(s_evk, body * 4 + (step * 2 + 1 + h))
                                w = slice(h * P, h * P + P)
                                for i in range(2):
                                    c = slice(i * 384, i * 384 + 384)
                                    mm = three(PB[2 + 2 * h + i][:, 0:384], wh[:, j, w], wl[:, j, w], H0h[:, kt, c],
                                               H0l[:, kt, c], first, last)
                        else:
                            for i in range(KT):
                                if first and i == 0:
                                    pe.wait_ge(s_evv, body * 6 + (step * 3 + 1))
                                if first and i in (2, 4):
                                    pe.wait_ge(s_evq, body * 4 + (step * 2 + i // 2))
                                c = slice(i * P, i * P + P)
                                mm = three(PB[(6, 0, 1)[i // 2]][:, i % 2 * 256:i % 2 * 256 + 256], H0h[:, kt, c],
                                           H0l[:, kt, c], wh[:, j, :], wl[:, j, :], first and i % 2 == 0, last,
                                           skip_group_check=True)
                    mm.then_inc(s_pw, 1)
                pe_ada_columns(pe, body * 2 + (step + 1))

    def act_weights_hi(act, body, k):
        act.wait_ge(s_wland[k % RW_], body * 64 + (k // RW_ + 1) * 16)
        act.wait_ge(s_pw, body * 12 + (k + 1))
        nc.scalar.activation(st0h[k % 2][:, :, :], raww[k % RW_][:, :, :], ACT.Copy).then_inc(s_hi, 1)

    def act_head(act):
        for dst, src in SMALL_LOADS:
            act.dma_start(dst, src).then_inc(s_small, 16)
        for dst, src in LATER_LOADS:
            act.dma_start(dst, src).then_inc(s_later, 16)
        act.wait_ge(s_rowT, 1)
        nc.scalar.activation(CT1[:, :], PB[0][:, 0:R_N], ACT.Copy).then_inc(s_ct, 1)
        act.wait_ge(s_rowT, 2)
        nc.scalar.activation(CT2[:, :], PB[1][:, 0:96], ACT.Copy).then_inc(s_ct, 1)
        act.wait_ge(s_const, 3)
        act.wait_ge(s_ct, 1)
        for r in range(2):
            nc.scalar.activation(silu_c[:, :, r], CT1[:, 8 * r:8 * r + 8], ACT.Silu).then_inc(s_silu, 1)
        act_squares(act, nx, XT, SQ0, SEQ, (s_xtc, lambda d: d + 1))
        act_squares(act, nc_, CXT, SQC, CTX, (s_xtc, lambda d: 9 + d // 2))
        act.wait_ge(s_lamr, 1)
        nc.scalar.activation(lam_s[:, 2:4], lam_s[:, 0:2], ACT.Exp).then_inc(s_lam, 1)
        act.wait_ge(s_ada, 16)
        nc.scalar.activation(ADS[:, :], PB[7], ACT.Copy).then_inc(s_ads, 1)
        act_weights_hi(act, 0, 0)
        for d in range(DT):
            act.wait_ge(*nx("scaled", d + 1))
            nc.scalar.activation(H0h[:, d, CTX:], U0[:, d, :], ACT.Copy).then_inc(nx["hi"], 1)
            if d == 3:
                act_weights_hi(act, 0, 1)

    def act_projections(act):
        def copy_sums(body, k, r, banks, width, done):
            for i, b in enumerate(banks):
                if i == 0:
                    act.wait_ge(s_pw, body * 12 + (k + 3))
                    act.wait_ge(s_shuf, body * 8 + (r + 1))
                ins = nc.scalar.activation(QT[:, i * width:i * width + width], PB[b][:, 0:width], ACT.Copy)
            ins.then_inc(done, 1)

        for body in range(2):
            for step in range(2):
                k = step * 6
                for j in range(2 if body == step == 0 else 0, 3):
                    act_weights_hi(act, body, k + j)
                for h in range(2):
                    copy_sums(body, k + 1, step * 4 + h, (h,), SEQ, s_evq)
                for j in range(3, 6):
                    act_weights_hi(act, body, k + j)
                for h in range(2):
                    copy_sums(body, k + 3, step * 4 + 2 + h, (2 + 2 * h, 3 + 2 * h), 384, s_evk)
                act.wait_ge(s_ada, body * 32 + (HEAD_PIECES + 16 * (step + 1)))
                nc.scalar.activation(ADS[:, :], PB[7], ACT.Copy).then_inc(s_ads, 1)

    def dve_modulation(dst, r, bias, bank_=PB[7]):
        src = bank_.rearrange("p (b g r) -> p g b r", b=4, g=4)[:, :, :, r]
        return nc.vector.tensor_tensor(dst.rearrange("p (g b) -> p g b", g=4), src,
                                       bias.rearrange("p (g b) -> p g b", g=4), ALU.add)

    def dve_coef(ch, n, scale_cols, gain_cols):
        ch.link(nc.vector.scalar_tensor_tensor(coef[:, n, :], scale_cols, 1.0, gain_cols, ALU.add, ALU.mult))

    def dve_head(dve, ch):
        dve.wait_ge(s_small, SMALL)
        nc.vector.tensor_copy(tri[:, :], TRI0[:, :]).then_inc(s_const, 1)
        for n in range(12):
            dve.wait_ge(s_xtT, n + 1)
            dst = XT[:, n, :] if n < 8 else CXT[:, 2 * (n - 8):2 * (n - 8) + 2, :].rearrange("p a n -> p (a n)")
            nc.vector.tensor_copy(dst, PB[n % 4]).then_inc(s_xtc, 1)
        dve.wait_ge(s_ct, 2)
        ch.link(nc.vector.tensor_scalar(subg[:, :], CT1[:, R_SUB:R_SUB + 1], SUB_SCALE, None, ALU.mult))
        dve_copy_sums(dve, nx, PB[5], ROWX)
        dve_copy_sums(dve, nc_, PB[6], ROWC)
        dve.wait_ge(*nc_("sums", 1))
        rsqrt(ch, PB[4][:, 0:TT + CT], TT + CT, 1.0 / D)
        diagonal(DG0, TT, nx["diag"])
        diagonal(DGC, CT, nc_["diag"], TT)
        dve.wait_ge(s_later, LATER)
        ch.link(nc.vector.tensor_tensor(lam4[:, 0:4:2, :], lam4[:, 0:4:2, :], lam4[:, 1:4:2, :], ALU.mult))
        nc.vector.tensor_reduce(lam_s[:, 0:2], lam4[:, 0:4:2, :], AX.X, ALU.add).then_inc(s_lamr, 1)
        for N, src, u, b in ((nx, XT, U0, 0), (nc_, CXT, UC0, 3)):
            dve.wait_ge(*N("spread", 1))
            for d in range(DT):
                nc.vector.tensor_tensor(u[:, d, :], src[:, d, :], PB[b][:, 0:u.shape[2]], ALU.mult).then_inc(s_unit, 1)
        dve.wait_ge(s_lam, 1)
        ch.link(nc.vector.scalar_tensor_tensor(neg_lam[:, :], lam_s[:, 3:4], -LAM_INIT, lam_s[:, 2:3], ALU.add,
                                               ALU.subtract))
        dve.wait_ge(s_adt, 1)
        dve_modulation(MODC[:, :], 1, CT2[:, 0:16])
        ch.link(dve_modulation(MOD[:, 0, 0:16], 0, CT2[:, 0:16]))
        dve_coef(ch, 0, MOD[:, 0, 8:16], CT1[:, R_MIX:R_MIX + 8])
        nc.vector.scalar_tensor_tensor(coef[:, 1, :], MODC[:, 8:16], 1.0, CT1[:, R_MIX:R_MIX + 8], ALU.add,
                                       ALU.mult).then_inc(s_mod, 1)
        dve.wait_ge(s_mod, 1)
        dve.wait_ge(s_unit, 2 * DT)
        for N, u, n, c0, B in ((nx, U0, 0, CTX, MOD[:, 0, :]), (nc_, UC0, 1, 0, MODC[:, :])):
            for d in range(DT + 1):
                c = slice(c0, c0 + u.shape[2])
                if d < DT:
                    nc.vector.tensor_scalar(u[:, d, :], u[:, d, :], coef[:, n, d:d + 1], B[:, d:d + 1], ALU.mult,
                                            ALU.add).then_inc(N["scaled"], 1)
                if d < DT and N is nc_:
                    dve.wait_ge(*N("scaled", d + 1))
                    nc.vector.tensor_copy(H0h[:, d, c], u[:, d, :]).then_inc(N["hi"], 1)
                if d > 0:
                    dve.wait_ge(*N("hi", d))
                    nc.vector.tensor_tensor(H0l[:, d - 1, c], u[:, d - 1, :], H0h[:, d - 1, c], ALU.subtract).then_inc(
                        N["lo"], 1)

    def dve_projections(dve):
        with dve.Fori(0, 2) as body:
            for step in range(2):
                for r in range(4):
                    kind, h = r // 2, r % 2
                    idx = step * 4 + r
                    dve.wait_ge((s_evq, s_evk)[kind], body * 4 + (kind * 2 + step * 2 + h + 1))
                    dve.wait_ge(s_rope, body * 8 + (idx + 1))
                    lat = QT[:, 0:SEQ] if kind == 0 else QT[:, CTX:]
                    head = bass.ds(body * 4 + (step * 2 + h), 1)
                    if kind == 0:
                        dst = QF[:, head, :].rearrange("p a n -> p (a n)")
                    else:
                        dst = KF[:, head, CTX:].rearrange("p a n -> p (a n)")
                        nc.vector.tensor_scalar(KF[:, head, 0:CTX].rearrange("p a n -> p (a n)"), QT[:, 0:CTX], 1.0, None,
                                                ALU.mult)
                    nc.vector.tensor_tensor(dst, lat, COS[:, :], ALU.mult).then_inc(s_cos, 1)
                    nc.vector.stream_shuffle(RT[:, :], lat, [(i + 16) % 32 for i in range(32)]).then_inc(s_shuf, 1)
                    dve.wait_ge(s_cos, body * 8 + (idx + 1))
                    dve.wait_ge(s_sin, body * 8 + (idx + 1))
                    nc.vector.tensor_tensor(dst, dst, RT[:, :], ALU.add).then_inc(s_rope, 1)
                dve.wait_ge(s_pw, body * 12 + (step * 6 + 8))
                for i, b in enumerate((6, 0, 1)):
                    dst = VF[:, 2 * i:2 * i + 2, bass.ds(body * 512 + step * 256, 256)]
                    nc.vector.tensor_scalar(dst, PB[b].rearrange("p (a n) -> p a n", a=2), 1.0, None, ALU.mult).then_inc(
                        s_evv, 1)
                dve.wait_ge(s_adt, body * 2 + (step + 2))
                c = (step + 1) * 16
                dst = MOD[:, bass.ds(body, 1), c:c + 16].rearrange("p a n -> p (a n)")
                dve_modulation(dst, 0, CT2[:, bass.ds(body * 48 + c, 16)]).then_inc(s_mod, 1)

    def pool_head(pool):
        nc.gpsimd.memset(ones[:, :], 1.0).then_inc(s_const, 1)
        nc.gpsimd.memset(silu_c[:, :, :], 0.0).then_inc(s_const, 1)
        nc.gpsimd.memset(ones_b[:, 0:32], 1.0).then_inc(s_lo, RW_)
        nc.gpsimd.memset(ones_b[:, 32:64], 1.0).then_inc(s_pw, 2)
        nc.gpsimd.memset(ones_b[:, 64:96], 1.0).then_inc(s_evv, 3)
        nc.gpsimd.memset(ones_b[:, 96:112], 1.0).then_inc(s_evk, 2)
        nc.gpsimd.memset(ones_b[:, 112:120], 1.0).then_inc(s_gel, 8)
        nc.gpsimd.memset(ones_b[:, 120:124], 1.0).then_inc(s_shuf, 1)
        nc.gpsimd.memset(ones_b[:, 124:128], 1.0).then_inc(s_rope, 1)

    def pool_projections(pool):
        def lo(body, k):
            pool.wait_ge(s_hi, body * 12 + (k + 1))
            nc.gpsimd.tensor_tensor(st0l[k % 2][:, :, :], raww[k % RW_][:, :, :], st0h[k % 2][:, :, :],
                                    ALU.subtract).then_inc(s_lo, 1)

        def sine(body, r):
            pool.wait_ge(s_shuf, body * 8 + (r + 2))
            nc.gpsimd.tensor_tensor(RT[:, :], RT[:, :], SIN[:, :], ALU.mult).then_inc(s_sin, 1)

        with pool.Fori(0, 2) as body:
            for step in range(2):
                for j in range(3):
                    lo(body, step * 6 + j)
                for h in range(2):
                    sine(body, step * 4 + h)
                for j in range(3, 6):
                    lo(body, step * 6 + j)
                for h in range(2):
                    sine(body, step * 4 + 2 + h)
    s_dupk = sem("k_on_both_halves")
    s_dupq = sem("q_on_both_halves")
    s_qkh = sem("qk_hi_ready")
    s_qkl = sem("qk_lo_ready")
    s_vb = sem("v_of_head_ready")
    s_sc = sem("scores_ready")
    s_bias = sem("maximum_ready")
    s_exp = sem("exponentials_ready")
    s_rat = sem("ratio_chain")
    s_comb = sem("softmaxes_combined")
    s_tra = sem("keys_0_to_3_transposed")
    s_trb = sem("keys_4_and_5_transposed")
    s_at = sem("transposes_copied")
    s_pv = sem("tile_times_v_ready")
    s_osq = sem("tile_output_copied")
    s_sub = sem("tile_squares_summed")
    PROJ_ADA = HEAD_PIECES + 64
    PROJ_PW = 2 + 24
    PV0 = 256
    SUMS0 = 384
    SLOTS = HEADS * TT

    def over_heads(eng, slot):
        for h in range(2):
            for qt in range(TT):
                slot(0, h, qt)
        with eng.Fori(1, HEADS // 2 - 1) as body:
            for h in range(2):
                for qt in range(TT):
                    slot(body * 2, h, qt)
        for h in range(2):
            for qt in range(TT):
                slot(HEADS - 2, h, qt)
        for qt in range(TT):
            slot(HEADS, 0, qt)

    def due(base, h, qt, late):
        if not isinstance(base, int):
            return True
        s = (base + h) * TT + qt - late
        return 0 <= s < SLOTS

    def begun(base, h, qt, late):
        return not isinstance(base, int) or (base + h) * TT + qt >= late

    def rest_bank(base):
        return PB[3] if isinstance(base, int) and base == HEADS else PB[1]

    def pe_attention(pe):
        pe.wait_ge(s_evv, 3 + 12)
        pe.wait_ge(s_evk, 2 + 4 * 2)
        pe.wait_ge(s_mod, 5)

        def slot(base, h, qt):
            s = base * TT + (TT * h + qt)
            rest = rest_bank(base)
            if qt == 2 and isinstance(base, int) and base == HEADS:
                pe_spread_head(pe, 0)
                pe_spread_head(pe, 1)
            if due(base, h, qt, 0):
                if qt == 0:
                    pe.wait_ge(s_qkl, base * 2 + (2 * h + 2))
                if due(base, h, qt, 2):
                    pe.wait_ge(s_exp, s - 1)
                S = SCP[qt % 2]
                q = slice(qt * P, qt * P + P)
                for j in range(2):
                    for c0, c1 in ((0, 512), (512, 768)) if j == 0 else ((0, 256), (256, 768)):
                        o0 = j * KEYS
                        nc.tensor.matmul(S[:, o0 + c0:o0 + c1], QP[h][:, j, q], KA[h][:, j, c0:c1],
                                         start=(j, c0) != (1, 0), stop=False, skip_group_check=True)
                        mm = nc.tensor.matmul(S[:, o0 + c0:o0 + c1], QP[h][:, j, q], KB_[h][:, j, c0:c1],
                                              start=False, stop=True, skip_group_check=True)
                mm.then_inc(s_sc, 1)
            if due(base, h, qt, 3):
                pe.wait_ge(s_at, s * 2 - 4)
            if due(base, h, qt, 4):
                pe.wait_ge(s_osq, s - 3)
            if due(base, h, qt, 2):
                pe.wait_ge(s_comb, s - 1)
                src = E[(qt - 2) % 4]
                for kt in range(KT):
                    mm = nc.tensor.transpose((PB[0], rest)[kt // 4][:, kt % 4 * P:kt % 4 * P + P], src[:, 0, kt * P:kt * P + P],
                                             ident[:, :])
                    if kt in (3, 5):
                        mm.then_inc((s_tra, s_trb)[kt // 4], 1)
            if due(base, h, qt, 4):
                dst = rest[:, bass.ds(s + (SUMS0 - 4), 1)]
                nc.tensor.matmul(dst, OSQ[qt % 2][:, :], ones[:, 0:1], start=True, stop=True,
                                 skip_group_check=True).then_inc(s_sub, 1)
            if due(base, h, qt, 3):
                if qt == 3:
                    pe.wait_ge(s_vb, base + (h + 1))
                v = VB[h] if qt == 3 else VB[1 - h]
                for kt in range(KT):
                    mm = nc.tensor.matmul(rest[:, PV0:PV0 + P], v[:, kt, :], AT[(qt - 3) % 2][:, kt, :],
                                          start=(kt == 0), stop=(kt == KT - 1), skip_group_check=True)
                mm.then_inc(s_pv, 1)

        over_heads(pe, slot)

    def act_attention(act):
        act.wait_ge(s_pw, PROJ_PW)
        act.wait_ge(s_ada, PROJ_ADA)

        def slot(base, h, qt):
            s = base * TT + (TT * h + qt)
            rest = rest_bank(base)
            if due(base, h, qt, 2):
                if due(base, h, qt, 5):
                    act.wait_ge(s_pv, s - 4)
                act.wait_ge(s_tra, s - 1)
                src = PB[0].rearrange("p (a n) -> p a n", a=4)
                nc.scalar.activation(AT[qt % 2][:, 0:4, :], src, ACT.Copy).then_inc(s_at, 1)
            if due(base, h, qt, 3):
                if due(base, h, qt, 5):
                    act.wait_ge(s_sub, s - 4)
                act.wait_ge(s_pv, s - 2)
            if due(base, h, qt, 2):
                act.wait_ge(s_trb, s - 1)
                src = rest[:, 0:2 * P].rearrange("p (a n) -> p a n", a=2)
                nc.scalar.activation(AT[qt % 2][:, 4:6, :], src, ACT.Copy).then_inc(s_at, 1)
            if due(base, h, qt, 3):
                nc.scalar.activation(OSQ[(qt - 3) % 2][:, :], rest[:, PV0:PV0 + P], ACT.Square)
                q = (qt - 3) % TT
                dst = OF[:, bass.ds(base + (h - (qt < 3)), 1), q * P:q * P + P].rearrange("p a n -> p (a n)")
                nc.scalar.activation(dst, rest[:, PV0:PV0 + P], ACT.Copy).then_inc(s_osq, 1)
            if due(base, h, qt, 0):
                if due(base, h, qt, 4):
                    act.wait_ge(s_trb, s - 3)
                act.wait_ge(s_bias, s + 1)
                for j in range(2):
                    ins = nc.scalar.activation(E[qt][:, j, :], SCP[qt % 2][:, j * KEYS:(j + 1) * KEYS], ACT.Exp,
                                               bias=row_bias[:, qt % 2, j:j + 1], scale=HD ** -0.5,
                                               accum_out=row_sum[:, qt % 2, j:j + 1])
                ins.then_inc(s_exp, 1)
            if qt == 1 and isinstance(base, int) and base == HEADS:
                act.wait_ge(s_trb, SLOTS - 2)
                act_w_out_hi(act, 0)

        over_heads(act, slot)

    def sp_attention(sp):
        def both_halves(h):
            for src, dst, done in ((KF, KD, s_dupk), (QF, QD, s_dupq)):
                for j in range(2):
                    for half in range(2):
                        sp.dma_start(dst[half * HD:half * HD + HD, j, :],
                                     src[j * HD:j * HD + HD, h, :].rearrange("p a n -> p (a n)")).then_inc(done, 16)

        sp.wait_ge(s_rope, 1 + 16)
        sp.wait_ge(s_ada, PROJ_ADA)
        both_halves(slice(0, 1))
        sp_out_projection(sp, range(5))
        with sp.Fori(1, HEADS) as h:
            sp.wait_ge(s_qkl, h * 2)
            both_halves(bass.ds(h, 1))

    def dve_hi(b, n):
        dst, src = ((KA[b], KD), (QP[b], QD))[n]
        nc.vector.tensor_copy(dst[:, :, :], src[:, :, :]).then_inc(s_qkh, 1)

    def dve_attention(dve):
        dve.wait_ge(s_pw, PROJ_PW)
        dve.wait_ge(s_dupk, 64)
        dve_hi(0, 0)
        dve.wait_ge(s_dupq, 64)
        dve_hi(0, 1)
        dve.wait_ge(s_qkh, 2)
        low = QP[0][HD:P, :, :]
        nc.vector.tensor_tensor(low, QD[HD:P, :, :], low, ALU.subtract).then_inc(s_qkl, 1)

        def slot(base, h, qt):
            s = base * TT + (TT * h + qt)
            par = qt % 2
            live = due(base, h, qt, 0)
            if live:
                dve.wait_ge(s_sc, s + 1)
                need(dve, s_bias, s)
                nc.vector.tensor_reduce(row_max[:, :], SCP[par].rearrange("p (j n) -> p j n", j=2), AX.X, ALU.max
                                        ).then_inc(s_rat, 1)
                dve.wait_ge(s_rat, s * 3 - 1 if begun(base, h, qt, 1) else 1)
                nc.vector.tensor_scalar(row_bias[:, par, :], row_max[:, :], -HD ** -0.5, None, ALU.mult).then_inc(
                    s_bias, 1)
            if due(base, h, qt, 1):
                par = 1 - par
                e = E[(qt - 1) % 4]
                dve.wait_ge(s_exp, s)
                if due(base, h, qt, 2):
                    dve.wait_ge(s_comb, s - 1)
                dst = sum_all[:, bass.ds(s - 1, 1)]
                nc.vector.tensor_scalar(dst, row_sum[:, par, 0:1], 1.0, None, ALU.mult)
                nc.vector.reciprocal(row_ratio[:, par, 0:1], row_sum[:, par, 1:2]).then_inc(s_rat, 1)
                dve.wait_ge(s_rat, s * 3 - (0 if live else 1))
                nc.vector.scalar_tensor_tensor(row_ratio[:, par, 1:2], row_ratio[:, par, 0:1], neg_lam[:, :],
                                               row_sum[:, par, 0:1], ALU.mult, ALU.mult).then_inc(s_rat, 1)
                dve.wait_ge(s_rat, s * 3 + (1 if live else 0))
                nc.vector.scalar_tensor_tensor(e[:, 0, :], e[:, 1, :], row_ratio[:, par, 1:2], e[:, 0, :], ALU.mult,
                                               ALU.add).then_inc(s_comb, 1)
            if qt < 2 and due(base, h, qt, -TT):
                dve.wait_ge((s_dupk, s_dupq)[qt], base * 64 + (h + 2) * 64)
                need(dve, s_qkl, base * 2 + 2 * h)
                dve_hi(1 - h, qt)

        over_heads(dve, slot)

    def pool_attention(pool):
        pool.wait_ge(s_pw, PROJ_PW)
        pool.wait_ge(s_sin, 16)

        def lo(count, b):
            pool.wait_ge(s_qkh, count + 1)
            nc.gpsimd.tensor_tensor(KB_[b][:, :, :], KD[:, :, :], KA[b][:, :, :], ALU.subtract).then_inc(s_qkl, 1)
            pool.wait_ge(s_qkh, count + 2)
            pool.wait_ge(s_qkl, count + 1)
            low = QP[b][HD:P, :, :]
            nc.gpsimd.tensor_tensor(low, QD[HD:P, :, :], low, ALU.subtract).then_inc(s_qkl, 1)
            pool.wait_ge(s_qkl, count + 2)

        def v_of_head(b, columns, count):
            nc.gpsimd.tensor_copy(VB[b][:, :, :], VF[:, :, columns]).then_inc(s_vb, 1)
            pool.wait_ge(s_vb, count)

        pool.wait_ge(s_qkh, 1)
        nc.gpsimd.tensor_tensor(KB_[0][:, :, :], KD[:, :, :], KA[0][:, :, :], ALU.subtract).then_inc(s_qkl, 1)
        pool.wait_ge(s_qkl, 2)
        pool.wait_ge(s_evv, 3 + 12)
        pool.wait_ge(s_ada, PROJ_ADA)
        v_of_head(0, slice(0, P), 1)
        lo(2, 1)
        v_of_head(1, slice(P, 2 * P), 2)
        with pool.Fori(1, HEADS // 2) as body:
            for h in range(2):
                lo(body * 4 + 2 * h, h)
                pool.wait_ge(s_pv, body * (2 * TT) + (TT * h - TT))
                v_of_head(h, bass.ds(body * (2 * P) + h * P, P), body * 2 + (h + 1))
    s_oland = [sem(f"w_out_landed_{i}") for i in range(8)]
    s_ohi = sem("w_out_hi_ready")
    s_olo = sem("w_out_lo_ready")
    s_opw = sem("w_out_piece_used")
    s_dga = sem("head_factors_on_diagonal")
    s_osp = sem("head_factors_spread")
    s_on = sem("head_output_normed")
    s_ohh = sem("head_output_hi_ready")
    s_ohl = sem("head_output_lo_ready")
    s_xo = sem("attention_added_to_stream")

    def split_piece(act, n, src, hi, landed, used, done):
        act.wait_ge(*landed)
        if n >= 2:
            act.wait_ge(used, n - 1)
        nc.scalar.activation(hi, src, ACT.Copy).then_inc(done, 1)

    def sp_out_projection(sp, pieces):
        for n in pieces:
            if n == 0:
                sp.wait_ge(s_ada, PROJ_ADA)
                sp.wait_ge(s_lo, RW_ + 24)
                sp.wait_ge(s_rope, 1 + 16)
            if n > 4:
                sp.wait_ge(s_olo, n - 4)
            src = t["da_w_out"][0, n % 4 * 256:n % 4 * 256 + 256, n // 4 * 512:n // 4 * 512 + 512]
            sp.dma_start(rawo[n][:, :, :], src.rearrange("(a p) n -> p a n", p=P)).then_inc(s_oland[n], 16)

    SPREAD = (PB[2], PB[1])

    def pe_spread_head(pe, h):
        pe.wait_ge(s_dga, h + 1)
        if h >= 2:
            pe.wait_ge(s_on, h - 1)
        pe_spread(pe, s_osp, DGA[h % 2], SPREAD[h % 2], TT)

    def pe_out_projection(pe):
        pe.wait_ge(s_exp, SLOTS)
        for n in range(8):
            chunk, kp = n // 4, n % 4
            pe.wait_ge(s_olo, n + 1)
            if n == 4:
                pe.wait_ge(s_on, HEADS)
            for j in range(2):
                kt = 2 * kp + j
                if chunk == 0:
                    pe.wait_ge(s_ohl, kt + 1)
                for m in range(4):
                    w = slice(m * P, m * P + P)
                    mm = three(PB[4 * (1 - chunk) + m], stoh[n % 2][:, j, w], stol[n % 2][:, j, w], OHh[:, kt, :],
                               OHl[:, kt, :], kt == 0, kt == HEADS - 1)
                if chunk == 0 and kt + 2 < HEADS:
                    if j == 1:
                        mm.then_inc(s_opw, 1)
                    pe_spread_head(pe, kt + 2)
                elif j == 1:
                    mm.then_inc(s_opw, 1)

    def act_w_out_hi(act, n):
        split_piece(act, n, rawo[n][:, :, :], stoh[n % 2][:, :, :], (s_oland[n], 16), s_opw, s_ohi)

    def act_out_projection(act):
        for h in range(HEADS):
            act.wait_ge(s_on, h + 1)
            nc.scalar.activation(OHh[:, h, :], OF[:, h, :], ACT.Copy).then_inc(s_ohh, 1)
            if h == 1:
                act.wait_ge(s_sub, SLOTS)
                act_w_out_hi(act, 1)
            if h in (3, 5):
                act_w_out_hi(act, 2 + (h - 3) // 2)
        for n in range(4, 8):
            act_w_out_hi(act, n)

    def pool_out_projection(pool):
        for n in range(8):
            pool.wait_ge(s_ohi, n + 1)
            nc.gpsimd.tensor_tensor(stol[n % 2][:, :, :], rawo[n][:, :, :], stoh[n % 2][:, :, :],
                                    ALU.subtract).then_inc(s_olo, 1)

    def dve_out_projection(dve, ch):
        dve.wait_ge(s_comb, SLOTS)

        def factors(a, b, bank_):
            c = sum_all[:, a:b]
            dve.wait_ge(s_sub, b)
            ch.link(nc.vector.reciprocal(c, c))
            ch.link(nc.vector.tensor_tensor(fv[:, 0:b - a], bank_[:, SUMS0 + a:SUMS0 + b], c, ALU.mult))
            ch.link(nc.vector.tensor_tensor(fv[:, 0:b - a], fv[:, 0:b - a], c, ALU.mult))
            rsqrt(ch, fv[:, 0:b - a], b - a, 1.0 / P)
            ch.link(nc.vector.tensor_tensor(head_f[:, a:b], ny[:, 0:b - a], c, ALU.mult))

        done = SLOTS - 4
        dve.wait_ge(s_osq, done + 1)
        factors(0, done, PB[1])

        def diag(h):
            if h >= 2:
                dve.wait_ge(s_osp, h - 1)
            for i in range(TT):
                ins = nc.vector.tensor_scalar(DGA[h % 2][:, i, :], ident[:, :], head_f[:, TT * h + i:TT * h + i + 1], None,
                                              ALU.mult)
            ins.then_inc(s_dga, 1)

        diag(0)
        diag(1)
        for h in range(HEADS):
            dve.wait_ge(s_osq, TT * (h + 1))
            if h == 4:
                factors(done, SLOTS, PB[3])
            dve.wait_ge(s_osp, h + 1)
            nc.vector.scalar_tensor_tensor(OF[:, h, :], OF[:, h, :], subg[:, :], SPREAD[h % 2], ALU.mult,
                                           ALU.mult).then_inc(s_on, 1)
            if h + 2 < HEADS:
                diag(h + 2)
            dve.wait_ge(s_ohh, h + 1)
            nc.vector.tensor_tensor(OHl[:, h, :], OF[:, h, :], OHh[:, h, :], ALU.subtract).then_inc(s_ohl, 1)
        dve_router_weights(ch, 0)
        dve_add_to_stream(dve, s_opw, 0, 16, (4, 0), s_xo)

    def dve_add_to_stream(dve, used, layer, gate, banks, done):
        for d in range(DT):
            if d % 4 == 0:
                dve.wait_ge(used, 4 * (d // 4 + 1))
            g = MOD[:, layer, gate + d:gate + d + 1]
            nc.vector.scalar_tensor_tensor(XT[:, d, :], PB[banks[d // 4] + d % 4], g, XT[:, d, :], ALU.mult,
                                           ALU.add).then_inc(done, 1)
    PAIRS = NE // 2
    PIECES = 12

    class Signals:

        KINDS = dict(
            rwc=("router_weights_ready", 3), fac=("token_factors_ready", 1), soft=("router_softmax_chain", 3), aff=("affinities_ready", 1),
            afft=("affinities_turned", 1), wk=("affinities_by_expert", 1), mask=("chosen_ready", 1),
            maskt=("chosen_turned", 1), mb=("chosen_in_bf16", 1), rank=("ranks_summed", 1),
            hb=("token_blocks_turned", 2 * TT), tm=("token_blocks_ready", 2 * TT), parts=("row_parts_summed", 1),
            pc0=("square_sums_copied", 1), pc1=("logit_parts_copied", 1), oh=("one_hots_ready", PAIRS),
            smt=("one_hots_turned", PAIRS), sm=("one_hots_by_slot_ready", PAIRS), afm=("slot_affinities_summed", PAIRS),
            afc=("slot_affinities_ready", PAIRS), gath=("half_of_tokens_features_gathered", 2 * PAIRS),
            xsa=("gathered_first_half_copied", PAIRS), xsb=("gathered_second_half_copied", PAIRS),
            used=("expert_piece_used", PAIRS * PIECES), sg=("silu_ready", NE), hid=("hidden_ready", NE),
            hidm=("hidden_turned", NE), hidt=("hidden_by_feature_ready", NE), ys=("outputs_scaled", 2 * NE),
            yh=("outputs_hi_ready", 2 * PAIRS), yl=("outputs_lo_ready", 2 * PAIRS), sc=("outputs_scattered", PAIRS * DT),
            acc=("outputs_added", PAIRS * DT))
        sems = {k: sem(name) for k, (name, _) in KINDS.items()}
        landed = [sem(f"ring_landed_{i}") for i in range(WR)]

        def __init__(self, layer):
            self.layer = layer

        def __getitem__(self, name):
            return self.landed if name == "land" else self.sems[name]

        def __call__(self, name, n, slot=None):
            if name == "land":
                return self.landed[slot], n + self.layer * (PAIRS * PIECES // WR * 16)
            return self.sems[name], n + self.layer * self.KINDS[name][1]

    ME = [Signals(0), Signals(1)]
    RING = [[ring[i] for i in (2, 3, 4, 5, 0, 1, 6, 7)], ring]
    TURN = 2 * PIECES

    def over_pairs(eng, pair):
        for c in range(2):
            pair(0, c, c == 0, False)
        with eng.Fori(1, PAIRS // 2 - 1) as b:
            for c in range(2):
                pair(b, c, False, False)
        for c in range(2):
            pair(PAIRS // 2 - 1, c, False, c == 1)

    def sp_moe(sp, L, before):
        S = ME[L]

        def load(b, r):
            name = ("moe_w_gate", "moe_w_up", "moe_w_down")[r % 6 // 2]
            src = t[name][L, bass.ds(b * 4 + r // 6, 1), r % 2 * 512:r % 2 * 512 + 512, :]
            sp.dma_start(RING[L][r % WR][:, :, :], src.rearrange("e (a p) n -> p (e a) n", p=P)).then_inc(
                S["land"][r % WR], 16)

        for r in range(WR):
            before(r)
            load(0, r)
        for r in range(WR, TURN):
            sp.wait_ge(*S("used", r - WR + 1))
            load(0, r)
        with sp.Fori(1, PAIRS // 2) as b:
            for r in range(TURN):
                sp.wait_ge(*S("used", b * TURN + (r - WR + 1)))
                load(b, r)

    FREE = [(4, 5, 6, 7, 0, 1, 2, 3), (0, 1, 2, 3, 4, 5, 6, 7)]
    CONST0 = TT * NE
    SUM0 = CONST0 + NE
    BLOCK = (2, 3, 4, 0)

    def sp_last_sweep(sp):
        n = len(adap)
        for m in range(16):
            if m == 0:
                sp.wait_ge(s_olo, 6)
            if m == 3:
                sp.wait_ge(*ME[0]("parts", 1))
            if m >= n:
                sp.wait_ge(s_ada, PROJ_ADA + m - n + 1)
            c0 = m % 2 * 1024
            sp.dma_start(adap[m % n][:, :], t["ada_w"][1, m // 2 * P:m // 2 * P + P, c0:c0 + 1024]).then_inc(
                s_aland[m % n], 16)

    def pe_moe_head(pe, L, N, added):
        S, F = ME[L], FREE[L]
        pe.wait_ge(*S("rwc", 3))
        for d in range(DT):
            pe.wait_ge(added, max(d, 1) + 1)
            g, h = d % 4 * 32, (d + 2) % 4 * 32
            nc.tensor.matmul(PB[F[1]][g:g + 32, :], rw_pad[:, d, :], XT[:, d, :], start=(d < 4), stop=(d >= 4))
            pe.wait_ge(*N("squares", d + 1))
            mm = nc.tensor.matmul(PB[F[0]][h:h + 32, :], ones[:, 0:32], SQ[:, d, :], start=(d < 4), stop=(d >= 4))
        mm.then_inc(S["parts"], 1)
        small = PB[F[5]]
        nc.tensor.matmul(small[:, CONST0:CONST0 + NE], ones[:, :], const_lg[:, :], start=True, stop=True,
                         skip_group_check=True)
        pe.wait_ge(*S("pc0", 1))
        for i in range(TT):
            nc.tensor.matmul(small[:, SUM0 + i:SUM0 + i + 1], SUMC[:, i * P:i * P + P], select[:, 0:1], start=False,
                             stop=True, skip_group_check=True)
        pe.wait_ge(*S("pc1", 1))
        for i in range(TT):
            mm = nc.tensor.matmul(small[:, i * NE:i * NE + NE], LOGC[:, i * P:i * P + P], select[:, 0:NE],
                                  start=False, stop=True, skip_group_check=True)
        mm.then_inc(N["sums"], 1)

        def last_sweep(pieces):
            for m in pieces:
                pe_ada(pe, adap[m % 4], m, (s_aland[m % 4], (PROJ_ADA // RA + m // 4 + 1) * 16), PB[F[7]])

        def tokens(n):
            i, half = n % TT, n // TT
            if n >= 4:
                pe.wait_ge(*S("tm", n - 3))
            for j in range(4):
                mm = nc.tensor.transpose(PB[F[BLOCK[n % 4]]][:, j * P:j * P + P],
                                         XT[:, half * 4 + j, i * P:i * P + P], ident[:, :])
            mm.then_inc(S["hb"], 1)

        if L == 0:
            last_sweep(range(3))
        for n in range(4):
            tokens(n)
        if L == 0:
            last_sweep(range(3, 5))
        pe.wait_ge(*S("aff", 1))
        for i in range(TT):
            mm = nc.tensor.transpose(PB[F[6]][0:NE, i * P:i * P + P], AFF[:, i, :], ident[:, :])
        mm.then_inc(S["afft"], 1)

        for n in range(4, 8):
            if L == 0:
                last_sweep(range(5 + n - 4, 5 + n - 3))
            tokens(n)
        if L == 0:
            last_sweep(range(5 + 4, 13))
        pe.wait_ge(*S("mask", 1))
        for i in range(TT):
            mm = nc.tensor.transpose(PB[F[6]][:, i * NE:i * NE + NE], MKT[:, i * P:i * P + P], ident[0:NE, 0:NE])
        mm.then_inc(S["maskt"], 1)
        if L == 0:
            last_sweep(range(13, 13))
        pe.wait_ge(*S("mb", 1))
        for i in range(TT):
            for j in range(i + 1):
                mm = nc.tensor.matmul(PB[F[5]][:, i * NE:i * NE + NE], tri[:, :] if j == i else ones_b[:, :],
                                      MB[:, j, :], start=(i == 0), stop=(j == i), skip_group_check=True)
        mm.then_inc(S["rank"], 1)
        if L == 0:
            last_sweep(range(13, 16))
        pe.wait_ge(*S("oh", 1))
        pe.wait_ge(*S("tm", 2 * TT))
        pe_gather(S)

    def pe_gather(S):
        for d in range(DT):
            for j in range(TT):
                mm = nc.tensor.matmul(PB[4 + d // 4][:, d % 4 * P:d % 4 * P + P], XTM[:, j, d * P:d * P + P],
                                      OH[:, j, :], start=(d % 4 == 0 and j == 0), stop=(j == TT - 1),
                                      skip_group_check=True)
            if d % 4 == 3:
                mm.then_inc(S["gath"], 1)

    def pe_scatter(pe, S, i):
        for d in range(DT):
            if d % 4 == 0:
                pe.wait_ge(*S("yl", i * 2 - (d == 0)))
            if d == 0:
                pe.wait_ge(*S("afc", i))
            if d >= 2:
                pe.wait_ge(*S("acc", i * DT + (d - DT - 1)))
            w = slice(d * P, d * P + P)
            nc.tensor.matmul(PB[6 + d % 2], YH[:, w], SM[:, :], start=True, stop=False)
            nc.tensor.matmul(PB[6 + d % 2], YL[:, w], SM[:, :], start=False, stop=True).then_inc(S["sc"], 1)

    def pe_moe(pe, L):
        S = ME[L]

        def pair(b, c, first, last):
            i = b * 2 + c
            for a in range(2):
                for m in range(3):
                    if L == 0 and first and a == 0 and m == 1:
                        pe_ada_columns(pe, 5, PB[3])
                    if m == 2:
                        if a == 0:
                            if L == 0 and first:
                                pe.wait_ge(s_mod, 6)
                            if not first:
                                pe_scatter(pe, S, i)
                            for j in range(TT):
                                mm = nc.tensor.transpose(PB[3][:, j * P:j * P + P], OH[:, j, :],
                                                         ident[:, :])
                            mm.then_inc(S["smt"], 1)
                            if not first:
                                pe.wait_ge(*S("acc", i * DT))
                            for e in range(2):
                                for j in range(TT):
                                    for half in range(2):
                                        mm = nc.tensor.matmul(PB[6][half * 64:half * 64 + 64, e * NE:e * NE + NE],
                                                              OH[:, j, e * 64:e * 64 + 64],
                                                              AFF[:, j, :],
                                                              start=(e == 0 and j == 0), stop=(j == TT - 1),
                                                              skip_group_check=True)
                            mm.then_inc(S["afm"], 1)
                            pe.wait_ge(*S("sm", i + 1))
                        elif not last:
                            pe.wait_ge(*S("oh", i + 2))
                            pe.wait_ge(*S("xsa", i + 1))
                            pe.wait_ge(*S("xsb", i + 1))
                            pe_gather(S)
                        pe.wait_ge(*S("hid", i * 2 + (a + 1)))
                        for j in range(4):
                            mm = nc.tensor.transpose(PB[3][:, j * P:j * P + P], HID[:, j * P:j * P + P], ident[:, :])
                        mm.then_inc(S["hidm"], 1)
                        pe.wait_ge(*S("hidt", i * 2 + (a + 1)))
                        if a == 1 or not first:
                            pe.wait_ge(*S("ys", i * 4 + (2 * a)))
                    elif m == 0 and a == 1:
                        pe.wait_ge(*S("hid", i * 2 + 1))
                    for half in range(2):
                        if m == 0 and a == 0:
                            pe.wait_ge(*S(("xsa", "xsb")[half], i + 1))
                        r = c * PIECES + a * 6 + m * 2 + half
                        pe.wait_ge(*S("land", b * (TURN // WR * 16) + (r // WR + 1) * 16, r % WR))
                        for j in range(4):
                            for n in range(2):
                                k = half * 4 + j
                                if m < 2:
                                    x = XS[:, k, a * 64:a * 64 + 64]
                                else:
                                    x = HIDT[:, j, half * 64:half * 64 + 64]
                                mm = nc.tensor.matmul(PB[m][n * 64:n * 64 + 64, :], x,
                                                      RING[L][r % WR][:, j, n * 512:n * 512 + 512], start=(k == 0),
                                                      stop=(k == DT - 1))
                        mm.then_inc(S["used"], 1)

        over_pairs(pe, pair)
        pe_scatter(pe, S, PAIRS)

    def act_moe_head(act, L, N, added):
        S, F = ME[L], FREE[L]
        act_squares(act, N, XT, SQ, SEQ, (added, lambda d: d + 1))

        act.wait_ge(*S("parts", 1))
        nc.scalar.activation(LOGC[:, :], PB[F[1]], ACT.Copy).then_inc(S["pc1"], 1)

        def tokens(n):
            act.wait_ge(*S("hb", n + 1))
            i, half = n % TT, n // TT * 512
            nc.scalar.activation(XTM[:, i, half:half + 512], PB[F[BLOCK[n % 4]]], ACT.Copy,
                                 scale=ny[:, i:i + 1]).then_inc(S["tm"], 1)

        act.wait_ge(*S("soft", 2))
        nc.scalar.activation(LG[:, :, :], LG[:, :, :], ACT.Exp).then_inc(S["soft"], 1)
        act.wait_ge(*S("fac", 1))
        tokens(0)
        act.wait_ge(*S("afft", 1))
        nc.scalar.activation(WK[:, :], PB[F[6]][0:NE, :], ACT.Copy).then_inc(S["wk"], 1)
        for n in range(1, 2 * TT):
            tokens(n)
        act_gathered(act, L, 1)
        if L == 0:
            act.wait_ge(s_ada, PROJ_ADA + 16)
            nc.scalar.activation(ADS[:, :], PB[F[7]], ACT.Copy).then_inc(s_ads, 1)

    def act_gathered(act, L, count):
        S = ME[L]
        act.wait_ge(*S("gath", count * 2 - 1))
        for d in range(4):
            ins = nc.scalar.activation(XS[:, d, :], PB[4][:, d * P:d * P + P], ACT.Identity,
                                       bias=MOD[:, L, 24 + d:25 + d], scale=coef[:, 2 + 2 * L, d:d + 1])
        ins.then_inc(S["xsa"], 1)

    def act_moe(act, L):
        S = ME[L]

        def pair(b, c, first, last):
            i = b * 2 + c
            for a in range(2):
                act.wait_ge(*S("used", i * PIECES + (6 * a + 2)))
                if not first or a == 1:
                    act.wait_ge(*S("hid", i * 2 + a))
                nc.scalar.activation(SG[:, :], PB[0], ACT.Silu).then_inc(S["sg"], 1)
                if a == 0:
                    act.wait_ge(*S("smt", i + 1))
                    nc.scalar.activation(SM[:, :], PB[3], ACT.Copy).then_inc(S["sm"], 1)
                    act.wait_ge(*S("afm", i + 1))
                    if not first:
                        act.wait_ge(*S("ys", i * 4))
                    for e in range(2):
                        column = PB[6][:, bass.ds(i * 2 + (e * NE + e), 1)]
                        ins = nc.scalar.activation(aff_c[:, e:e + 1], column, ACT.Copy)
                    ins.then_inc(S["afc"], 1)
                elif not last:
                    act_gathered(act, L, i + 2)
                act.wait_ge(*S("hidm", i * 2 + (a + 1)))
                nc.scalar.activation(HIDT[:, :, :], PB[3].rearrange("p (a n) -> p a n", a=4), ACT.Copy).then_inc(
                    S["hidt"], 1)
                act.wait_ge(*S("used", i * PIECES + (6 * a + 6)))
                if a == 0:
                    act.wait_ge(*S("afc", i + 1))
                    if not first:
                        act.wait_ge(*S("yl", i * 2))
                for half in range(2):
                    rows, cols = slice(half * 64, half * 64 + 64), slice(half * 512, half * 512 + 512)
                    nc.scalar.activation(YS[a * 64:a * 64 + 64, cols], PB[2][rows, :], ACT.Copy,
                                         scale=aff_c[rows, a:a + 1]).then_inc(S["ys"], 1)
                    if a == 1:
                        act.wait_ge(*S("ys", i * 4 + (3 + half)))
                        if not first:
                            act.wait_ge(*S("sc", i * DT))
                        nc.scalar.activation(YH[:, cols], YS[:, cols], ACT.Copy).then_inc(S["yh"], 1)

        over_pairs(act, pair)

    def dve_one_hots(S, e):
        for j in range(TT):
            for a in range(2):
                ins = nc.vector.tensor_scalar(OH[:, j, a * CAP:a * CAP + CAP], slots[:, :], PM[:, j, e(a)], None,
                                              ALU.is_equal)
        ins.then_inc(S["oh"], 1)

    def dve_router_weights(ch, L):
        S = ME[L]
        n = 2 + 2 * L
        dve_coef(ch, n, MOD[:, L, 32:40], CT1[:, R_MOE + 8 * L:R_MOE + 8 * L + 8])
        for d in range(DT):
            ins = nc.vector.tensor_scalar(shift_rw[:, d, :], rw[:, L, d, :], MOD[:, L, 24 + d:25 + d], None, ALU.mult)
        ins.then_inc(S["rwc"], 1)
        nc.vector.memset(rw_pad[:, :, NE:32], 0.0)
        for d in range(DT):
            ins = nc.vector.tensor_scalar(rw_pad[:, d, 0:NE], rw[:, L, d, :], coef[:, n, d:d + 1], None, ALU.mult)
        ins.then_inc(S["rwc"], 1)
        ch.eng.wait_ge(*S("rwc", 1))
        nc.vector.tensor_reduce(const_lg[:, :], shift_rw.rearrange("p a n -> p n a"), AX.X, ALU.add).then_inc(
            S["rwc"], 1)

    def dve_moe_head(dve, ch, L, N, added):
        S, F = ME[L], FREE[L]
        dve.wait_ge(*S("parts", 1))
        nc.vector.tensor_copy(SUMC[:, :], PB[F[0]]).then_inc(S["pc0"], 1)
        sums = PB[F[5]]
        dve.wait_ge(*N("sums", 1))
        rsqrt(ch, sums[:, SUM0:SUM0 + TT], TT, 1.0 / D)
        ch.link(nc.vector.tensor_copy(const_lg[:, :], sums[:, CONST0:CONST0 + NE]))
        for i in range(TT):
            lg = sums[:, i * NE:i * NE + NE]
            ins = nc.vector.scalar_tensor_tensor(LG[:, i, :], lg, ny[:, i:i + 1], const_lg[:, :], ALU.mult, ALU.add)
        ch.link(ins)
        nc.vector.tensor_reduce(st4[:, 0, :], LG[:, :, :], AX.X, ALU.max).then_inc(S["soft"], 1)
        dve.wait_ge(*S("soft", 1))
        for i in range(TT):
            ins = nc.vector.tensor_scalar(LG[:, i, :], LG[:, i, :], st4[:, 0, i:i + 1], None, ALU.subtract)
        ins.then_inc(S["soft"], 1)
        nc.vector.tensor_copy(na[:, 0:TT], ny[:, 0:TT]).then_inc(S["fac"], 1)
        dve.wait_ge(*S("soft", 3))
        ch.link(nc.vector.tensor_reduce(st4[:, 1, :], LG[:, :, :], AX.X, ALU.add))
        ch.link(nc.vector.reciprocal(st4[:, 0, :], st4[:, 1, :]))
        for i in range(TT):
            ins = nc.vector.tensor_scalar(AFF[:, i, :], LG[:, i, :], st4[:, 0, i:i + 1], None, ALU.mult)
        ins.then_inc(S["aff"], 1)

        dve.wait_ge(*S("wk", 1))
        for n in range(CAP // 8):
            ch.link(nc.vector.max(M8[:, :], WK[:, :]))
            ch.link(nc.vector.match_replace(WK[:, :], M8[:, :], WK[:, :], -1.0))
        nc.vector.tensor_scalar(MKT[:, :], WK[:, :], 0.0, None, ALU.is_lt).then_inc(S["mask"], 1)
        dve.wait_ge(*S("maskt", 1))
        nc.vector.tensor_copy(MB[:, :, :], PB[F[6]][:, 0:TT * NE].rearrange("p (a n) -> p a n", a=TT)).then_inc(
            S["mb"], 1)
        dve.wait_ge(*S("mb", 1))
        dve.wait_ge(*S("rank", 1))
        ch.link(nc.vector.tensor_tensor(PM[:, :, :], PB[F[5]][:, 0:TT * NE].rearrange("p (a n) -> p a n", a=TT),
                                        MB[:, :, :], ALU.mult))
        dve_one_hots(S, lambda a: slice(a, a + 1))
        dve_gathered(dve, L, 1)
        if L == 0:
            dve.wait_ge(s_adt, 6)
            dve_modulation(MOD[:, 1, 0:16], 0, CT2[:, 48:64], PB[F[7]]).then_inc(s_mod, 1)

    def dve_gathered(dve, L, count):
        S = ME[L]
        dve.wait_ge(*S("gath", count * 2))
        for d in range(4, DT):
            ins = nc.vector.tensor_scalar(XS[:, d, :], PB[5][:, (d - 4) * P:(d - 3) * P], coef[:, 2 + 2 * L, d:d + 1],
                                          MOD[:, L, 24 + d:25 + d], ALU.mult, ALU.add)
        ins.then_inc(S["xsb"], 1)

    def dve_moe(dve, L):
        S = ME[L]
        def add(i):
            for d in range(DT):
                if d == 0 and not (isinstance(i, int) and i == 1):
                    dve.wait_ge(*S("yl", i * 2))
                dve.wait_ge(*S("sc", i * DT + (d - DT + 1)))
                nc.vector.scalar_tensor_tensor(XT[:, d, :], PB[6 + d % 2], MOD[:, L, 40 + d:41 + d], XT[:, d, :],
                                               ALU.mult, ALU.add).then_inc(S["acc"], 1)

        def pair(b, c, first, last):
            i = b * 2 + c
            for a in range(2):
                dve.wait_ge(*S("sg", i * 2 + (a + 1)))
                dve.wait_ge(*S("used", i * PIECES + (6 * a + 4)))
                if not first or a == 1:
                    dve.wait_ge(*S("hidm", i * 2 + a))
                nc.vector.tensor_tensor(HID[:, :], PB[1], SG[:, :], ALU.mult).then_inc(S["hid"], 1)
                if a == 0 and not first:
                    add(i)
                if a == 0 and not last:
                    dve.wait_ge(*S("afm", i + 1))
                    dve_one_hots(S, lambda a: bass.ds(i * 2 + (2 + a), 1))
            if not last:
                dve_gathered(dve, L, i + 2)
            for half in range(2):
                cols = slice(half * 512, half * 512 + 512)
                dve.wait_ge(*S("yh", i * 2 + (1 + half)))
                if not first:
                    dve.wait_ge(*S("sc", i * DT))
                nc.vector.tensor_tensor(YL[:, cols], YS[:, cols], YH[:, cols], ALU.subtract).then_inc(S["yl"], 1)

        over_pairs(dve, pair)
        add(PAIRS)
    V_PIECES = U_PIECES = GW // 512 * (DT // 2)
    O_PIECES = D // 512 * (GW // P // 2)
    s_gland = [sem(f"gmlp_w_landed_{i}") for i in range(RAWG)]
    s_ghi = sem("gmlp_w_hi_ready")
    s_glo = sem("gmlp_w_lo_ready")
    s_gused = sem("gmlp_w_piece_used")
    s_gs = sem("spatial_weights_landed")
    s_vsq = sem("v_squared")
    s_ws = sem("spatial_weights_turned")
    s_wc = sem("spatial_weights_copied")
    s_rl = sem("scaled_spatial_weights_ready")
    s_ut = sem("u_activated")
    s_sv = sem("gates_summed")
    s_gt = sem("gate_chain")
    s_gh = sem("gated_hi_ready")
    s_gl = sem("gated_lo_ready")
    s_xg = sem("gmlp_added_to_stream")
    V_AHEAD = 8

    def sp_gmlp(sp):
        sp.wait_ge(*ME[0]("used", PAIRS * PIECES))
        sp.dma_start(WSR[:, :, :], t["gm_w_s"][0].rearrange("g p q -> p g q")).then_inc(s_gs, 16)
        sp.dma_start(BSB.rearrange("p g n -> p (g n)"), t["gm_b_s"][0].rearrange("g n -> (g n)").partition_broadcast(P)
                     ).then_inc(s_gs, 16)
        sp.wait_ge(*ME[0]("sc", PAIRS * DT))
        sp.wait_ge(*ME[0]("yl", PAIRS))
        for n in range(V_PIECES + U_PIECES + O_PIECES):
            if n >= RAWG:
                sp.wait_ge(s_glo, n - RAWG + 1)
            if n < V_PIECES + U_PIECES:
                c = GW + n // 4 * 512 if n < V_PIECES else (n - V_PIECES) // 4 * 512
                src = t["gm_w_in"][0, n % 4 * 256:n % 4 * 256 + 256, c:c + 512]
            else:
                m = n - V_PIECES - U_PIECES
                src = t["gm_w_out"][0, m % 8 * 256:m % 8 * 256 + 256, m // 8 * 512:m // 8 * 512 + 512]
            sp.dma_start(rawg[n % RAWG][:, :, :], src.rearrange("(a p) n -> p a n", p=P)).then_inc(
                s_gland[n % RAWG], 16)

    def pool_gmlp(pool):
        for n in range(V_PIECES + U_PIECES + O_PIECES):
            pool.wait_ge(s_ghi, n + 1)
            nc.gpsimd.tensor_tensor(stgl[n % 2][:, :, :], rawg[n % RAWG][:, :, :], stgh[n % 2][:, :, :],
                                    ALU.subtract).then_inc(s_glo, 1)

    def pe_gmlp(pe):
        pe_sums(pe, ng, SQ1, PB[0])
        pe_sums_by_token(pe, ng, ROWG, PB[1])
        pe.wait_ge(*ng("diag", 1))
        pe_spread(pe, ng["spread"], DG1, PB[7], TT)
        pe.wait_ge(s_gs, 32)
        for g in range(GROUPS):
            mm = nc.tensor.transpose(PB[5 + g // 4][:, g % 4 * P:g % 4 * P + P], WSR[:, g, :], ident[:, :])
        mm.then_inc(s_ws, 1)
        with pe.Fori(0, 2) as body:
            for c in range(2):
                if c == 1:
                    pe.wait_ge(s_wc, 2)
                for n in range(4):
                    pe.wait_ge(s_glo, body * 8 + (c * 4 + n + 1))
                    for j in range(2):
                        kt = 2 * n + j
                        pe.wait_ge(*ng("lo", kt + 1))
                        for i in range(TT):
                            if kt == 0:
                                pe.wait_ge(s_gel, body * 8 + (c * 4 + i + 1))
                            tok = slice(i * P, i * P + P)
                            mm = three(PB[4 * c + i], H1h[:, kt, tok], H1l[:, kt, tok], stgh[n % 2][:, j, :],
                                       stgl[n % 2][:, j, :], kt == 0, kt == DT - 1)
                    mm.then_inc(s_gused, 1)
        for c in range(4):
            for n in range(4):
                pe.wait_ge(s_glo, V_PIECES + c * 4 + n + 1)
                for j in range(2):
                    kt = 2 * n + j
                    for m in range(4):
                        if kt == 0:
                            if c == 0:
                                pe.wait_ge(s_gel, V_AHEAD + 8 + m + 1)
                            else:
                                pe.wait_ge(s_ut, (c - 1) * 4 + m + 1)
                        w = slice(m * P, m * P + P)
                        mm = three(PB[m], stgh[n % 2][:, j, w], stgl[n % 2][:, j, w], H1h[:, kt, :], H1l[:, kt, :],
                                   kt == 0, kt == DT - 1)
                mm.then_inc(s_gused, 1)
            for m in range(4):
                f = 4 * c + m
                if c == 0:
                    pe.wait_ge(s_gel, V_AHEAD + 16)
                    pe.wait_ge(s_rl, TT)
                else:
                    pe.wait_ge(s_gt, 2 * (f - 4) + 1)
                g = slice(f // 2 * P, f // 2 * P + P)
                for i in range(TT):
                    mm = nc.tensor.matmul(PB[4 + m][:, i * P:i * P + P], V1[:, f, i, :], RW1[:, i, g], start=(i == 0),
                                          stop=True, skip_group_check=True)
                mm.then_inc(s_sv, 1)
        for n in range(O_PIECES):
            chunk, kp = n // 8, n % 8
            pe.wait_ge(s_glo, V_PIECES + U_PIECES + n + 1)
            for j in range(2):
                kt = 2 * kp + j
                if chunk == 0:
                    pe.wait_ge(s_gl, kt + 1)
                for m in range(4):
                    if kt == 0:
                        if chunk == 0:
                            pe.wait_ge(s_ut, 12 + m + 1)
                        else:
                            pe.wait_ge(s_gt, 2 * (12 + m) + 1)
                    w = slice(m * P, m * P + P)
                    mm = three(PB[4 * chunk + m], stgh[n % 2][:, j, w], stgl[n % 2][:, j, w], GH[:, kt, :],
                               GL[:, kt, :], kt == 0, kt == GW // P - 1)
            mm.then_inc(s_gused, 1)

    def act_gmlp(act):
        def hi(n):
            split_piece(act, n, rawg[n % RAWG][:, :, :], stgh[n % 2][:, :, :], (s_gland[n % RAWG], (n // RAWG + 1) * 16),
                        s_gused, s_ghi)

        act_squares(act, ng, XT, SQ1, SEQ, (ME[0]["acc"], lambda d: (PAIRS - 1) * DT + d + 1))
        for n in (0, 1):
            hi(n)
        for d in range(DT):
            act.wait_ge(*ng("scaled", d + 1))
            nc.scalar.activation(H1h[:, d, :], U1[:, d, :], ACT.Identity, bias=MOD[:, 1, d:d + 1]).then_inc(ng["hi"], 1)
            if d == 6:
                hi(2)
        act.wait_ge(s_ws, 1)
        for i in range(2):
            src = PB[5 + i].rearrange("p (a n) -> p a n", a=4)
            nc.scalar.activation(WST[:, 4 * i:4 * i + 4, :], src, ACT.Copy).then_inc(s_wc, 1)

        def v_tile(c, i):
            n = 4 * c + i
            act.wait_ge(s_gused, 4 * c + 4)
            v = V1[:, 4 * c:4 * c + 4, i, :]
            src = PB[4 * (c % 2) + i].rearrange("p (a n) -> p a n", a=4)
            nc.scalar.activation(v, src, ACT.Gelu_apprx_tanh).then_inc(s_gel, 1)
            act.wait_ge(s_gel, V_AHEAD + n + 1)
            need(act, s_vsq, n)
            nc.scalar.activation(VT.rearrange("p (a n) -> p a n", a=4), v, ACT.Square,
                                 accum_out=vsq[:, i, c:c + 1]).then_inc(s_vsq, 1)

        def u_tile(c, m):
            act.wait_ge(s_gused, V_PIECES + 4 * c + 4)
            if c > 0:
                act.wait_ge(s_gt, 2 * (4 * (c - 1) + m) + 2)
            nc.scalar.activation(UT[:, m, :], PB[m], ACT.Gelu_apprx_tanh).then_inc(s_ut, 1)

        for n in range(3, V_PIECES + U_PIECES + O_PIECES):
            c = n // 4 - 1
            if 4 <= c < 8 and n % 4 == 1:
                for i in range(4):
                    u_tile(c - 4, i)
            hi(n)
            if 0 <= c < 4 and n % 4 in (1, 2):
                for i in range(2):
                    v_tile(c, 2 * (n % 4 - 1) + i)

    def dve_gmlp(dve, ch):
        dve_coef(ch, 3, MOD[:, 1, 8:16], CT1[:, R_MIX + 8:R_MIX + 16])
        dve_copy_sums(dve, ng, PB[0], ROWG)
        dve.wait_ge(*ng("sums", 1))
        rsqrt(ch, PB[1][:, 0:TT], TT, 1.0 / D)
        diagonal(DG1, TT, ng["diag"])
        dve.wait_ge(*ng("spread", 1))
        dve.wait_ge(*ME[0]("acc", PAIRS * DT))
        for d in range(DT + 1):
            if d < DT:
                nc.vector.scalar_tensor_tensor(U1[:, d, :], XT[:, d, :], coef[:, 3, d:d + 1], PB[7], ALU.mult,
                                               ALU.mult).then_inc(ng["scaled"], 1)
            if d > 0:
                dve.wait_ge(*ng("hi", d))
                nc.vector.scalar_tensor_tensor(H1l[:, d - 1, :], U1[:, d - 1, :], MOD[:, 1, d - 1:d],
                                               H1h[:, d - 1, :], ALU.add, ALU.subtract).then_inc(ng["lo"], 1)
        dve.wait_ge(s_vsq, 16)
        ch.link(nc.vector.tensor_reduce(nv[:, 0:TT], vsq[:, :, :], AX.X, ALU.add))
        rsqrt(ch, nv[:, 0:TT], TT, 1.0 / GW)
        for i in range(TT):
            nc.vector.tensor_scalar(RW1[:, i, :], WST.rearrange("p g n -> p (g n)"), ny[:, i:i + 1], None,
                                    ALU.mult).then_inc(s_rl, 1)
        for f in range(GW // P):
            buf = (VT, GT)[f % 2]
            dve.wait_ge(s_sv, f + 1)
            if f >= 2:
                dve.wait_ge(s_gl, f - 1)
            for i in range(TT):
                tok = slice(i * P, i * P + P)
                ins = nc.vector.scalar_tensor_tensor(buf[:, tok], PB[4 + f % 4][:, tok], CT1[:, R_VG + f:R_VG + f + 1],
                                                     BSB[:, f // 2, :], ALU.mult, ALU.add)
            ins.then_inc(s_gt, 1)
            dve.wait_ge(s_gt, 2 * f + 1)
            dve.wait_ge(s_ut, f + 1)
            nc.vector.tensor_tensor(buf[:, :], buf[:, :], UT[:, f % 4, :], ALU.mult).then_inc(s_gt, 1)
            dve.wait_ge(s_gt, 2 * f + 2)
            nc.vector.tensor_copy(GH[:, f, :], buf[:, :]).then_inc(s_gh, 1)
            dve.wait_ge(s_gh, f + 1)
            nc.vector.tensor_tensor(GL[:, f, :], buf[:, :], GH[:, f, :], ALU.subtract).then_inc(s_gl, 1)
        dve_router_weights(ch, 1)
        for d in range(DT):
            if d % 4 == 0:
                dve.wait_ge(s_gused, V_PIECES + U_PIECES + 8 * (d // 4 + 1))
            nc.vector.scalar_tensor_tensor(XT[:, d, :], PB[d], MOD[:, 1, 16 + d:17 + d], XT[:, d, :], ALU.mult,
                                           ALU.add).then_inc(s_xg, 1)

    s_fg = sem("stream_times_gain_first_half_ready")
    s_fga = sem("stream_times_gain_second_half_ready")
    s_fny = sem("final_factors_ready")
    s_ft = sem("final_blocks_turned")
    s_fo = sem("final_second_halves_ready")
    s_fo2 = sem("final_first_halves_ready")
    s_out = sem("output_written")

    def act_final(act):
        act_squares(act, nf, XT, FSQ, SEQ, (ME[0]["acc"], lambda d: (2 * PAIRS - 1) * DT + d + 1))
        for d in range(4, DT):
            nc.scalar.activation(FG[:, d, :], XT[:, d, :], ACT.Copy, scale=CT1[:, R_FIN + d:R_FIN + d + 1]).then_inc(
                s_fga, 1)
        act.wait_ge(s_fny, 1)
        for n in range(1, 2 * TT, 2):
            act.wait_ge(s_ft, n + 1)
            nc.scalar.activation(FO[:, n // 2, 512:1024], PB[(n + 2) % 8], ACT.Copy, scale=ny[:, n // 2:n // 2 + 1]).then_inc(
                s_fo, 1)

    def dve_final(dve, ch):
        for d in range(4):
            dve.wait_ge(*ME[1]("acc", (PAIRS - 1) * DT + d + 1))
            nc.vector.tensor_scalar(FG[:, d, :], XT[:, d, :], CT1[:, R_FIN + d:R_FIN + d + 1], None, ALU.mult).then_inc(
                s_fg, 1)
        dve_copy_sums(dve, nf, PB[0], ROWF)
        dve.wait_ge(*nf("sums", 1))
        rsqrt(ch, PB[1][:, 0:TT], TT, 1.0 / D)
        nc.vector.tensor_copy(st4[:, 0, :], ny[:, 0:TT]).then_inc(s_fny, 1)
        for n in range(0, 2 * TT, 2):
            dve.wait_ge(s_ft, n + 1)
            nc.vector.tensor_scalar(FO[:, n // 2, 0:512], PB[(n + 2) % 8], ny[:, n // 2:n // 2 + 1], None, ALU.mult).then_inc(
                s_fo2, 1)

    def pe_final(pe):
        pe_sums(pe, nf, FSQ, PB[0])
        pe_sums_by_token(pe, nf, ROWF, PB[1])
        pe.wait_ge(s_fg, 4)
        for n in range(2 * TT):
            if n == 1:
                pe.wait_ge(s_fga, 4)
            if n == 6:
                pe.wait_ge(s_fny, 1)
            for j in range(4):
                mm = nc.tensor.transpose(PB[(n + 2) % 8][:, j * P:j * P + P],
                                         FG[:, n % 2 * 4 + j, n // 2 * P:n // 2 * P + P], ident[:, :])
            mm.then_inc(s_ft, 1)

    def sp_final(sp):
        for i in range(TT):
            sp.wait_ge(s_fo, i + 1)
            sp.wait_ge(s_fo2, i + 1)
            sp.dma_start(out[0, i * P:i * P + P, :], FO[:, i, :]).then_inc(s_out, 16)
        sp.wait_ge(s_out, TT * 16)

    def before_experts_0(sp):
        def before(r):
            if r == 0:
                sp.wait_ge(s_qkl, 2 * HEADS)
                sp.wait_ge(s_vb, HEADS)
            elif r == 4:
                sp_out_projection(sp, (5, 6, 7))
                sp.wait_ge(s_ohl, HEADS)
            elif r == 5:
                sp.wait_ge(s_osp, HEADS)
                sp.wait_ge(s_olo, 7)
            elif r == 6:
                sp_last_sweep(sp)
                sp.wait_ge(s_opw, 8)
        return before

    def before_experts_1(sp):
        def before(r):
            if r == 0:
                sp.wait_ge(s_gused, V_PIECES + U_PIECES)
            elif r == 2:
                sp.wait_ge(s_sv, GW // P)
            elif r == 4:
                sp.wait_ge(s_gl, GW // P)
            elif r == 5:
                sp.wait_ge(s_gused, V_PIECES + U_PIECES + O_PIECES)
        return before

    block = ctx.enter_context(nc.Block())

    @block.sync
    def _(sp):
        sp_projections(sp)
        sp_attention(sp)
        sp_moe(sp, 0, before_experts_0(sp))
        sp_gmlp(sp)
        sp_moe(sp, 1, before_experts_1(sp))
        sp_final(sp)

    @block.tensor
    def _(pe):
        pe_head(pe)
        pe_projections(pe)
        pe_attention(pe)
        pe_out_projection(pe)
        pe_moe_head(pe, 0, nm0, s_xo)
        pe_moe(pe, 0)
        pe_gmlp(pe)
        pe_moe_head(pe, 1, nm1, s_xg)
        pe_moe(pe, 1)
        pe_final(pe)

    @block.scalar
    def _(act):
        act_head(act)
        act_projections(act)
        act_attention(act)
        act_out_projection(act)
        act_moe_head(act, 0, nm0, s_xo)
        act_moe(act, 0)
        act_gmlp(act)
        act_moe_head(act, 1, nm1, s_xg)
        act_moe(act, 1)
        act_final(act)

    @block.vector
    def _(dve):
        ch = Chain(dve, s_dve)
        dve_head(dve, ch)
        dve_projections(dve)
        dve_attention(dve)
        dve_out_projection(dve, ch)
        dve_moe_head(dve, ch, 0, nm0, s_xo)
        dve_moe(dve, 0)
        dve_gmlp(dve, ch)
        dve_moe_head(dve, ch, 1, nm1, s_xg)
        dve_moe(dve, 1)
        dve_final(dve, ch)

    @block.gpsimd
    def _(pool):
        pool_head(pool)
        pool_projections(pool)
        pool_attention(pool)
        pool_out_projection(pool)
        pool_gmlp(pool)


def bass_hybrid_trunk(nc, t, out):
    with ExitStack() as ctx:
        build(nc, ctx, t, out)


_INS = ['x', 'c', 'ctx', 'c_ctx', 'ada_w', 'ada_b', 'mixer_norm_g', 'moe_norm_g', 'router_w', 'moe_w_gate', 'moe_w_up',
        'moe_w_down', 'da_w_in', 'da_lambda_q1', 'da_lambda_k1', 'da_lambda_q2', 'da_lambda_k2', 'da_subln_g',
        'da_w_out', 'gm_w_in', 'gm_v_g', 'gm_w_s', 'gm_b_s', 'gm_w_out', 'final_norm_g']


def kernel(**inputs):
    import numpy as _np
    import concourse.bacc as _bacc
    from concourse import mybir as _mybir
    from concourse.bass_utils import run_bass_kernel_spmd as _run

    nc = _bacc.Bacc("TRN2", target_bir_lowering=False, num_devices=1)
    arrays = {f"in_{name}_dram": _np.ascontiguousarray(inputs[name]) for name in _INS}
    arrays["in_shape_constants_dram"] = shape_constants()
    tensors = {}
    for name, a in arrays.items():
        dtype = _mybir.dt.from_np(a.dtype)
        tensors[name[3:-5]] = nc.dram_tensor(name, a.shape, dtype, kind="ExternalInput").ap()
    out = nc.dram_tensor("out_0_dram", (1, SEQ, D), _mybir.dt.from_np(_np.dtype("float32")), kind="ExternalOutput").ap()
    bass_hybrid_trunk(nc, tensors, out)
    return _run(nc, [arrays], core_ids=[0]).results[0]["out_0_dram"]
```
